# Optimizing a Trainium2 kernel written in Bass

```python
import jax, jax.numpy as jnp
from jax import lax
import numpy as np

D_MODEL = 1024
BATCH = 1
SEQ = 512
DEPTH = 1

HEAD_DIM = 64
ATTN_GROUPS = ((128, 1), (512, 4), (2048, 16))
HEADS_PER_GROUP = 4
N_ATTN_HEADS = HEADS_PER_GROUP * len(ATTN_GROUPS)
ATTN_WIDTH = N_ATTN_HEADS * HEAD_DIM
BLK = 128
ROPE_THETA = 10000.0
SGU_CHUNK = 128
SGU_GROUPS = 12
SGU_GROUP_DIM = 64
SGU_WIDTH = SGU_GROUPS * SGU_GROUP_DIM
IN_WIDTH = 3 * ATTN_WIDTH + 2 * SGU_WIDTH + 2 * D_MODEL
SPLITS = (ATTN_WIDTH, 2 * ATTN_WIDTH, 3 * ATTN_WIDTH, 3 * ATTN_WIDTH + 2 * SGU_WIDTH, 3 * ATTN_WIDTH + 2 * SGU_WIDTH + D_MODEL)
N_EXPERTS = 32
TOP_K = 4
D_EXPERT = D_MODEL
SWIGLU_LIMIT = 7.0
SWIGLU_ALPHA = 1.702
MOE_BLOCK = 128
EPS = 1e-6
NEG_INF = -1e30

kernel_name = "hybrid_dilated_attn_sgu_moe"

def rms_norm(x, g):
    x32 = x.astype(jnp.float32)
    y = x32 * lax.rsqrt(jnp.mean(x32 * x32, axis=-1, keepdims=True) + EPS)
    return (y * g.astype(jnp.float32)).astype(x.dtype)

def layer_norm(x, g, b):
    x32 = x.astype(jnp.float32)
    mu = jnp.mean(x32, axis=-1, keepdims=True)
    xc = x32 - mu
    y = xc * lax.rsqrt(jnp.mean(xc * xc, axis=-1, keepdims=True) + EPS)
    return (y * g.astype(jnp.float32) + b.astype(jnp.float32)).astype(x.dtype)

def rope(x, positions):
    half = HEAD_DIM // 2
    inv_freq = ROPE_THETA ** (-jnp.arange(half, dtype=jnp.float32) / half)
    ang = positions.astype(jnp.float32)[..., None] * inv_freq
    cos = jnp.cos(ang)[:, :, None, :]
    sin = jnp.sin(ang)[:, :, None, :]
    x32 = x.astype(jnp.float32)
    x1, x2 = x32[..., :half], x32[..., half:]
    out = jnp.concatenate([x1 * cos - x2 * sin, x2 * cos + x1 * sin], axis=-1)
    return out.astype(x.dtype)

def dilated_window_attention(q, k, v, window, dilation):
    B, S, H, hd = q.shape
    n_back = window // dilation
    assert n_back <= BLK
    L = S // dilation
    nb = -(-L // BLK)
    Lp = nb * BLK

    def to_res(t):
        return t.reshape(B, L, dilation, H, hd).transpose(0, 2, 3, 1, 4)

    qr = jnp.pad(to_res(q), ((0, 0), (0, 0), (0, 0), (0, Lp - L), (0, 0)))
    qr = qr.reshape(B, dilation, H, nb, BLK, hd)

    def windows(t):
        tp = jnp.pad(to_res(t), ((0, 0), (0, 0), (0, 0), (BLK, Lp - L), (0, 0)))
        tp = tp.reshape(B, dilation, H, nb + 1, BLK, hd)
        return jnp.concatenate([tp[:, :, :, :-1], tp[:, :, :, 1:]], axis=4)

    kw = windows(k)
    vw = windows(v)
    s = jnp.einsum('brhnqc,brhnkc->brhnqk', qr.astype(jnp.float32), kw.astype(jnp.float32)) * (hd ** -0.5)
    qi = jnp.arange(BLK)[:, None]
    kj = jnp.arange(2 * BLK)[None, :]
    dist = BLK + qi - kj
    key_m = jnp.arange(nb)[:, None, None] * BLK + kj[None] - BLK
    valid = (dist >= 0)[None] & (dist <= n_back)[None] & (key_m >= 0)
    s = jnp.where(valid, s, NEG_INF)
    m = jnp.max(s, axis=-1, keepdims=True)
    p = jnp.exp(s - m)
    l = jnp.sum(p, axis=-1, keepdims=True)
    o = jnp.einsum('brhnqk,brhnkc->brhnqc', p, vw.astype(jnp.float32)) / l
    lse = (m + jnp.log(l))[..., 0]
    o = o.reshape(B, dilation, H, Lp, hd)[:, :, :, :L].transpose(0, 3, 1, 2, 4).reshape(B, S, H, hd)
    lse = lse.reshape(B, dilation, H, Lp)[:, :, :, :L].transpose(0, 3, 1, 2).reshape(B, S, H)
    return o, lse

def spatial_gating(z, ln_g, ln_b, w_s, b_s):
    B, S, _ = z.shape
    u, v = z[..., :SGU_WIDTH], z[..., SGU_WIDTH:]
    v = layer_norm(v, ln_g, ln_b)
    vg = v.reshape(B, S // SGU_CHUNK, SGU_CHUNK, SGU_GROUPS, SGU_GROUP_DIM)
    causal = jnp.tril(jnp.ones((SGU_CHUNK, SGU_CHUNK), dtype=bool))
    w = jnp.where(causal[None], w_s, jnp.zeros_like(w_s))
    mixed = jnp.einsum('gts,bcsgd->bctgd', w, vg) + b_s.T[None, None, :, :, None]
    return u * mixed.reshape(B, S, SGU_WIDTH)

def mixer_block(x, positions, norm1_g, w_in, q_norm_g, k_norm_g, sgu_ln_g, sgu_ln_b,
                w_spatial, b_spatial, w_branch_a, w_branch_b, w_out):
    B, S, _ = x.shape
    h = rms_norm(x, norm1_g)
    proj = h @ w_in
    q, k, v, z, g_a, g_b = jnp.split(proj, SPLITS, axis=-1)
    q = rope(rms_norm(q.reshape(B, S, N_ATTN_HEADS, HEAD_DIM), q_norm_g), positions)
    k = rope(rms_norm(k.reshape(B, S, N_ATTN_HEADS, HEAD_DIM), k_norm_g), positions)
    v = v.reshape(B, S, N_ATTN_HEADS, HEAD_DIM)
    outs, lses = [], []
    for gi, (window, dilation) in enumerate(ATTN_GROUPS):
        sl = slice(gi * HEADS_PER_GROUP, (gi + 1) * HEADS_PER_GROUP)
        o, lse = dilated_window_attention(q[:, :, sl], k[:, :, sl], v[:, :, sl], window, dilation)
        outs.append(o)
        lses.append(lse)
    alpha = jax.nn.softmax(jnp.stack(lses, axis=0), axis=0)
    attn = jnp.concatenate([outs[i] * alpha[i][..., None] for i in range(len(ATTN_GROUPS))], axis=2)
    attn = attn.reshape(B, S, ATTN_WIDTH).astype(x.dtype)
    y_a = attn @ w_branch_a
    sgu = spatial_gating(jax.nn.gelu(z, approximate=False), sgu_ln_g, sgu_ln_b, w_spatial, b_spatial)
    y_b = sgu @ w_branch_b
    merged = jax.nn.sigmoid(g_a) * y_a + jax.nn.sigmoid(g_b) * y_b
    return x + merged @ w_out

def moe_block(x, norm2_g, w_router, b_router, w_gate_up, b_gate_up, w_down, b_down):
    B, S, D = x.shape
    T = B * S
    hf = rms_norm(x, norm2_g).reshape(T, D)
    logits = (hf @ w_router + b_router).astype(jnp.float32)
    top_v, top_e = lax.top_k(logits, TOP_K)
    gates = jax.nn.softmax(top_v, axis=-1)
    n_assign = T * TOP_K
    e_flat = top_e.reshape(-1)
    w_flat = gates.reshape(-1)
    tok_flat = jnp.arange(n_assign, dtype=jnp.int32) // TOP_K
    order = jnp.argsort(e_flat)
    e_sorted = e_flat[order]
    counts = jnp.bincount(e_flat, length=N_EXPERTS)
    padded = (counts + MOE_BLOCK - 1) // MOE_BLOCK * MOE_BLOCK
    start = jnp.cumsum(counts) - counts
    pend = jnp.cumsum(padded)
    pstart = pend - padded
    dest = pstart[e_sorted] + (jnp.arange(n_assign) - start[e_sorted])
    cap = (-(-n_assign // MOE_BLOCK) + N_EXPERTS) * MOE_BLOCK
    n_blocks = cap // MOE_BLOCK
    buf_tok = jnp.full((cap,), T, dtype=jnp.int32).at[dest].set(tok_flat[order])
    buf_w = jnp.zeros((cap,), jnp.float32).at[dest].set(w_flat[order])
    blk_e = jnp.sum(jnp.arange(n_blocks)[:, None] * MOE_BLOCK >= pend[None, :], axis=1)
    blk_e = jnp.minimum(blk_e, N_EXPERTS - 1)
    hpad = jnp.concatenate([hf, jnp.zeros((1, D), hf.dtype)], axis=0)
    xb = hpad[buf_tok].reshape(n_blocks, MOE_BLOCK, D)

    def expert_rows(args):
        xblk, e = args
        gu = xblk @ w_gate_up[e] + b_gate_up[e]
        gate, up = gu[:, :D_EXPERT], gu[:, D_EXPERT:]
        gate = jnp.minimum(gate, SWIGLU_LIMIT)
        up = jnp.clip(up, -SWIGLU_LIMIT, SWIGLU_LIMIT)
        act = (up + 1.0) * (gate * jax.nn.sigmoid(SWIGLU_ALPHA * gate))
        return act @ w_down[e] + b_down[e]

    yb = lax.map(expert_rows, (xb, blk_e)).reshape(cap, D)
    y = jnp.zeros((T + 1, D), jnp.float32).at[buf_tok].add(yb.astype(jnp.float32) * buf_w[:, None])[:T]
    return x + y.reshape(B, S, D).astype(x.dtype)

def setup_inputs(seed: int = 0) -> dict:
    key = jax.random.key(seed)
    ks = jax.random.split(key, 20)
    f32 = jnp.float32
    nrm = lambda k, shape, scale: jax.random.normal(k, shape, f32) * scale
    x = jax.random.normal(ks[0], (BATCH, SEQ, D_MODEL), f32)
    offset = jax.random.randint(ks[1], (BATCH, 1), 0, 1024, dtype=jnp.int32)
    positions = offset + jnp.arange(SEQ, dtype=jnp.int32)[None, :]
    return {
        "x": x,
        "positions": positions,
        "norm1_g": 1.0 + nrm(ks[2], (DEPTH, D_MODEL), 0.02),
        "w_in": nrm(ks[3], (DEPTH, D_MODEL, IN_WIDTH), D_MODEL ** -0.5),
        "q_norm_g": 1.0 + nrm(ks[4], (DEPTH, HEAD_DIM), 0.02),
        "k_norm_g": 1.0 + nrm(ks[5], (DEPTH, HEAD_DIM), 0.02),
        "sgu_ln_g": 1.0 + nrm(ks[6], (DEPTH, SGU_WIDTH), 0.02),
        "sgu_ln_b": nrm(ks[7], (DEPTH, SGU_WIDTH), 0.02),
        "w_spatial": nrm(ks[8], (DEPTH, SGU_GROUPS, SGU_CHUNK, SGU_CHUNK), SGU_CHUNK ** -0.5),
        "b_spatial": 1.0 + nrm(ks[9], (DEPTH, SGU_GROUPS, SGU_CHUNK), 0.1),
        "w_branch_a": nrm(ks[10], (DEPTH, ATTN_WIDTH, D_MODEL), ATTN_WIDTH ** -0.5),
        "w_branch_b": nrm(ks[11], (DEPTH, SGU_WIDTH, D_MODEL), SGU_WIDTH ** -0.5),
        "w_out": nrm(ks[12], (DEPTH, D_MODEL, D_MODEL), D_MODEL ** -0.5),
        "norm2_g": 1.0 + nrm(ks[13], (DEPTH, D_MODEL), 0.02),
        "w_router": nrm(ks[14], (DEPTH, D_MODEL, N_EXPERTS), D_MODEL ** -0.5),
        "b_router": nrm(ks[15], (DEPTH, N_EXPERTS), 0.01),
        "w_gate_up": nrm(ks[16], (DEPTH, N_EXPERTS, D_MODEL, 2 * D_EXPERT), D_MODEL ** -0.5),
        "b_gate_up": nrm(ks[17], (DEPTH, N_EXPERTS, 2 * D_EXPERT), 0.01),
        "w_down": nrm(ks[18], (DEPTH, N_EXPERTS, D_EXPERT, D_MODEL), D_EXPERT ** -0.5),
        "b_down": nrm(ks[19], (DEPTH, N_EXPERTS, D_MODEL), 0.01),
    }

def reference(x, positions, norm1_g, w_in, q_norm_g, k_norm_g, sgu_ln_g, sgu_ln_b,
              w_spatial, b_spatial, w_branch_a, w_branch_b, w_out, norm2_g,
              w_router, b_router, w_gate_up, b_gate_up, w_down, b_down):
    for layer in range(DEPTH):
        x = mixer_block(x, positions, norm1_g[layer], w_in[layer], q_norm_g[layer], k_norm_g[layer],
                        sgu_ln_g[layer], sgu_ln_b[layer], w_spatial[layer], b_spatial[layer],
                        w_branch_a[layer], w_branch_b[layer], w_out[layer])
        x = moe_block(x, norm2_g[layer], w_router[layer], b_router[layer], w_gate_up[layer],
                      b_gate_up[layer], w_down[layer], b_down[layer])
    return x


_drawn_inputs = setup_inputs


def setup_inputs(seed=0):
    import zlib

    import numpy as np

    out = dict(_drawn_inputs(seed))
    spreads = {}
    factors = {'q_norm_g': 5.157, 'k_norm_g': 7.281, 'b_gate_up': 8.0, 'b_down': 8.0, 'sgu_ln_b': 3.037}
    for name, (base, spread) in spreads.items():
        noise = np.random.default_rng([zlib.crc32(name.encode()), seed]).standard_normal(out[name].shape)
        drawn = base * np.exp(spread * noise) if base else spread * noise
        out[name] = __import__('jax').numpy.asarray(drawn.astype(out[name].dtype))
    for name, factor in factors.items():
        out[name] = (out[name] * factor).astype(out[name].dtype)
    return out
```

```python
from contextlib import ExitStack

import numpy as np
import concourse.bass as bass
from concourse import mybir

P = 128
F32 = mybir.dt.float32
I32 = mybir.dt.int32
U32 = mybir.dt.uint32
ALU = mybir.AluOpType
ACT = mybir.ActivationFunctionType
AX_X = mybir.AxisListType.X
WIDTHS = (64, 96)
HW = WIDTHS[0]
ROUND = 1.5 * 2.0 ** 23
PI_IN = 3.1415925
TWO_PI = (6.28125, 0.0019354820251464844, -1.7484556025237907e-07)


class Steps:

    def __init__(self, eng, sem, before=0):
        self.eng, self.sem, self.before, self.n = eng, sem, before, 0

    def __call__(self, ins):
        ins.then_inc(self.sem, 1)
        self.n += 1
        self.eng.wait_ge(self.sem, self.before + self.n)


def hybrid_layer(nc, x, positions, norm1_g, w_in, q_norm_g, k_norm_g, sgu_ln_g, sgu_ln_b, w_spatial,
                 b_spatial, w_branch_a, w_branch_b, w_out, norm2_g, w_router, b_router, w_gate_up,
                 b_gate_up, w_down, b_down, out):
    _, T, D = x.shape
    TT = T // P
    KD = D // P
    HD = q_norm_g.shape[1]
    HALF = HD // 2
    AW = w_branch_a.shape[1]
    KA = AW // P
    HEADS = AW // HD
    GROUPS = 3
    HPG = HEADS // GROUPS
    GW = HPG * HD
    SG = w_spatial.shape[1]
    SW = SG * HD
    E = w_router.shape[2]
    F = w_down.shape[2]
    KF = F // P
    TOPK = 4
    CW = 256
    PAIRS = D // CW
    CH = KD * CW
    EPS = 1e-6
    NEG = -1e30
    SCALE = float(HD) ** -0.5
    LIMIT, ALPHA = 7.0, 1.702
    COL_V = 3 * AW + SW
    COL_U = 3 * AW
    COL_GA = 3 * AW + 2 * SW
    COL_GB = COL_GA + D
    assert T == 4 * P and GW == CW and SW == AW and D == F and KD == 8
    RING = KD + KF // 2
    BW = D // 2

    with ExitStack() as ctx:
        def sb(name, shape, dt=F32):
            return ctx.enter_context(nc.sbuf_tensor(name, shape, dt))

        def sem(name):
            return ctx.enter_context(nc.semaphore(name))

        SLOT = 2 * F
        ring = sb("ring", [P, RING, SLOT])
        flat = ring[:, :, :].rearrange("p s n -> p (s n)")
        qk = flat[:, 0:2 * TT * AW].rearrange("p (k t n) -> p k t n", k=2, t=TT)
        at = 2 * TT * AW
        vtok = flat[:, at:at + TT * AW].rearrange("p (t n) -> p t n", t=TT)
        at += TT * AW
        utok = flat[:, at:at + TT * SW].rearrange("p (t n) -> p t n", t=TT)
        at += TT * SW
        ztok = flat[:, at:at + TT * SW].rearrange("p (t n) -> p t n", t=TT)
        assert at + TT * SW <= 8 * SLOT
        xr = flat[:, 0:TT * D].rearrange("p (t n) -> p t n", t=TT)
        trig = flat[:, TT * D:TT * D + 4 * 8 * HALF].rearrange("p (a u c) -> p a u c", a=4, c=HALF)
        stream = [ring[:, 8 + s, :] for s in range(4)]
        mlrow = flat[0:HPG, 0:6 * T].rearrange("p (a g t) -> p a g t", a=2, g=GROUPS)
        wrow = flat[0:HPG, 6 * T:9 * T].rearrange("p (g t) -> p g t", g=GROUPS)
        mrow = flat[0:HPG, 9 * T:10 * T]
        drow = flat[0:HPG, 10 * T:11 * T]

        work = sb("work", [P, 20480])
        o_x, o_h, o_qk, o_a, o_s = 0, 4096, 8192, 14336, 17408
        xs = work[:, o_x:o_x + TT * D].rearrange("p (t n) -> p t n", t=TT)
        hT = work[:, o_h:o_h + KD * T].rearrange("p (k t) -> p k t", k=KD)
        qkT = work[:, o_qk:o_qk + 12 * T].rearrange("p (k t) -> p k t", k=12)
        mergedT = work[:, o_qk:o_qk + KD * T].rearrange("p (k t) -> p k t", k=KD)
        g2b = work[:, o_qk + KD * T:o_qk + KD * T + D]
        attnT = work[:, o_a:o_a + KA * T].rearrange("p (k t) -> p k t", k=KA)
        sguT = work[:, o_s:o_s + KA * T].rearrange("p (k t) -> p k t", k=KA)
        bias_raw = work[0:E, o_qk:o_qk + 2 * F]
        bdn = work[0:E, o_qk + (KD * T) + D:o_qk + (KD * T) + 2 * D]
        wsp_raw = work[:, o_a:o_a + SG * P].rearrange("p (g s) -> p g s", g=SG)
        bsp_raw = work[0:SG, o_a + SG * P:o_a + SG * P + P]
        lnb = work[:, o_s:o_s + 2 * SW].rearrange("p (a n) -> p a n", a=2)
        hf = work[:, o_a:o_a + TT * D].rearrange("p (t n) -> p t n", t=TT)
        hfT = hT
        xgT = work[:, o_qk:o_qk + KD * P].rearrange("p (k c) -> p k c", k=KD)
        yrow = work[:, o_qk + D:o_qk + 2 * D]
        gu_tok = work[:, o_qk + 2 * D:o_qk + 4 * D].rearrange("p (b n) -> p b n", b=4)
        bsum = work[:, o_h:o_h + TT * D].rearrange("p (t n) -> p t n", t=TT)
        gate = work[:, o_h:o_h + D].rearrange("p (k c) -> p k c", k=KF)
        up = work[:, o_h + D:o_h + 2 * D].rearrange("p (k c) -> p k c", k=KF)
        sg = work[:, o_h + 2 * D:o_h + 3 * D].rearrange("p (k c) -> p k c", k=KF)
        act = work[:, o_h + 3 * D:o_h + 4 * D].rearrange("p (k c) -> p k c", k=KF)
        sel = work[:, o_a + TT * D:o_a + TT * D + TT * P].rearrange("p (t c) -> p t c", t=TT)
        aux_at = o_a + TT * D + TT * P
        aux = work[:, aux_at:aux_at + TT * E * 2].rearrange("p (t e a) -> p t e a", t=TT, e=E)
        hot_at = aux_at + TT * E * 2
        hot = work[:, hot_at:hot_at + TT * TOPK * E].rearrange("p (t k e) -> p t k e", t=TT, k=TOPK)
        hotg_at = hot_at + TT * TOPK * E
        hotg = work[:, hotg_at:hotg_at + TT * TOPK * E].rearrange("p (t k e) -> p t k e", t=TT, k=TOPK)
        assert hotg_at + TT * TOPK * E <= 20480

        sc = sb("sc", [P, 2, 1024])
        pt = sb("pt", [P, 1024])
        dist = pt[:, 0:P].bitcast(I32)
        slots_iota, slots_twice = pt[:, 0:T], pt[:, T:T + P]
        ident = sb("ident", [P, P])
        upper = sb("upper", [P, P])
        ones = sb("ones", [P, P])
        wspT = sb("wspT", [P, SG, P])
        cos_t = sb("cos_t", [P, 8, HALF])
        sin_t = sb("sin_t", [P, 8, HALF])
        band = sb("band", [P, 2 * P])
        diag = sb("diag", [P, P])
        qkg = sb("qkg", [P, 2, HD])
        biases = sb("biases", [P, 2 * KF, E])
        wr = sb("wr", [P, KD, E])
        brb = sb("brb", [P, E])
        pick = sb("pick", [HPG, 2, P])
        bsp = sb("bsp", [P, SG])
        g1 = sb("g1", [P, KD])
        pos_i = sb("pos_i", [P, 8], I32)
        pos_f = sb("pos_f", [P, 8])
        inv_f = sb("inv_f", [P, HALF])
        ss = sb("ss", [P, TT])
        rs = sb("rs", [P, TT])
        hss = sb("hss", [P, 2, TT, HEADS])
        mstat = sb("mstat", [P, 12, HPG])
        nmstat = sb("nmstat", [P, 12, HPG])
        lstat = sb("lstat", [P, 12, HPG])
        bn = sb("bn", [P, TT, 2, 6])
        mv = sb("mv", [P, TT, 2])
        iota_e = sb("iota_e", [P, E])
        pcol = sb("pcol", [P, 3])
        tiny = sb("tiny", [P, 16])
        MI = 64
        meta_i = cos_t[0:1, 0:4 * MI // HALF, :].rearrange("p a c -> p (a c)").bitcast(I32)
        idx = sb("idx", [P, 1], U32)
        scf = sc[:, :, :].rearrange("p a n -> p (a n)")
        lg = scf[:, 0:128].rearrange("p (t e) -> p t e", t=TT)
        top = scf[:, 128:160].rearrange("p (t k) -> p t k", t=TT)
        topi = scf[:, 160:192].bitcast(U32).rearrange("p (t k) -> p t k", t=TT)
        topf = scf[:, 192:208].rearrange("p (t k) -> p t k", t=TT)
        ge = scf[:, 208:224].rearrange("p (t k) -> p t k", t=TT)
        gsum = scf[:, 224:228]
        chosen = scf[:, 256:384].rearrange("p (t e) -> p t e", t=TT)
        posm = scf[:, 384:512].rearrange("p (t e) -> p t e", t=TT)
        cnt = scf[:, 512:544]
        nblk = scf[:, 544:576]
        scan = scf[:, 576:576 + 96].rearrange("p (a n) -> p a n", a=2)
        cmpe = scf[:, 672:704]
        cmpn = scf[:, 704:736]
        meta = scf[:, 736:740]
        bias_now = scf[:, 768:768 + 2 * KF]
        aux_now = scf[:, 800:800 + 2 * TT].rearrange("p (t a) -> p t a", t=TT)
        slot_now = scf[:, 810:812]
        slot_next = scf[:, 812:814]
        slot_pad = scf[:, 814:815]
        rel = scf[:, 816:820]
        row_f = scf[:, 820:821]
        gates = scf[:, 1024:1024 + TT * E].rearrange("p (t e) -> p t e", t=TT)
        gatesT = scf[0:E, 1280:1280 + T]

        bank = ctx.enter_context(nc.psum_tensor("bank", [P, 8, 512], F32))

        y_acc = nc.dram_tensor("y_acc", [T + P, D], F32, kind="Internal").ap()
        y_halves = y_acc.rearrange("t (h n) -> (t h) n", h=2)

        s_x, s_small, s_g2 = sem("x_loaded"), sem("small_loaded"), sem("g2_loaded")
        psum_clear, trig_ready, trig_done = sem("psum_clear"), sem("trig_ready"), sem("trig_done")
        consts2, ln_scaled = sem("moe_consts_made"), sem("ln_scaled")
        s_chunk = [sem(f"chunk_loaded{s}") for s in range(4)]
        consts = sem("consts_made")
        dve_step, act_step, pool_step = sem("dve_step"), sem("act_step"), sem("pool_step")
        dve_moe = sem("dve_moe_step")
        rms_sum, rms_var, rms_root, xr_ready = sem("rms_sum"), sem("rms_var"), sem("rms_root"), sem("xr_ready")
        setup_t, setup_e = sem("setup_transposed"), sem("setup_evacuated")
        hT_t, hT_e = sem("hT_transposed"), sem("hT_evacuated")
        proj_done, proj_read = sem("proj_done"), sem("proj_read")
        sq_done, sq_read, hvar, hroot = sem("squares_done"), sem("squares_read"), sem("head_var"), sem("head_root")
        scaled, gained, roped = sem("qk_scaled"), sem("qk_gained"), sem("qk_roped")
        pair_t, pair_e = sem("pair_transposed"), sem("pair_evacuated")
        score_done, max_done, prob_done = sem("score_done"), sem("max_done"), sem("prob_done")
        pt_t, pt_e, o_done, o_read = sem("probT_done"), sem("probT_evacuated"), sem("o_done"), sem("o_read")
        ztok_ready, utok_ready, ln_var, ln_root, ln_done = (
            sem("z_gelu"), sem("u_gelu"), sem("ln_var"), sem("ln_root"), sem("ln_done"))
        ml_t, ml_e, gexp_in, gexp, wrow_ready = sem("ml_t"), sem("ml_e"), sem("gexp_in"), sem("gexp"), sem("wrow_ready")
        mix_done, mix_read = sem("mix_done"), sem("mix_read")
        spread_done, spread_read = sem("spread_done"), sem("spread_read")
        sgu_t, sgu_e = sem("sgu_transposed"), sem("sgu_evacuated")
        gate_done, gate_read, y_done, y_read = sem("gate_done"), sem("gate_read"), sem("branch_done"), sem("branch_read")
        part_b, merged = sem("part_b"), sem("merged")
        out_done, out_read = sem("out_done"), sem("out_read")
        x1_stored = sem("x1_stored")
        rms2_sum, rms2_var, rms2_root, hf_ready = sem("rms2_sum"), sem("rms2_var"), sem("rms2_root"), sem("hf_ready")
        hf_t, hf_e, logit_done = sem("hf_transposed"), sem("hf_evacuated"), sem("logits_done")
        topd, topexp, chosen_ready, place_done, meta_ready, metarow_done, meta_loaded = (
            sem("top_diff"), sem("top_exp"), sem("chosen_ready"), sem("places_done"), sem("meta_ready"),
            sem("meta_rows"), sem("meta_loaded"))
        s_slot = [sem(f"slot_loaded{s}") for s in range(RING)]
        slot_used = sem("slot_used")
        sel_ready, gather_done, gather_read = sem("sel_ready"), sem("gather_done"), sem("gather_read")
        gu_done, gated, sig_done, act_ready, up_read = (
            sem("gate_up_done"), sem("gate_ready"), sem("sigmoid_done"), sem("act_ready"), sem("gu_read"))
        down_done, yrow_ready, y_added = sem("down_done"), sem("yrow_ready"), sem("y_added")
        gu_out_a, gu_out_b, gu_t = sem("gate_up_out_a"), sem("gate_up_out_b"), sem("gate_up_transposed")
        gates_ready, gatesT_t, gatesT_e, bsum_done, bsum_read, bias_added = (
            sem("gates_ready"), sem("gatesT_transposed"), sem("gatesT_evacuated"), sem("bias_sum_done"),
            sem("bias_sum_read"), sem("bias_added"))
        slot_idx, slot_idx_read, now_ready = sem("slot_idx_done"), sem("slot_idx_read"), sem("slot_now_ready")
        row_ready = sem("slot_rows_ready")
        out_stored, add_turn, rows_free = sem("out_stored"), sem("add_turn"), sem("rows_free")


        block = ctx.enter_context(nc.Block())

        pos = positions[0]
        smalls = [
            (pos_i[:, 0:4], pos.rearrange("(j p) -> p j", p=P)),
            (pos_i[:, 4:8], pos.rearrange("(p j) -> p j", p=P)),
            (g1[:, :], norm1_g[0].rearrange("(k p) -> p k", p=P)),
            (qkg[:, 0, :], q_norm_g[0].partition_broadcast(P)),
            (qkg[:, 1, :], k_norm_g[0].partition_broadcast(P)),
            (wsp_raw, w_spatial[0].rearrange("g t s -> t g s")),
            (bsp_raw, b_spatial[0]),
            (bias_raw[:, 0:2 * F], b_gate_up[0]),
            (wr[:, :, :], w_router[0].rearrange("(k p) e -> p k e", p=P)),
            (brb[:, :], b_router[0].partition_broadcast(P)),
            (lnb[:, 0, :], sgu_ln_g[0].partition_broadcast(P)),
            (lnb[:, 1, :], sgu_ln_b[0].partition_broadcast(P)),
        ]
        SMALL = len(smalls)
        SETUP = SG // 4 + 1 + 2 * KF // 4
        CONSTS = 5
        SLOTS = 31

        def unit_blocks(u):
            return [u % 4 - 1, u % 4] if 0 < u < 4 else [u % 4]

        def unit_width(u):
            return P * len(unit_blocks(u))

        def unit_mask(u):
            return band[:, :] if 0 < u < 4 else band[:, P:2 * P] if u < 8 else diag[:, :]

        def heads(ap, width):
            return ap[:, 0:HPG * width].rearrange("p (h w) -> p h w", h=HPG)

        def order_cols(ap, group, j):
            if group == 0:
                return ap[:, j * P:(j + 1) * P]
            return ap[:, j:T:4]

        def chunk_src(n):
            if n < 9:
                return w_in, n * CW, KD
            if n < 12:
                return w_in, COL_V + (n - 9) * CW, KD
            if n < 15:
                return w_in, COL_U + (n - 12) * CW, KD
            if n < 15 + 4 * PAIRS:
                i, s = divmod(n - 15, 4)
                w, c, k = [(w_in, COL_GA, KD), (w_in, COL_GB, KD), (w_branch_a, 0, KA), (w_branch_b, 0, KA)][s]
                return w, c + i * CW, k
            return w_out, (n - 15 - 4 * PAIRS) * CW, KD

        def chunk_slot(n):
            return n % 3 if n < 15 else (n - 15) % 4

        CHUNKS = 15 + 5 * PAIRS

        def chunk_used(n):
            if n < 15:
                return proj_done, TT * (n + 1)
            if n < 15 + 4 * PAIRS:
                i, part = divmod(n - 15, 4)
                return (gate_done, y_done)[part // 2], 4 * i + 2 * (part % 2) + 2
            return out_done, TT * (n - 15 - 4 * PAIRS + 1)

        chunk_turn = [sum(chunk_slot(m) == chunk_slot(n) for m in range(n + 1)) for n in range(CHUNKS)]

        @block.sync
        def _(sp):
            for t in range(TT):
                sp.dma_start(xs[:, t, :], x[0, t * P:(t + 1) * P, :]).then_inc(s_x, 16)
            last = {}
            for n in range(CHUNKS):
                w, c, k = chunk_src(n)
                s = chunk_slot(n)
                if s in last:
                    sp.wait_ge(*chunk_used(last[s]))
                last[s] = n
                sp.dma_start(stream[s][:, 0:k * CW].rearrange("p (k n) -> p k n", k=k),
                             w[0].rearrange("(k p) n -> p k n", p=P)[:, :, c:c + CW]).then_inc(s_chunk[s], 16)
            sp.wait_ge(o_read, 12)
            sp.dma_start(g2b, norm2_g[0].partition_broadcast(P)).then_inc(s_g2, 16)
            sp.dma_start(bdn, b_down[0]).then_inc(s_g2, 16)
            sp.wait_ge(sgu_t, KA)
            sp.wait_ge(spread_done, KA)

            def slot_copy(s, gate_up, down):
                if s < KD:
                    return ring[:, s, :], gate_up[s * P:(s + 1) * P, :]
                j = 2 * (s - KD)
                return (ring[:, s, :].rearrange("p (j n) -> p j n", j=2),
                        down.rearrange("(j p) n -> p j n", p=P)[:, j:j + 2, :])

            for s in range(RING):
                if s >= KD:
                    sp.wait_ge(*chunk_used(CHUNKS - 4 + s - KD))
                sp.dma_start(*slot_copy(s, w_gate_up[0, 0], w_down[0, 0])).then_inc(s_slot[s], 16)
            for t in range(TT):
                sp.wait_ge(bias_added, t + 1)
                sp.dma_start(y_acc[t * P:(t + 1) * P, :], xs[:, t, :]).then_inc(x1_stored, 16)
            sp.dma_start(y_acc[T:T + P, :], xs[:, 0, :]).then_inc(x1_stored, 16)
            sp.wait_ge(meta_loaded, 1)
            items = sp.value_load(meta_i[0:1, 3 * MI:3 * MI + 1], min_val=E, max_val=E + 15)
            with sp.Fori(1, items) as i:
                e = sp.value_load(meta_i[0:1, bass.ds(i, 1)], min_val=0, max_val=E - 1)
                gu = w_gate_up[0, bass.ds(e, 1)].rearrange("e k n -> (e k) n")
                dn = w_down[0, bass.ds(e, 1)].rearrange("e k n -> (e k) n")
                for s in range(RING):
                    if s == KD - 1:
                        sp.wait_ge(gu_done, i * 2)
                    elif s == RING - 1:
                        sp.wait_ge(down_done, i)
                    else:
                        sp.wait_ge(slot_used, (i - 1) * (RING - 2) + s + 1 - (s > KD - 1))
                    sp.dma_start(*slot_copy(s, gu, dn)).then_inc(s_slot[s], 16)
            sp.wait_ge(y_added, items * 16)
            sp.dma_start(out[0], y_acc[0:T, :]).then_inc(out_stored, 16)
            sp.wait_ge(out_stored, 16)

        @block.gpsimd
        def _(pool):
            step = Steps(pool, pool_step)
            pool.sem_inc(rows_free, 1)
            pool.sem_inc(merged, 1)
            step(pool.memset(ident[:, :], 0.0))
            pool.affine_select(out=ident[:, :], in_=ident[:, :], compare_op=ALU.not_equal, fill=1.0, base=0,
                               pattern=[[-1, P]], channel_multiplier=1).then_inc(consts, 1)
            step(pool.memset(ones[:, :], 1.0))
            pool.affine_select(out=upper[:, :], in_=ones[:, :], compare_op=ALU.is_gt, fill=0.0, base=0,
                               pattern=[[1, P]], channel_multiplier=-1)
            for c in range(HALF):
                ins = pool.memset(inv_f[:, c:c + 1], float(np.float32(10000.0) ** (-np.float32(c) / np.float32(HALF))))
            ins.then_inc(consts, 1)
            pool.wait_ge(s_small, 16 * SMALL)
            pool.affine_select(out=wsp_raw, in_=wsp_raw, compare_op=ALU.is_ge, fill=0.0, base=0,
                               pattern=[[0, SG], [-1, P]], channel_multiplier=1).then_inc(consts, 1)
            step(pool.memset(band[:, :], 0.0))
            step(pool.affine_select(out=band[:, :], in_=band[:, :], compare_op=ALU.is_ge, fill=NEG, base=P,
                                    pattern=[[-1, 2 * P]], channel_multiplier=1))
            step(pool.affine_select(out=band[:, :], in_=band[:, :], compare_op=ALU.is_ge, fill=NEG, base=0,
                                    pattern=[[1, 2 * P]], channel_multiplier=-1))
            pool.iota(dist, pattern=[[-1, P]], base=T, channel_multiplier=1)
            pool.iota(iota_e[:, :], pattern=[[1, E]], base=0, channel_multiplier=0,
                      allow_small_or_imprecise_dtypes=True)
            pool.iota(pcol[:, 0:1], pattern=[[1, 1]], base=0, channel_multiplier=1,
                      allow_small_or_imprecise_dtypes=True)
            step(pool.memset(pcol[:, 2:3], 1.0))
            pool.affine_select(out=pcol[:, 2:3], in_=pcol[:, 2:3], compare_op=ALU.is_ge, fill=0.0, base=-HW,
                               pattern=[[0, 1]], channel_multiplier=1)
            pool.iota(pcol[:, 1:2], pattern=[[1, 1]], base=T + 1, channel_multiplier=1,
                      allow_small_or_imprecise_dtypes=True).then_inc(consts, 1)
            step(pool.memset(pick[:, :, :], 1.0))
            pool.affine_select(out=pick[:, :, :].rearrange("p i (a d) -> p i a d", a=2),
                               in_=pick[:, :, :].rearrange("p i (a d) -> p i a d", a=2),
                               compare_op=ALU.is_equal, fill=0.0, base=0,
                               pattern=[[-1, 2], [-2, 2], [0, HD]], channel_multiplier=1).then_inc(consts, 1)
            for kind in range(2):
                for t in range(TT):
                    pool.wait_ge(scaled, kind * TT + t + 1)
                    v = qk[:, kind, t, :].rearrange("p (h d) -> p h d", d=HD)
                    pool.tensor_tensor(v, v, qkg[:, kind, :].unsqueeze(1).to_broadcast([P, HEADS, HD]),
                                       ALU.mult).then_inc(gained, 1)
            for t in range(TT):
                pool.wait_ge(ln_scaled, t + 1)
                step(pool.tensor_tensor(ztok[:, t, :], ztok[:, t, :], lnb[:, 0, :], ALU.mult))
                pool.tensor_tensor(ztok[:, t, :], ztok[:, t, :], lnb[:, 1, :], ALU.add).then_inc(ln_done, 1)
            with pool.Fori(0, PAIRS) as i:
                for jj in range(2):
                    pool.wait_ge(part_b, 2 * i + jj + 1)
                    m = mergedT[:, bass.ds(2 * i + jj, 1), :].rearrange("p a t -> p (a t)")
                    pool.tensor_tensor(m, m, pt[:, jj * T:jj * T + T], ALU.add).then_inc(merged, 1)
            pool.wait_ge(out_done, 1)
            pool.iota(slots_iota, pattern=[[1, T]], base=0, channel_multiplier=0,
                      allow_small_or_imprecise_dtypes=True)
            pool.iota(slots_twice, pattern=[[0, 2], [1, HW]], base=0, channel_multiplier=0,
                      allow_small_or_imprecise_dtypes=True)
            pool.iota(aux[:, :, :, 0], pattern=[[P, TT], [0, E]], base=1, channel_multiplier=1,
                      allow_small_or_imprecise_dtypes=True).then_inc(consts2, 1)
            for t in range(TT):
                pool.wait_ge(bsum_read, t + 1)
                pool.tensor_tensor(xs[:, t, :], xs[:, t, :], bsum[:, t, :], ALU.add).then_inc(bias_added, 1)
            pool.wait_ge(meta_loaded, 1)
            items = pool.value_load(meta_i[0:1, 3 * MI:3 * MI + 1], min_val=E, max_val=E + 15)
            with pool.Fori(0, items) as i:
                pool.wait_ge(yrow_ready, i + 2)
                pool.wait_ge(x1_stored, 16 * (TT + 1))
                pool.sem_inc(add_turn, 1)
                cls = pool.value_load(meta_i[0:1, bass.ds(i + 2 * MI, 1)], min_val=0, max_val=2)
                with pool.If(cls < 1):
                    pool.indirect_dma_start(y_halves, bass.IndirectOffsetOnAxis(ap=idx[:, 0:1], axis=0),
                                            yrow[:, 0:BW], None, compute_op=ALU.add).then_inc(y_added, 16)
                with pool.Else():
                    pool.indirect_dma_start(y_acc, bass.IndirectOffsetOnAxis(ap=idx[:, 0:1], axis=0), yrow, None,
                                            compute_op=ALU.add).then_inc(y_added, 16)
                pool.wait_ge(y_added, i * 16 + 16)
                pool.sem_inc(rows_free, 1)

        @block.scalar
        def _(ae):
            ae.sem_inc(yrow_ready, 1)
            for dst, src in smalls:
                ae.dma_start(dst, src, allow_slow_non_contiguous=True).then_inc(s_small, 16)
            ae.wait_ge(s_x, 16 * TT)
            for t in range(TT):
                ae.activation(work[:, o_h + t * D:o_h + (t + 1) * D], xs[:, t, :], ACT.Square,
                              accum_out=ss[:, t:t + 1]).then_inc(rms_sum, 1)
            ae.wait_ge(rms_var, 1)
            ae.activation(rs[:, :], rs[:, :], ACT.Sqrt).then_inc(rms_root, 1)
            ae.wait_ge(trig_ready, 1)
            ae.activation(sin_t[:, :, :], trig[:, 2], ACT.Sin).then_inc(trig_done, 1)
            ae.activation(cos_t[:, :, :], trig[:, 3], ACT.Sin).then_inc(trig_done, 1)
            for b in range(SETUP):
                ae.wait_ge(setup_t, b + 1)
                src = bank[:, 4 + b % 4, :]
                if b < SG // 4:
                    ins = ae.copy(wspT[:, 4 * b:4 * b + 4, :], src.rearrange("p (g t) -> p g t", g=4))
                elif b == SG // 4:
                    ins = ae.copy(bsp[:, :], src[:, 0:SG])
                else:
                    j = 4 * (b - SG // 4 - 1)
                    ins = ae.copy(biases[:, j:j + 4, :], src[:, 0:4 * E].rearrange("p (j e) -> p j e", j=4))
                ins.then_inc(setup_e, 1)
            ae.sem_inc(proj_read, 2)

            for kind in range(3):
                for g in range(GROUPS):
                    for t in range(TT):
                        n = kind * 12 + g * TT + t
                        ae.wait_ge(proj_done, n + 1)
                        dst = (qk[:, kind] if kind < 2 else vtok)[:, t, g * GW:(g + 1) * GW]
                        ae.copy(dst, bank[:, n % 2, 0:CW]).then_inc(proj_read, 1)
                if kind < 2:
                    ae.wait_ge(proj_read, 2 + 12 * (kind + 1))
                    for t in range(TT):
                        m = kind * TT + t
                        if m >= 2:
                            ae.wait_ge(sq_read, m - 1)
                        ae.activation(sc[:, m % 2, 0:AW], qk[:, kind, t, :], ACT.Square).then_inc(sq_done, 1)
                    ae.wait_ge(hvar, kind + 1)
                    ae.activation(hss[:, kind], hss[:, kind], ACT.Sqrt).then_inc(hroot, 1)

            def exps(u):
                ae.wait_ge(max_done, u + 1)
                p = heads(sc[:, u % 2, :], unit_width(u))
                for h in range(HPG):
                    ins = ae.activation(p[:, h, :], p[:, h, :], ACT.Exp, bias=nmstat[:, u, h:h + 1], scale=SCALE,
                                        accum_out=lstat[:, u, h:h + 1])
                ins.then_inc(prob_done, 1)

            for s in range(SLOTS):
                if s < 12:
                    ae.wait_ge(pair_t, s + 1)
                    g, r = divmod(s, 4)
                    ae.copy(qkT[:, (r // 2) * KA + 2 * g + r % 2, :], bank[:, 6, :]).then_inc(pair_e, 1)
                if s < 24:
                    ae.wait_ge(proj_done, 36 + s + 1)
                    c, t = divmod(s, TT)
                    dst = ztok if c < 3 else utok
                    ae.copy(dst[:, t, (c % 3) * CW:(c % 3 + 1) * CW], bank[:, s % 2, 0:CW]).then_inc(proj_read, 1)
                if s % 2 == 1 and 5 <= s < 29:
                    exps((s - 5) // 2)
                if s == 12 or s == 24:
                    half, ready = (ztok, ztok_ready) if s == 12 else (utok, utok_ready)
                    ae.wait_ge(proj_read, 2 + 36 + s)
                    for t in range(TT):
                        ae.activation(half[:, t, :], half[:, t, :], ACT.Gelu).then_inc(ready, 1)
                if s == 16:
                    ae.wait_ge(ln_var, TT)
                    ae.activation(mv[:, :, 1], mv[:, :, 1], ACT.Sqrt).then_inc(ln_root, 1)
            for a in range(2):
                for g in range(GROUPS):
                    ae.wait_ge(ml_t, 3 * a + g + 1)
                    src, dst = bank[0:HPG, 2 + 3 * a + g, :], mlrow[:, a, g, :]
                    if g > 0:
                        dst = dst.rearrange("p (m s) -> p s m", s=4)
                        src = src.rearrange("p (s m) -> p s m", s=4)
                    ae.copy(dst, src).then_inc(ml_e, 1)
            ae.wait_ge(gexp_in, 1)
            ae.activation(wrow, wrow, ACT.Exp, scale=SCALE).then_inc(gexp, 1)
            for k in range(KA):
                ae.wait_ge(sgu_t, k + 1)
                ae.copy(sguT[:, k, :], bank[:, 2 + k, :]).then_inc(sgu_e, 1)
            ae.sem_inc(gate_read, 4)
            with ae.Fori(0, PAIRS) as i:
                for ab in range(2):
                    for jj in range(2):
                        n = 4 * i + 2 * ab + jj
                        ae.wait_ge(gate_done, n + 1)
                        ae.wait_ge(y_read, n + 1)
                        ae.activation(sc[:, ab, jj * T:jj * T + T], bank[:, 4 * jj + ab, :],
                                      ACT.Sigmoid).then_inc(gate_read, 1)
            for t in range(TT):
                ae.wait_ge(out_read, 4 * (PAIRS - 1) + t + 1)
                ae.activation(work[:, o_h + t * D:o_h + (t + 1) * D], xs[:, t, :], ACT.Square,
                              accum_out=ss[:, t:t + 1]).then_inc(rms2_sum, 1)
            ae.wait_ge(rms2_var, 1)
            ae.activation(rs[:, :], rs[:, :], ACT.Sqrt).then_inc(rms2_root, 1)
            for t in range(TT):
                ae.wait_ge(hf_t, t + 1)
                b = 2 * (t % 2)
                ae.copy(hfT[:, :, t * P:(t + 1) * P].rearrange("p (a k) c -> p a k c", a=2),
                        bank[:, b:b + 2, :].rearrange("p a (k c) -> p a k c", k=4)).then_inc(hf_e, 1)
            ae.wait_ge(topd, 1)
            ae.activation(ge, ge, ACT.Exp).then_inc(topexp, 1)
            ae.wait_ge(gatesT_t, 1)
            ae.copy(gatesT, bank[0:E, 7, :]).then_inc(gatesT_e, 1)
            for t in range(TT):
                ae.wait_ge(bsum_done, t + 1)
                b = 2 * (t % 2)
                ae.copy(bsum[:, t, :], bank[:, b:b + 2, :].rearrange("p a n -> p (a n)")).then_inc(bsum_read, 1)

            def read_gather(half, n):
                ae.wait_ge(gather_done, n)
                ae.copy(xgT[:, 4 * half:4 * half + 4, :],
                        bank[:, 6 + half, :].rearrange("p (k c) -> p k c", k=4)).then_inc(gather_read, 1)

            ae.wait_ge(meta_loaded, 1)
            items = ae.value_load(meta_i[0:1, 3 * MI:3 * MI + 1], min_val=E, max_val=E + 15)
            read_gather(0, 1)
            read_gather(1, 2)
            with ae.Fori(0, items) as i:
                cls = ae.value_load(meta_i[0:1, bass.ds(i + 2 * MI, 1)], min_val=0, max_val=2)

                def sigmoids(N):
                    for h in range(2):
                        ae.wait_ge(gated, 2 * i + h + 1)
                        ae.activation(sg[:, 4 * h:4 * h + 4, 0:N], gate[:, 4 * h:4 * h + 4, 0:N], ACT.Sigmoid,
                                      scale=ALPHA).then_inc(sig_done, 1)

                for h in range(2):
                    ae.wait_ge(gu_done, 2 * i + h + 1)
                    ae.copy(gu_tok[:, h, :], bank[:, h, :]).then_inc(gu_out_a, 1)
                with ae.If(cls < 1):
                    sigmoids(HW)
                with ae.Else():
                    sigmoids(P)
                for h in range(2):
                    read_gather(h, 2 * i + h + 3)

                def scale_rows(dst, src):
                    ae.wait_ge(down_done, i + 1)
                    ae.wait_ge(now_ready, i + 1)
                    ae.wait_ge(rows_free, i + 1)
                    ae.activation(dst, src, ACT.Copy, scale=slot_now[:, 1:2]).then_inc(yrow_ready, 1)

                with ae.If(cls < 1):
                    scale_rows(yrow[:, 0:BW], bank[:, 4, :])
                with ae.Else():
                    scale_rows(yrow, bank[:, 4:6, :].rearrange("p a n -> p (a n)"))

        @block.vector
        def _(ve):
            step = Steps(ve, dve_step)
            for b in range(8):
                ins = ve.memset(bank[:, b, :], 0.0)
            ins.then_inc(psum_clear, 1)
            ve.wait_ge(consts, 4)
            step(ve.tensor_scalar(dist, dist, 3, None, ALU.bitwise_and))
            step(ve.scalar_tensor_tensor(out=diag[:, :], in0=dist, scalar=NEG, in1=band[:, P:2 * P],
                                         op0=ALU.mult, op1=ALU.add))
            ve.wait_ge(rms_sum, TT)
            ve.tensor_scalar(rs[:, :], ss[:, :], 1.0 / D, EPS, ALU.mult, ALU.add).then_inc(rms_var, 1)
            ve.wait_ge(rms_root, 1)
            step(ve.reciprocal(rs[:, :], rs[:, :]))
            for t in range(TT):
                ve.tensor_scalar(xr[:, t, :], xs[:, t, :], rs[:, t:t + 1], None, ALU.mult).then_inc(xr_ready, 1)
            ve.wait_ge(consts, 2)
            ve.wait_ge(s_small, 16 * SMALL)
            step(ve.tensor_copy(pos_f[:, :], pos_i[:, :]))
            ang, n_t = trig[:, 0], trig[:, 1]
            step(ve.tensor_tensor(ang, pos_f[:, :].unsqueeze(2).to_broadcast([P, 8, HALF]),
                                  inv_f[:, :].unsqueeze(1).to_broadcast([P, 8, HALF]), ALU.mult))
            for which, dst in ((0, trig[:, 2]), (1, trig[:, 3])):
                step(ve.tensor_scalar(n_t, ang, 0.5 / np.pi, 0.25 * which, ALU.mult, ALU.add))
                step(ve.tensor_scalar(n_t, n_t, ROUND, None, ALU.add))
                step(ve.tensor_scalar(n_t, n_t, -ROUND, None, ALU.add))
                src = ang
                for part in TWO_PI:
                    step(ve.scalar_tensor_tensor(out=dst, in0=n_t, scalar=-part, in1=src, op0=ALU.mult, op1=ALU.add))
                    src = dst
                step(ve.tensor_scalar(dst, dst, 0.5 * float(np.pi) * which, PI_IN, ALU.add, ALU.min))
                step(ve.tensor_scalar(dst, dst, -PI_IN, None, ALU.max))
            ve.sem_inc(trig_ready, 1)
            for k in range(KD):
                ve.wait_ge(hT_t, k + 1)
                ve.tensor_scalar(hT[:, k, :], bank[:, k % 4, :], g1[:, k:k + 1], None, ALU.mult).then_inc(hT_e, 1)
            ve.wait_ge(trig_done, 2)
            for kind in range(2):
                def q4(t):
                    return qk[:, kind, t, :].rearrange("p (h d) -> p h d", d=HD)
                for t in range(TT):
                    m = kind * TT + t
                    ve.wait_ge(sq_done, m + 1)
                    ins = ve.tensor_reduce(hss[:, kind, t, :],
                                           sc[:, m % 2, 0:AW].rearrange("p (h d) -> p h d", d=HD), AX_X, ALU.add)
                    ins.then_inc(sq_read, 1)
                ve.wait_ge(sq_read, TT * (kind + 1))
                ve.tensor_scalar(hss[:, kind], hss[:, kind], 1.0 / HD, EPS, ALU.mult, ALU.add).then_inc(hvar, 1)
                ve.wait_ge(hroot, kind + 1)
                step(ve.reciprocal(hss[:, kind], hss[:, kind]))
                for t in range(TT):
                    ve.tensor_tensor(q4(t), q4(t), hss[:, kind, t, :].unsqueeze(2).to_broadcast([P, HEADS, HD]),
                                     ALU.mult).then_inc(scaled, 1)
                for t in range(TT):
                    ve.wait_ge(gained, kind * TT + t + 1)
                    prod = pt[:, 0:AW].rearrange("p (a h d) -> p a h d", a=2, d=HALF)
                    a, b = q4(t)[:, :, 0:HALF], q4(t)[:, :, HALF:HD]
                    for order, hs in ((0, slice(0, HPG)), (1, slice(HPG, HEADS))):
                        n = hs.stop - hs.start
                        cs = cos_t[:, order * TT + t, :].unsqueeze(1).to_broadcast([P, n, HALF])
                        sn = sin_t[:, order * TT + t, :].unsqueeze(1).to_broadcast([P, n, HALF])
                        ve.tensor_tensor(prod[:, 0, hs, :], b[:, hs, :], sn, ALU.mult)
                        step(ve.tensor_tensor(prod[:, 1, hs, :], a[:, hs, :], sn, ALU.mult))
                        ve.tensor_tensor(a[:, hs, :], a[:, hs, :], cs, ALU.mult)
                        step(ve.tensor_tensor(b[:, hs, :], b[:, hs, :], cs, ALU.mult))
                    ve.tensor_tensor(a, a, prod[:, 0], ALU.subtract)
                    step(ve.tensor_tensor(b, b, prod[:, 1], ALU.add))
                    ve.sem_inc(roped, 1)

            def mask_max(u):
                W = unit_width(u)
                ve.wait_ge(score_done, u + 1)
                if u >= 2:
                    ve.wait_ge(pt_t, u - 1)
                s_u = sc[:, u % 2, 0:HPG * W].rearrange("p (a i w) -> p a i w", a=2, i=2)
                step(ve.tensor_tensor(s_u, bank[:, 2:4, 0:2 * W].rearrange("p a (i w) -> p a i w", i=2),
                                      unit_mask(u).unsqueeze(1).unsqueeze(1).to_broadcast([P, 2, 2, W]), ALU.add))
                step(ve.tensor_reduce(mstat[:, u, :], heads(sc[:, u % 2, :], W), AX_X, ALU.max))
                ve.tensor_scalar(nmstat[:, u, :], mstat[:, u, :], -SCALE, None, ALU.mult).then_inc(max_done, 1)

            def read_pt(u):
                ve.wait_ge(pt_t, u + 1)
                ve.wait_ge(o_done, u)
                n = HPG * unit_width(u)
                ve.tensor_copy(pt[:, 0:n], bank[:, 4:6, :].rearrange("p a n -> p (a n)")[:, 0:n]).then_inc(pt_e, 1)

            def read_o(u):
                g, j = divmod(u, 4)
                ve.wait_ge(o_done, u + 1)
                for i in range(2):
                    ins = ve.tensor_copy(order_cols(attnT[:, 2 * g + i, :], g, j), bank[:, 7, i * P:(i + 1) * P])
                ins.then_inc(o_read, 1)

            for s in range(SLOTS):
                if s % 2 == 1 and 5 <= s < 29:
                    mask_max((s - 5) // 2)
                if s % 2 == 1 and 7 <= s < 31:
                    read_pt((s - 7) // 2)
                if s % 2 == 0 and 8 <= s < 31:
                    read_o((s - 8) // 2)
                if s == 14:
                    for t in range(TT):
                        ve.wait_ge(ztok_ready, t + 1)
                        ve.bn_stats(bn[:, t, 0, :], ztok[:, t, 0:SW // 2])
                        step(ve.bn_stats(bn[:, t, 1, :], ztok[:, t, SW // 2:SW]))
                        step(ve.bn_aggr(mv[:, t, :], bn[:, t, :, :]))
                        ve.tensor_scalar(mv[:, t, 1:2], mv[:, t, 1:2], EPS, None, ALU.add).then_inc(ln_var, 1)
                if s == 18:
                    ve.wait_ge(ln_root, 1)
                    step(ve.reciprocal(mv[:, :, 1], mv[:, :, 1]))
                    for t in range(TT):
                        ve.tensor_scalar(ztok[:, t, :], ztok[:, t, :], mv[:, t, 0:1], mv[:, t, 1:2],
                                         ALU.subtract, ALU.mult).then_inc(ln_scaled, 1)
            ve.wait_ge(utok_ready, TT)
            for g in range(SG):
                ve.wait_ge(mix_done, g + 1)
                u_g = utok[:, :, g * HD:(g + 1) * HD]
                ve.scalar_tensor_tensor(out=u_g, in0=bank[:, g % 2, 0:TT * HD].rearrange("p (t d) -> p t d", t=TT),
                                        scalar=bsp[:, g:g + 1], in1=u_g, op0=ALU.add, op1=ALU.mult).then_inc(mix_read, 1)
            ve.wait_ge(ml_e, 6)
            mr, lr = mlrow[:, 0], mlrow[:, 1]
            step(ve.tensor_tensor(mrow, mr[:, 0, :], mr[:, 1, :], ALU.max))
            step(ve.tensor_tensor(mrow, mrow, mr[:, 2, :], ALU.max))
            ve.tensor_tensor(wrow, mr, mrow.unsqueeze(1).to_broadcast([HPG, GROUPS, T]), ALU.subtract).then_inc(gexp_in, 1)
            ve.wait_ge(gexp, 1)
            step(ve.tensor_tensor(lr, lr, wrow, ALU.mult))
            step(ve.tensor_tensor(drow, lr[:, 0, :], lr[:, 1, :], ALU.add))
            step(ve.tensor_tensor(drow, drow, lr[:, 2, :], ALU.add))
            step(ve.reciprocal(drow, drow))
            ve.tensor_tensor(wrow, wrow, drow.unsqueeze(1).to_broadcast([HPG, GROUPS, T]), ALU.mult).then_inc(wrow_ready, 1)
            for k in range(KA):
                ve.wait_ge(spread_done, k + 1)
                ve.tensor_tensor(attnT[:, k, :], attnT[:, k, :], bank[:, 2 + k, :], ALU.mult).then_inc(spread_read, 1)
            ve.sem_inc(y_read, 4)
            with ve.Fori(0, PAIRS) as i:
                for ab in range(2):
                    for jj in range(2):
                        n = 4 * i + 2 * ab + jj
                        ve.wait_ge(y_done, n + 1)
                        ve.wait_ge(gate_read, n + 1 + 4)
                        if ab == 0:
                            dst = mergedT[:, bass.ds(2 * i + jj, 1), :].rearrange("p a t -> p (a t)")
                        else:
                            dst = pt[:, jj * T:jj * T + T]
                            ve.wait_ge(merged, 2 * i + 1)
                        step_ins = ve.tensor_tensor(dst, bank[:, 4 * jj + 2 + ab, :], sc[:, ab, jj * T:jj * T + T],
                                                    ALU.mult)
                        step_ins.then_inc(y_read, 1)
                        if ab == 1:
                            ve.wait_ge(y_read, n + 1 + 4)
                            ve.sem_inc(part_b, 1)
            for c in range(PAIRS):
                for t in range(TT):
                    n = c * TT + t
                    ve.wait_ge(out_done, n + 1)
                    v = xs[:, t, c * CW:(c + 1) * CW]
                    ve.tensor_tensor(v, v, bank[:, n % 2, 0:CW], ALU.add).then_inc(out_read, 1)
            ve.wait_ge(rms2_sum, TT)
            ve.tensor_scalar(rs[:, :], ss[:, :], 1.0 / D, EPS, ALU.mult, ALU.add).then_inc(rms2_var, 1)
            ve.wait_ge(rms2_root, 1)
            step(ve.reciprocal(rs[:, :], rs[:, :]))
            ve.wait_ge(s_g2, 32)
            for t in range(TT):
                ve.scalar_tensor_tensor(out=hf[:, t, :], in0=xs[:, t, :], scalar=rs[:, t:t + 1], in1=g2b,
                                        op0=ALU.mult, op1=ALU.mult).then_inc(hf_ready, 1)
            ve.wait_ge(logit_done, 1)
            step(ve.tensor_tensor(lg, bank[:, 4, 0:TT * E].rearrange("p (t e) -> p t e", t=TT),
                                  brb[:, :].unsqueeze(1).to_broadcast([P, TT, E]), ALU.add))
            for t in range(TT):
                ins = ve.max(out=top[:, t, :], in_=lg[:, t, :])
            step(ins)
            for t in range(TT):
                ins = ve.max_index(out=topi[:, t, :], in_max=top[:, t, :], in_values=lg[:, t, :])
            ve.tensor_tensor(ge, top[:, :, 0:TOPK], top[:, :, 0:1].to_broadcast([P, TT, TOPK]),
                             ALU.subtract).then_inc(topd, 1)
            step(ins)
            step(ve.tensor_copy(topf, topi[:, :, 0:TOPK]))
            step(ve.tensor_tensor(hot, iota_e[:, :].unsqueeze(1).unsqueeze(1).to_broadcast([P, TT, TOPK, E]),
                                  topf.unsqueeze(3).to_broadcast([P, TT, TOPK, E]), ALU.is_equal))
            ve.tensor_reduce(chosen, hot.rearrange("p t k e -> p t e k"), AX_X, ALU.add).then_inc(chosen_ready, 1)
            ve.wait_ge(topexp, 1)
            step(ve.tensor_reduce(gsum, ge, AX_X, ALU.add))
            step(ve.reciprocal(gsum, gsum))
            step(ve.tensor_tensor(ge, ge, gsum.unsqueeze(2).to_broadcast([P, TT, TOPK]), ALU.mult))
            step(ve.tensor_tensor(hotg, hot, ge.unsqueeze(3).to_broadcast([P, TT, TOPK, E]), ALU.mult))
            ve.wait_ge(consts2, 1)
            ve.tensor_reduce(gates, hotg.rearrange("p t k e -> p t e k"), AX_X, ALU.add).then_inc(gates_ready, 1)
            ve.wait_ge(gates_ready, 1)
            step(ve.tensor_copy(aux[:, :, :, 1], gates))
            ve.wait_ge(place_done, 1)
            places = bank[:, 5, 0:TT * E].rearrange("p (t e) -> p t e", t=TT)
            step(ve.scalar_tensor_tensor(out=posm, in0=places, scalar=1.0, in1=chosen, op0=ALU.add, op1=ALU.mult))
            ve.tensor_scalar(posm, posm, -1.0, None, ALU.add)
            step(ve.tensor_copy(cnt, bank[:, 5, TT * E:TT * E + E]))
            step(ve.tensor_scalar(nblk, cnt, float(P), 1.0, ALU.is_gt, ALU.add))
            for b in (2, 3):
                step(ve.scalar_tensor_tensor(out=nblk, in0=cnt, scalar=float(b * P), in1=nblk, op0=ALU.is_gt, op1=ALU.add))
            step(ve.memset(scan, 0.0))
            step(ve.tensor_copy(scan[:, 0, 16:16 + E], nblk))
            for b in range(5):
                w = 1 << b
                step(ve.tensor_tensor(scan[:, (b + 1) % 2, 16:16 + E], scan[:, b % 2, 16:16 + E],
                                      scan[:, b % 2, 16 - w:16 + E - w], ALU.add))
            ends = scan[:, 1, 16:16 + E]
            step(ve.tensor_scalar(cmpe, ends, pcol[:, 0:1], None, ALU.is_le))
            step(ve.tensor_reduce(tiny[:, 0:1], cmpe, AX_X, ALU.add))
            step(ve.tensor_tensor(cmpn, cmpe, nblk, ALU.mult))
            step(ve.tensor_reduce(tiny[:, 1:2], cmpn, AX_X, ALU.add))
            step(ve.tensor_scalar(meta[:, 0:1], tiny[:, 0:1], float(E - 1), None, ALU.min))
            step(ve.tensor_tensor(meta[:, 1:2], pcol[:, 0:1], tiny[:, 1:2], ALU.subtract))
            step(ve.scalar_tensor_tensor(out=cmpn, in0=iota_e[:, :], scalar=meta[:, 0:1], in1=cnt,
                                         op0=ALU.is_equal, op1=ALU.mult))
            step(ve.tensor_reduce(tiny[:, 2:3], cmpn, AX_X, ALU.add))
            step(ve.scalar_tensor_tensor(out=tiny[:, 3:4], in0=meta[:, 1:2], scalar=-float(P), in1=tiny[:, 2:3],
                                         op0=ALU.mult, op1=ALU.add))
            step(ve.tensor_scalar(tiny[:, 5:6], meta[:, 1:2], 0.0, None, ALU.is_gt))
            step(ve.scalar_tensor_tensor(out=tiny[:, 4:5], in0=tiny[:, 3:4], scalar=float(WIDTHS[0]), in1=tiny[:, 5:6],
                                         op0=ALU.is_gt, op1=ALU.max))
            step(ve.scalar_tensor_tensor(out=meta[:, 2:3], in0=tiny[:, 3:4], scalar=float(WIDTHS[1]), in1=tiny[:, 4:5],
                                         op0=ALU.is_gt, op1=ALU.add))
            step(ve.tensor_scalar(tiny[:, 6:7], tiny[:, 4:5], -float(T), float(T), ALU.mult, ALU.add))
            step(ve.scalar_tensor_tensor(out=meta[:, 1:2], in0=meta[:, 1:2], scalar=float(P), in1=tiny[:, 6:7],
                                         op0=ALU.mult, op1=ALU.add))
            ve.tensor_copy(meta[:, 3:4], ends[:, E - 1:E]).then_inc(meta_ready, 1)
            ve.wait_ge(metarow_done, 1)
            ve.tensor_copy(meta_i, bank[0:1, 6, 0:4 * MI]).then_inc(meta_loaded, 1)
            ve.wait_ge(meta_loaded, 1)
            items = ve.value_load(meta_i[0:1, 3 * MI:3 * MI + 1], min_val=E, max_val=E + 15)

            def select(e, at):
                ve.tensor_copy(aux_now, aux[:, :, bass.ds(e, 1), :].rearrange("p t e a -> p t (e a)"))
                step_v(ve.tensor_copy(rel, posm[:, :, bass.ds(e, 1)].rearrange("p t e -> p (t e)")))
                for t in range(TT):
                    ins = ve.tensor_scalar(sel[:, t, :], pt[:, bass.ds(at, P)], rel[:, t:t + 1], None,
                                           ALU.is_equal)
                ins.then_inc(sel_ready, 1)

            step_v = Steps(ve, dve_moe)
            at0 = ve.value_load(meta_i[0:1, MI:MI + 1], min_val=0, max_val=T)
            select(0, at0)
            MOE_STEPS = 11
            ve.wait_ge(slot_idx, 1)
            ve.tensor_copy(slot_next, bank[:, 0, 0:2]).then_inc(slot_idx_read, 1)
            ve.wait_ge(bias_added, TT)
            with ve.Fori(0, items) as i:
                step_v = Steps(ve, dve_moe, i * MOE_STEPS + 1)
                e = ve.value_load(meta_i[0:1, bass.ds(i, 1)], min_val=0, max_val=E - 1)
                cls = ve.value_load(meta_i[0:1, bass.ds(i + 2 * MI, 1)], min_val=0, max_val=2)
                step_v(ve.tensor_copy(bias_now, biases[:, :, bass.ds(e, 1)].rearrange("p j e -> p (j e)")))
                e1 = ve.value_load(meta_i[0:1, bass.ds(i + 1, 1)], min_val=0, max_val=E - 1)
                at1 = ve.value_load(meta_i[0:1, bass.ds(i + 1 + MI, 1)], min_val=0, max_val=T)
                ve.wait_ge(slot_idx, i + 1)
                select(e1, at1)
                ve.wait_ge(rows_free, i + 1)
                ve.wait_ge(yrow_ready, i + 1)
                ve.wait_ge(slot_idx_read, i + 1)
                ve.tensor_copy(slot_now, slot_next)
                step_v(ve.tensor_scalar(slot_pad, slot_next[:, 0:1], 0.0, pcol[:, 1:2], ALU.is_equal, ALU.mult))
                ve.scalar_tensor_tensor(out=row_f, in0=slot_next[:, 0:1], scalar=-1.0, in1=slot_pad,
                                        op0=ALU.add, op1=ALU.add).then_inc(row_ready, 1)

                def swiglu(h, N, g_in, u_in):
                    lo, hi = 4 * h, 4 * h + 4
                    bg = bias_now[:, lo:hi].unsqueeze(2).to_broadcast([P, 4, N])
                    bu = bias_now[:, KF + lo:KF + hi].unsqueeze(2).to_broadcast([P, 4, N])
                    g_h, u_h, s_h, a_h = (v[:, lo:hi, 0:N] for v in (gate, up, sg, act))
                    ve.wait_ge(gu_t, 2 * i + h + 1)
                    step_v(ve.tensor_tensor(g_h, g_in, bg, ALU.add))
                    ve.tensor_scalar(g_h, g_h, LIMIT, None, ALU.min).then_inc(gated, 1)
                    step_v(ve.tensor_tensor(u_h, u_in, bu, ALU.add))
                    step_v(ve.tensor_scalar(u_h, u_h, LIMIT, -LIMIT, ALU.min, ALU.max))
                    step_v(ve.scalar_tensor_tensor(out=u_h, in0=u_h, scalar=1.0, in1=g_h, op0=ALU.add, op1=ALU.mult))
                    ve.wait_ge(sig_done, 2 * i + h + 1)
                    ve.tensor_tensor(a_h, u_h, s_h, ALU.mult).then_inc(act_ready, 1)

                with ve.If(cls < 1):
                    ve.wait_ge(row_ready, i + 1)
                    ve.scalar_tensor_tensor(out=idx[:, :], in0=row_f, scalar=2.0, in1=pcol[:, 2:3],
                                            op0=ALU.mult, op1=ALU.add).then_inc(now_ready, 1)
                    ve.sem_inc(gu_out_b, 2)
                    n_steps = step_v.n
                    for h in range(2):
                        both = bank[:, 2 + h, :].rearrange("p (k a c) -> p k a c", k=4, a=2)
                        swiglu(h, HW, both[:, :, 0, :], both[:, :, 1, :])
                with ve.Else():
                    step_v.n = n_steps
                    ve.wait_ge(row_ready, i + 1)
                    ve.tensor_copy(idx[:, :], row_f).then_inc(now_ready, 1)
                    for h in range(2):
                        ve.wait_ge(gu_done, 2 * i + h + 1)
                        ve.tensor_copy(gu_tok[:, 2 + h, :], bank[:, 2 + h, :]).then_inc(gu_out_b, 1)
                    for h in range(2):
                        swiglu(h, P, bank[:, h, :].rearrange("p (k c) -> p k c", k=4),
                               bank[:, 2 + h, :].rearrange("p (k c) -> p k c", k=4))
                ve.wait_ge(slot_idx, i + 2)
                ve.tensor_copy(slot_next, bank[:, 0, 0:2]).then_inc(slot_idx_read, 1)
                assert step_v.n == MOE_STEPS, step_v.n

        @block.tensor
        def _(pe):
            pe.wait_ge(psum_clear, 1)
            pe.wait_ge(consts, 3)
            pe.wait_ge(s_small, 16 * SMALL)
            for b in range(SETUP):
                if b >= 4:
                    pe.wait_ge(setup_e, b - 3)
                for a in range(4):
                    dst = bank[:, 4 + b % 4, :]
                    if b < SG // 4:
                        ins = pe.transpose(dst[:, a * P:(a + 1) * P], wsp_raw[:, 4 * b + a, :], ident[:, :])
                    elif b == SG // 4:
                        if a == 0:
                            ins = pe.transpose(dst[:, 0:SG], bsp_raw, ident[0:SG, 0:SG])
                    else:
                        j = 4 * (b - SG // 4 - 1) + a
                        ins = pe.transpose(dst[:, a * E:(a + 1) * E], bias_raw[:, j * P:(j + 1) * P], ident[0:E, 0:E])
                ins.then_inc(setup_t, 1)
            pe.wait_ge(xr_ready, TT)
            for k in range(KD):
                if k >= 4:
                    pe.wait_ge(hT_e, k - 3)
                for t in range(TT):
                    ins = pe.transpose(bank[:, k % 4, t * P:(t + 1) * P], xr[:, t, k * P:(k + 1) * P], ident[:, :])
                ins.then_inc(hT_t, 1)
            pe.wait_ge(hT_e, KD)
            pe.wait_ge(setup_e, SETUP)

            def project(out_bank, group, t, slot):
                w = stream[slot].rearrange("p (k n) -> p k n", k=KD)
                for k in range(KD):
                    ins = pe.matmul(bank[:, out_bank, 0:CW], order_cols(hT[:, k, :], group, t), w[:, k, :],
                                    start=(k == 0), stop=(k == KD - 1))
                return ins

            with pe.Fori(0, 3) as kind:
                for g in range(GROUPS):
                    pe.wait_ge(s_chunk[g], 16 * (kind + 1))
                    for t in range(TT):
                        n = g * TT + t
                        pe.wait_ge(proj_read, 12 * kind + n + 1)
                        project(n % 2, g, t, g).then_inc(proj_done, 1)

            def transpose_pair(s):
                g, r = divmod(s, 4)
                kind, pair = r // 2, 2 * g + r % 2
                pe.wait_ge(roped, TT * (kind + 1))
                if s >= 1:
                    pe.wait_ge(pair_e, s)
                for t in range(TT):
                    ins = pe.transpose(bank[:, 6, t * P:(t + 1) * P], qk[:, kind, t, pair * P:(pair + 1) * P], ident[:, :])
                ins.then_inc(pair_t, 1)

            def scores(u):
                g, j = divmod(u, 4)
                W = unit_width(u)
                k0 = unit_blocks(u)[0] * P
                pe.wait_ge(pair_e, 4 * (g + 1))
                pe.wait_ge(max_done, u)
                for h in range(HPG):
                    par, i = divmod(h, 2)
                    d = slice(par * HD, par * HD + HD)
                    ins = pe.matmul(bank[:, 2 + par, i * W:(i + 1) * W], qkT[d, 2 * g + i, j * P:(j + 1) * P],
                                    qkT[d, KA + 2 * g + i, k0:k0 + W], start=True, stop=True)
                ins.then_inc(score_done, 1)

            def transpose_p(u):
                W = unit_width(u)
                pe.wait_ge(prob_done, u + 1)
                pe.wait_ge(pt_e, u)
                dst = bank[:, 4:6, :].rearrange("p a n -> p (a n)")
                for c in range(HPG * W // P):
                    ins = pe.transpose(dst[:, c * P:(c + 1) * P], sc[:, u % 2, c * P:(c + 1) * P], ident[:, :])
                ins.then_inc(pt_t, 1)

            def weighted(u):
                g, j = divmod(u, 4)
                blocks = unit_blocks(u)
                nb = len(blocks)
                pe.wait_ge(pt_e, u + 1)
                pe.wait_ge(o_read, u)
                for h in range(HPG):
                    par, i = divmod(h, 2)
                    head = g * HPG + 2 * i + par
                    for b, tile in enumerate(blocks):
                        ins = pe.matmul(bank[par * HD:(par + 1) * HD, 7, i * P:(i + 1) * P],
                                        vtok[:, tile, head * HD:(head + 1) * HD],
                                        pt[:, (h * nb + b) * P:(h * nb + b + 1) * P], start=(b == 0), stop=(b == nb - 1))
                ins.then_inc(o_done, 1)

            for s in range(SLOTS):
                if s < 24:
                    c, t = divmod(s, TT)
                    if t == 0:
                        pe.wait_ge(s_chunk[c % 3], 16 * (3 + c // 3 + 1))
                    pe.wait_ge(proj_read, 36 + s + 1)
                    ins = project(s % 2, 0, t, c % 3)
                    ins.then_inc(proj_done, 1)
                if s < 12:
                    transpose_pair(s)
                if s % 2 == 1 and 5 <= s < 29:
                    scores((s - 5) // 2)
                if s % 2 == 1 and 7 <= s < 31:
                    transpose_p((s - 7) // 2)
                if s % 2 == 0 and 8 <= s < 31:
                    weighted((s - 8) // 2)
            pe.wait_ge(o_read, 12)
            for a, stat in enumerate((mstat, lstat)):
                for g in range(GROUPS):
                    for j in range(4):
                        ins = pe.transpose(bank[0:HPG, 2 + 3 * a + g, j * P:(j + 1) * P], stat[:, 4 * g + j, :], ident[:, :])
                    ins.then_inc(ml_t, 1)
            pe.wait_ge(ln_done, TT)
            pe.wait_ge(proj_read, 62)
            for g in range(SG):
                if g >= 2:
                    pe.wait_ge(mix_read, g - 1)
                pe.matmul(bank[:, g % 2, 0:TT * HD].rearrange("p (t d) -> p t d", t=TT), wspT[:, g, :],
                          ztok[:, :, g * HD:(g + 1) * HD], start=True, stop=True).then_inc(mix_done, 1)
            pe.wait_ge(ml_e, 6)
            pe.wait_ge(wrow_ready, 1)
            pe.wait_ge(consts, CONSTS)
            for k in range(KA):
                g, i = divmod(k, 2)
                pe.matmul(bank[:, 2 + k, :], pick[:, i, :], wrow[:, g, :], start=True, stop=True).then_inc(spread_done, 1)
            pe.wait_ge(mix_read, SG)
            for k in range(KA):
                pe.wait_ge(spread_read, k + 1)
                for t in range(TT):
                    ins = pe.transpose(bank[:, 2 + k, t * P:(t + 1) * P], utok[:, t, k * P:(k + 1) * P], ident[:, :])
                ins.then_inc(sgu_t, 1)
            pe.wait_ge(sgu_e, KA)
            with pe.Fori(0, PAIRS) as i:
                for part in range(4):
                    w = stream[part]
                    pe.wait_ge(s_chunk[part], 16 * (i + (6 if part < 3 else 1)))
                    for jj in range(2):
                        free = gate_read if part < 2 else y_read
                        rhs, kt = (hT, KD) if part < 2 else (attnT, KA) if part == 2 else (sguT, KA)
                        pe.wait_ge(free, 4 * i + 2 * (part % 2) + jj + 1)
                        for k in range(kt):
                            ins = pe.matmul(bank[:, 4 * jj + part, :], w[:, k * CW + jj * P:k * CW + (jj + 1) * P],
                                            rhs[:, k, :], start=(k == 0), stop=(k == kt - 1))
                        ins.then_inc(gate_done if part < 2 else y_done, 1)
            pe.wait_ge(merged, 2 * PAIRS + 1)
            pe.wait_ge(gate_read, 4 + 4 * PAIRS)
            for c in range(PAIRS):
                w = stream[c].rearrange("p (k n) -> p k n", k=KD)
                pe.wait_ge(s_chunk[c], 16 * chunk_turn[15 + 4 * PAIRS + c])
                for t in range(TT):
                    n = c * TT + t
                    if n >= 2:
                        pe.wait_ge(out_read, n - 1)
                    for k in range(KD):
                        ins = pe.matmul(bank[:, n % 2, 0:CW], mergedT[:, k, t * P:(t + 1) * P], w[:, k, :],
                                        start=(k == 0), stop=(k == KD - 1))
                    ins.then_inc(out_done, 1)
            pe.wait_ge(out_read, 4 * PAIRS)
            for t in range(TT):
                pe.wait_ge(hf_ready, t + 1)
                if t >= 2:
                    pe.wait_ge(hf_e, t - 1)
                for k in range(KD):
                    ins = pe.transpose(bank[:, 2 * (t % 2) + k // 4, (k % 4) * P:(k % 4 + 1) * P],
                                       hf[:, t, k * P:(k + 1) * P], ident[:, :])
                ins.then_inc(hf_t, 1)
            for t in range(TT):
                pe.wait_ge(hf_e, t + 1)
                for k in range(KD):
                    ins = pe.matmul(bank[:, 4, t * E:(t + 1) * E], hfT[:, k, t * P:(t + 1) * P], wr[:, k, :],
                                    start=(k == 0), stop=(k == KD - 1))
            ins.then_inc(logit_done, 1)
            pe.wait_ge(chosen_ready, 1)
            for t in range(TT):
                for s in range(t + 1):
                    pe.matmul(bank[:, 5, t * E:(t + 1) * E], upper[:, :] if s == t else ones[:, :], chosen[:, s, :],
                              start=(s == 0), stop=(s == t))
            for s in range(TT):
                ins = pe.matmul(bank[:, 5, TT * E:TT * E + E], ones[:, :], chosen[:, s, :],
                                start=(s == 0), stop=(s == TT - 1))
            ins.then_inc(place_done, 1)
            pe.wait_ge(gates_ready, 1)
            pe.wait_ge(s_g2, 32)
            for t in range(TT):
                ins = pe.transpose(bank[0:E, 7, t * P:(t + 1) * P], gates[:, t, :], ident[:, :])
            ins.then_inc(gatesT_t, 1)
            pe.wait_ge(gatesT_e, 1)
            for t in range(TT):
                if t >= 2:
                    pe.wait_ge(bsum_read, t - 1)
                for b in range(2):
                    ins = pe.matmul(bank[:, 2 * (t % 2) + b, :], gatesT[:, t * P:(t + 1) * P], bdn[:, b * BW:(b + 1) * BW],
                                    start=True, stop=True)
                ins.then_inc(bsum_done, 1)
            pe.wait_ge(meta_ready, 1)
            for c in range(4):
                ins = pe.matmul(bank[0:1, 6, c * MI:(c + 1) * MI], meta[:, c:c + 1], ident[:, 0:MI], start=True, stop=True)
            ins.then_inc(metarow_done, 1)
            pe.wait_ge(meta_loaded, 1)
            items = pe.value_load(meta_i[0:1, 3 * MI:3 * MI + 1], min_val=E, max_val=E + 15)

            def by_width(cls, work_at):
                with pe.If(cls < 1):
                    work_at(WIDTHS[0])
                with pe.Else():
                    with pe.If(cls < 2):
                        work_at(WIDTHS[1])
                    with pe.Else():
                        work_at(P)

            def gather(half, N):
                for d in range(4 * half, 4 * half + 4):
                    for t in range(TT):
                        ins = pe.matmul(bank[:, 6 + half, (d % 4) * P:(d % 4) * P + N], hf[:, t, d * P:(d + 1) * P],
                                        sel[:, t, 0:N], start=(t == 0), stop=(t == TT - 1))
                ins.then_inc(gather_done, 1)

            def slots_of():
                for t in range(TT):
                    ins = pe.matmul(bank[:, 0, 0:2], sel[:, t, :], aux_now[:, t, :], start=(t == 0), stop=(t == TT - 1))
                ins.then_inc(slot_idx, 1)

            cls0 = pe.value_load(meta_i[0:1, 2 * MI:2 * MI + 1], min_val=0, max_val=2)
            pe.wait_ge(sel_ready, 1)

            def first_gather(N):
                gather(0, N)
                gather(1, N)

            by_width(cls0, first_gather)
            pe.wait_ge(bsum_read, TT)
            slots_of()
            with pe.Fori(0, items) as i:
                cls = pe.value_load(meta_i[0:1, bass.ds(i + 2 * MI, 1)], min_val=0, max_val=2)
                cls1 = pe.value_load(meta_i[0:1, bass.ds(i + 1 + 2 * MI, 1)], min_val=0, max_val=2)
                pe.wait_ge(gather_read, 2 * i + 2)
                pe.wait_ge(slot_idx_read, i + 1)

                def gate_up(halves):
                    for k in range(KD):
                        pe.wait_ge(s_slot[k], 16 * (i + 1))
                        for h in range(2):
                            for a in range(2):
                                out_ap, x_k = ((bank[a * HW:(a + 1) * HW, h, :], xgT[:, k, 0:HW]) if halves else
                                               (bank[:, 2 * a + h, :], xgT[:, k, :]))
                                at = a * F + h * BW
                                ins = pe.matmul(out_ap, x_k, ring[:, k, at:at + BW], start=(k == 0), stop=(k == KD - 1))
                            if k == KD - 1:
                                ins.then_inc(gu_done, 1)
                        if k < KD - 1:
                            ins.then_inc(slot_used, 1)

                def transpose_gu(halves):
                    for h in range(2):
                        pe.wait_ge(gu_out_a, 2 * i + h + 1)
                        pe.wait_ge(gu_out_b, 2 * i + h + 1)
                        for j in range(4):
                            f = slice(j * P, (j + 1) * P)
                            if halves:
                                ins = pe.transpose(bank[:, 2 + h, f], gu_tok[:, h, f], ident[:, :])
                            else:
                                pe.transpose(bank[:, h, f], gu_tok[:, h, f], ident[:, :])
                                ins = pe.transpose(bank[:, 2 + h, f], gu_tok[:, 2 + h, f], ident[:, :])
                        ins.then_inc(gu_t, 1)

                with pe.If(cls < 1):
                    gate_up(True)
                    transpose_gu(True)
                with pe.Else():
                    gate_up(False)
                    transpose_gu(False)
                pe.wait_ge(sel_ready, i + 2)
                by_width(cls1, lambda N: gather(0, N))
                pe.wait_ge(yrow_ready, i + 1)

                def down(halves):
                    for j in range(KF):
                        s = KD + j // 2
                        if j % 2 == 0:
                            pe.wait_ge(s_slot[s], 16 * (i + 1))
                        if j % 4 == 0:
                            pe.wait_ge(act_ready, 2 * i + j // 4 + 1)
                        for b in range(2):
                            out_ap, a_j = ((bank[b * HW:(b + 1) * HW, 4, :], act[:, j, 0:HW]) if halves else
                                           (bank[:, 4 + b, :], act[:, j, :]))
                            at = (j % 2) * D + b * BW
                            ins = pe.matmul(out_ap, a_j, ring[:, s, at:at + BW], start=(j == 0), stop=(j == KF - 1))
                        if j % 2 == 1 and j < KF - 1:
                            ins.then_inc(slot_used, 1)
                    ins.then_inc(down_done, 1)

                with pe.If(cls < 1):
                    down(True)
                with pe.Else():
                    down(False)
                by_width(cls1, lambda N: gather(1, N))
                slots_of()


_INS = ["x", "positions", "norm1_g", "w_in", "q_norm_g", "k_norm_g", "sgu_ln_g", "sgu_ln_b", "w_spatial", "b_spatial",
        "w_branch_a", "w_branch_b", "w_out", "norm2_g", "w_router", "b_router", "w_gate_up", "b_gate_up", "w_down",
        "b_down"]


def kernel(**inputs):
    import concourse.bacc as bacc
    from concourse.bass_utils import run_bass_kernel_spmd

    nc = bacc.Bacc("TRN2", target_bir_lowering=False, num_devices=1)
    arrays, args = {}, []
    for name in _INS:
        a = np.ascontiguousarray(inputs[name])
        arrays[f"in_{name}"] = a
        args.append(nc.dram_tensor(f"in_{name}", a.shape, mybir.dt.from_np(a.dtype), kind="ExternalInput").ap())
    shape = tuple(inputs["x"].shape)
    args.append(nc.dram_tensor("out_y", shape, F32, kind="ExternalOutput").ap())
    hybrid_layer(nc, *args)
    r = run_bass_kernel_spmd(nc, [arrays], core_ids=[0])
    return r.results[0]["out_y"]
```

```python
from contextlib import ExitStack

import numpy as np
import concourse.bass as bass
from concourse import mybir

P = 128
F32 = mybir.dt.float32
I32 = mybir.dt.int32
U32 = mybir.dt.uint32
ALU = mybir.AluOpType
ACT = mybir.ActivationFunctionType
AX_X = mybir.AxisListType.X
WIDTHS = (64, 96, 128)
HW = WIDTHS[0]
QW = 32
ROUNDS = ((2, 0, 0, 0), (1, 2, 1, 2), (3, 3, 3, 1))


def tile_slots(c, b):
    return QW * (b if c == 3 else c)


def by_class(eng, cls, work):
    with eng.If(cls < 1):
        work(0)
    with eng.Else():
        with eng.If(cls < 2):
            work(1)
        with eng.Else():
            work(2)

ROUND = 1.5 * 2.0 ** 23
PI_IN = 3.1415925
TWO_PI = (6.28125, 0.0019354820251464844, -1.7484556025237907e-07)


class Steps:

    def __init__(self, eng, sem, before=0):
        self.eng, self.sem, self.before, self.n = eng, sem, before, 0

    def __call__(self, ins):
        ins.then_inc(self.sem, 1)
        self.n += 1
        self.eng.wait_ge(self.sem, self.before + self.n)


def hybrid_layer(nc, x, positions, norm1_g, w_in, q_norm_g, k_norm_g, sgu_ln_g, sgu_ln_b, w_spatial,
                 b_spatial, w_branch_a, w_branch_b, w_out, norm2_g, w_router, b_router, w_gate_up,
                 b_gate_up, w_down, b_down, out):
    _, T, D = x.shape
    TT = T // P
    KD = D // P
    HD = q_norm_g.shape[1]
    HALF = HD // 2
    AW = w_branch_a.shape[1]
    KA = AW // P
    HEADS = AW // HD
    GROUPS = 3
    HPG = HEADS // GROUPS
    GW = HPG * HD
    SG = w_spatial.shape[1]
    SW = SG * HD
    E = w_router.shape[2]
    F = w_down.shape[2]
    KF = F // P
    TOPK = 4
    CW = 256
    PAIRS = D // CW
    CH = KD * CW
    EPS = 1e-6
    NEG = -1e30
    SCALE = float(HD) ** -0.5
    LIMIT, ALPHA = 7.0, 1.702
    COL_V = 3 * AW + SW
    COL_U = 3 * AW
    COL_GA = 3 * AW + 2 * SW
    COL_GB = COL_GA + D
    assert T == 4 * P and GW == CW and SW == AW and D == F and KD == 8
    RING = KD + KF // 2
    BW = D // 2

    with ExitStack() as ctx:
        def sb(name, shape, dt=F32):
            return ctx.enter_context(nc.sbuf_tensor(name, shape, dt))

        def sem(name):
            return ctx.enter_context(nc.semaphore(name))

        SLOT = 2 * F
        ring = sb("ring", [P, RING, SLOT])
        flat = ring[:, :, :].rearrange("p s n -> p (s n)")
        qk = flat[:, 0:2 * TT * AW].rearrange("p (k t n) -> p k t n", k=2, t=TT)
        at = 2 * TT * AW
        vtok = flat[:, at:at + TT * AW].rearrange("p (t n) -> p t n", t=TT)
        at += TT * AW
        utok = flat[:, at:at + TT * SW].rearrange("p (t n) -> p t n", t=TT)
        at += TT * SW
        ztok = flat[:, at:at + TT * SW].rearrange("p (t n) -> p t n", t=TT)
        assert at + TT * SW <= 8 * SLOT
        xr = flat[:, 0:TT * D].rearrange("p (t n) -> p t n", t=TT)
        trig = flat[:, TT * D:TT * D + 4 * 8 * HALF].rearrange("p (a u c) -> p a u c", a=4, c=HALF)
        stream = [ring[:, 8 + s, :] for s in range(4)]
        mlrow = flat[0:HPG, 0:6 * T].rearrange("p (a g t) -> p a g t", a=2, g=GROUPS)
        wrow = flat[0:HPG, 6 * T:9 * T].rearrange("p (g t) -> p g t", g=GROUPS)
        mrow = flat[0:HPG, 9 * T:10 * T]
        drow = flat[0:HPG, 10 * T:11 * T]

        work = sb("work", [P, 20480])
        o_x, o_h, o_qk, o_a, o_s = 0, 4096, 8192, 14336, 17408
        xs = work[:, o_x:o_x + TT * D].rearrange("p (t n) -> p t n", t=TT)
        hT = work[:, o_h:o_h + KD * T].rearrange("p (k t) -> p k t", k=KD)
        qkT = work[:, o_qk:o_qk + 12 * T].rearrange("p (k t) -> p k t", k=12)
        mergedT = work[:, o_qk:o_qk + KD * T].rearrange("p (k t) -> p k t", k=KD)
        g2b = work[:, o_qk + KD * T:o_qk + KD * T + D]
        attnT = work[:, o_a:o_a + KA * T].rearrange("p (k t) -> p k t", k=KA)
        sguT = work[:, o_s:o_s + KA * T].rearrange("p (k t) -> p k t", k=KA)
        bias_raw = work[0:E, o_qk:o_qk + 2 * F]
        bdn = work[0:E, o_qk + (KD * T) + D:o_qk + (KD * T) + 2 * D]
        wsp_raw = work[:, o_a:o_a + SG * P].rearrange("p (g s) -> p g s", g=SG)
        bsp_raw = work[0:SG, o_a + SG * P:o_a + SG * P + P]
        lnb = work[:, o_s:o_s + 2 * SW].rearrange("p (a n) -> p a n", a=2)
        hf = work[:, o_a:o_a + TT * D].rearrange("p (t n) -> p t n", t=TT)
        hfT = hT
        xgT = work[:, o_qk:o_qk + KD * P].rearrange("p (k c) -> p k c", k=KD)
        yrow = work[:, o_qk + D:o_qk + 2 * D]
        xg_tok = work[:, o_qk + 4 * D:o_qk + 5 * D]
        gu_tok = work[:, o_qk + 2 * D:o_qk + 4 * D].rearrange("p (b n) -> p b n", b=4)
        bsum = work[:, o_h:o_h + TT * D].rearrange("p (t n) -> p t n", t=TT)
        gate = work[:, o_h:o_h + D].rearrange("p (k c) -> p k c", k=KF)
        up = work[:, o_h + D:o_h + 2 * D].rearrange("p (k c) -> p k c", k=KF)
        sg = work[:, o_h + 2 * D:o_h + 3 * D].rearrange("p (k c) -> p k c", k=KF)
        act = work[:, o_h + 3 * D:o_h + 4 * D].rearrange("p (k c) -> p k c", k=KF)
        sel = work[:, o_a + TT * D:o_a + TT * D + TT * P].rearrange("p (t c) -> p t c", t=TT)
        aux_at = o_a + TT * D + TT * P
        aux = work[:, aux_at:aux_at + TT * E * 2].rearrange("p (t e a) -> p t e a", t=TT, e=E)
        hot_at = aux_at + TT * E * 2
        hot = work[:, hot_at:hot_at + TT * TOPK * E].rearrange("p (t k e) -> p t k e", t=TT, k=TOPK)
        hotg_at = hot_at + TT * TOPK * E
        hotg = work[:, hotg_at:hotg_at + TT * TOPK * E].rearrange("p (t k e) -> p t k e", t=TT, k=TOPK)
        assert hotg_at + TT * TOPK * E <= 20480

        sc = sb("sc", [P, 2, 1024])
        pt = sb("pt", [P, 1024])
        dist = pt[:, 0:P].bitcast(I32)
        slots_iota, slots_twice = pt[:, 0:T], pt[:, T:T + P]
        ident = sb("ident", [P, P])
        upper = sb("upper", [P, P])
        ones = sb("ones", [P, P])
        wspT = sb("wspT", [P, SG, P])
        cos_t = sb("cos_t", [P, 8, HALF])
        sin_t = sb("sin_t", [P, 8, HALF])
        band = sb("band", [P, 2 * P])
        diag = sb("diag", [P, P])
        qkg = sb("qkg", [P, 2, HD])
        biases = sb("biases", [P, 2 * KF, E])
        wr = sb("wr", [P, KD, E])
        brb = sb("brb", [P, E])
        pick = sb("pick", [HPG, 2, P])
        bsp = sb("bsp", [P, SG])
        g1 = sb("g1", [P, KD])
        pos_i = sb("pos_i", [P, 8], I32)
        pos_f = sb("pos_f", [P, 8])
        inv_f = sb("inv_f", [P, HALF])
        ss = sb("ss", [P, TT])
        rs = sb("rs", [P, TT])
        hss = sb("hss", [P, 2, TT, HEADS])
        mstat = sb("mstat", [P, 12, HPG])
        nmstat = sb("nmstat", [P, 12, HPG])
        lstat = sb("lstat", [P, 12, HPG])
        bn = sb("bn", [P, TT, 2, 6])
        mv = sb("mv", [P, TT, 2])
        iota_e = sb("iota_e", [P, E])
        pcol = sb("pcol", [P, 3])
        tiny = sb("tiny", [P, 16])
        MI = 64
        meta_i = cos_t[0:1, 0:4 * MI // HALF, :].rearrange("p a c -> p (a c)").bitcast(I32)
        idx = sb("idx", [P, 1], U32)
        idx_next = sb("idx_next", [P, 1], U32)
        scf = sc[:, :, :].rearrange("p a n -> p (a n)")
        lg = scf[:, 0:128].rearrange("p (t e) -> p t e", t=TT)
        top = scf[:, 128:160].rearrange("p (t k) -> p t k", t=TT)
        topi = scf[:, 160:192].bitcast(U32).rearrange("p (t k) -> p t k", t=TT)
        topf = scf[:, 192:208].rearrange("p (t k) -> p t k", t=TT)
        ge = scf[:, 208:224].rearrange("p (t k) -> p t k", t=TT)
        gsum = scf[:, 224:228]
        chosen = scf[:, 256:384].rearrange("p (t e) -> p t e", t=TT)
        posm = scf[:, 384:512].rearrange("p (t e) -> p t e", t=TT)
        cnt = scf[:, 512:544]
        nblk = scf[:, 544:576]
        scan = scf[:, 576:576 + 96].rearrange("p (a n) -> p a n", a=2)
        cmpe = scf[:, 672:704]
        cmpn = scf[:, 704:736]
        meta = scf[:, 736:740]
        bias_now = scf[:, 768:768 + 2 * KF]
        aux_now = scf[:, 800:800 + 2 * TT].rearrange("p (t a) -> p t a", t=TT)
        slot_now = scf[:, 810:812]
        slot_next = scf[:, 812:814]
        slot_pad = scf[:, 814:815]
        rel = scf[:, 816:820]
        row_f = scf[:, 820:821]
        row_next = scf[:, 821:822]
        gates = scf[:, 1024:1024 + TT * E].rearrange("p (t e) -> p t e", t=TT)
        gatesT = scf[0:E, 1280:1280 + T]

        bank = ctx.enter_context(nc.psum_tensor("bank", [P, 8, 512], F32))

        y_acc = nc.dram_tensor("y_acc", [T + P, D], F32, kind="Internal").ap()
        hf_rows = nc.dram_tensor("hf_rows", [T + P, D], F32, kind="Internal").ap()
        y_halves = y_acc.rearrange("t (h n) -> (t h) n", h=2)

        s_x, s_small, s_g2 = sem("x_loaded"), sem("small_loaded"), sem("g2_loaded")
        psum_clear, trig_ready, trig_done = sem("psum_clear"), sem("trig_ready"), sem("trig_done")
        consts2, ln_scaled = sem("moe_consts_made"), sem("ln_scaled")
        s_chunk = [sem(f"chunk_loaded{s}") for s in range(4)]
        consts = sem("consts_made")
        dve_step, act_step, pool_step = sem("dve_step"), sem("act_step"), sem("pool_step")
        dve_moe = sem("dve_moe_step")
        rms_sum, rms_var, rms_root, xr_ready = sem("rms_sum"), sem("rms_var"), sem("rms_root"), sem("xr_ready")
        setup_t, setup_e = sem("setup_transposed"), sem("setup_evacuated")
        hT_t, hT_e = sem("hT_transposed"), sem("hT_evacuated")
        proj_done, proj_read = sem("proj_done"), sem("proj_read")
        sq_done, sq_read, hvar, hroot = sem("squares_done"), sem("squares_read"), sem("head_var"), sem("head_root")
        scaled, gained, roped = sem("qk_scaled"), sem("qk_gained"), sem("qk_roped")
        pair_t, pair_e = sem("pair_transposed"), sem("pair_evacuated")
        score_done, max_done, prob_done = sem("score_done"), sem("max_done"), sem("prob_done")
        pt_t, pt_e, o_done, o_read = sem("probT_done"), sem("probT_evacuated"), sem("o_done"), sem("o_read")
        ztok_ready, utok_ready, ln_var, ln_root, ln_done = (
            sem("z_gelu"), sem("u_gelu"), sem("ln_var"), sem("ln_root"), sem("ln_done"))
        ml_t, ml_e, gexp_in, gexp, wrow_ready = sem("ml_t"), sem("ml_e"), sem("gexp_in"), sem("gexp"), sem("wrow_ready")
        mix_done, mix_read = sem("mix_done"), sem("mix_read")
        spread_done, spread_read = sem("spread_done"), sem("spread_read")
        sgu_t, sgu_e = sem("sgu_transposed"), sem("sgu_evacuated")
        gate_done, gate_read, y_done, y_read = sem("gate_done"), sem("gate_read"), sem("branch_done"), sem("branch_read")
        part_b, merged = sem("part_b"), sem("merged")
        out_done, out_read = sem("out_done"), sem("out_read")
        x1_stored = sem("x1_stored")
        rms2_sum, rms2_var, rms2_root, hf_ready = sem("rms2_sum"), sem("rms2_var"), sem("rms2_root"), sem("hf_ready")
        hf_t, hf_e, logit_done = sem("hf_transposed"), sem("hf_evacuated"), sem("logits_done")
        topd, topexp, chosen_ready, place_done, meta_ready, metarow_done, meta_loaded = (
            sem("top_diff"), sem("top_exp"), sem("chosen_ready"), sem("places_done"), sem("meta_ready"),
            sem("meta_rows"), sem("meta_loaded"))
        s_slot = [sem(f"slot_loaded{s}") for s in range(RING)]
        slot_used = sem("slot_used")
        sel_ready, hf_stored, next_rows, x_gathered = (
            sem("sel_ready"), sem("hf_stored"), sem("next_rows_known"), sem("x_gathered"))
        xg_t, xg_e, gather_turn = sem("xg_transposed"), sem("xg_evacuated"), sem("gather_turn")
        gu_done, gated, sig_done, act_ready, up_read = (
            sem("gate_up_done"), sem("gate_ready"), sem("sigmoid_done"), sem("act_ready"), sem("gu_read"))
        down_done, yrow_ready, y_added = sem("down_done"), sem("yrow_ready"), sem("y_added")
        gu_out_a, gu_out_b, gu_t = sem("gate_up_out_a"), sem("gate_up_out_b"), sem("gate_up_transposed")
        gates_ready, gatesT_t, gatesT_e, bsum_done, bsum_read, bias_added = (
            sem("gates_ready"), sem("gatesT_transposed"), sem("gatesT_evacuated"), sem("bias_sum_done"),
            sem("bias_sum_read"), sem("bias_added"))
        slot_idx, slot_idx_read, now_ready = sem("slot_idx_done"), sem("slot_idx_read"), sem("slot_now_ready")
        row_ready = sem("slot_rows_ready")
        out_stored, add_turn, rows_free = sem("out_stored"), sem("add_turn"), sem("rows_free")


        block = ctx.enter_context(nc.Block())

        pos = positions[0]
        smalls = [
            (pos_i[:, 0:4], pos.rearrange("(j p) -> p j", p=P)),
            (pos_i[:, 4:8], pos.rearrange("(p j) -> p j", p=P)),
            (g1[:, :], norm1_g[0].rearrange("(k p) -> p k", p=P)),
            (qkg[:, 0, :], q_norm_g[0].partition_broadcast(P)),
            (qkg[:, 1, :], k_norm_g[0].partition_broadcast(P)),
            (wsp_raw, w_spatial[0].rearrange("g t s -> t g s")),
            (bsp_raw, b_spatial[0]),
            (bias_raw[:, 0:2 * F], b_gate_up[0]),
            (wr[:, :, :], w_router[0].rearrange("(k p) e -> p k e", p=P)),
            (brb[:, :], b_router[0].partition_broadcast(P)),
            (lnb[:, 0, :], sgu_ln_g[0].partition_broadcast(P)),
            (lnb[:, 1, :], sgu_ln_b[0].partition_broadcast(P)),
        ]
        SMALL = len(smalls)
        SETUP = SG // 4 + 1 + 2 * KF // 4
        CONSTS = 5
        SLOTS = 31

        def unit_blocks(u):
            return [u % 4 - 1, u % 4] if 0 < u < 4 else [u % 4]

        def unit_width(u):
            return P * len(unit_blocks(u))

        def unit_mask(u):
            return band[:, :] if 0 < u < 4 else band[:, P:2 * P] if u < 8 else diag[:, :]

        def heads(ap, width):
            return ap[:, 0:HPG * width].rearrange("p (h w) -> p h w", h=HPG)

        def order_cols(ap, group, j):
            if group == 0:
                return ap[:, j * P:(j + 1) * P]
            return ap[:, j:T:4]

        def chunk_src(n):
            if n < 9:
                return w_in, n * CW, KD
            if n < 12:
                return w_in, COL_V + (n - 9) * CW, KD
            if n < 15:
                return w_in, COL_U + (n - 12) * CW, KD
            if n < 15 + 4 * PAIRS:
                i, s = divmod(n - 15, 4)
                w, c, k = [(w_in, COL_GA, KD), (w_in, COL_GB, KD), (w_branch_a, 0, KA), (w_branch_b, 0, KA)][s]
                return w, c + i * CW, k
            return w_out, (n - 15 - 4 * PAIRS) * CW, KD

        def chunk_slot(n):
            return n % 3 if n < 15 else (n - 15) % 4

        CHUNKS = 15 + 5 * PAIRS

        def chunk_used(n):
            if n < 15:
                return proj_done, TT * (n + 1)
            if n < 15 + 4 * PAIRS:
                i, part = divmod(n - 15, 4)
                return (gate_done, y_done)[part // 2], 4 * i + 2 * (part % 2) + 2
            return out_done, TT * (n - 15 - 4 * PAIRS + 1)

        chunk_turn = [sum(chunk_slot(m) == chunk_slot(n) for m in range(n + 1)) for n in range(CHUNKS)]

        @block.sync
        def _(sp):
            for t in range(TT):
                sp.dma_start(xs[:, t, :], x[0, t * P:(t + 1) * P, :]).then_inc(s_x, 16)
            last = {}
            for n in range(CHUNKS):
                w, c, k = chunk_src(n)
                s = chunk_slot(n)
                if s in last:
                    sp.wait_ge(*chunk_used(last[s]))
                last[s] = n
                sp.dma_start(stream[s][:, 0:k * CW].rearrange("p (k n) -> p k n", k=k),
                             w[0].rearrange("(k p) n -> p k n", p=P)[:, :, c:c + CW]).then_inc(s_chunk[s], 16)
            sp.wait_ge(o_read, 12)
            sp.dma_start(g2b, norm2_g[0].partition_broadcast(P)).then_inc(s_g2, 16)
            sp.dma_start(bdn, b_down[0]).then_inc(s_g2, 16)
            sp.wait_ge(sgu_t, KA)
            sp.wait_ge(spread_done, KA)

            def slot_copy(s, gate_up, down):
                if s < KD:
                    return ring[:, s, :], gate_up[s * P:(s + 1) * P, :]
                j = 2 * (s - KD)
                return (ring[:, s, :].rearrange("p (j n) -> p j n", j=2),
                        down.rearrange("(j p) n -> p j n", p=P)[:, j:j + 2, :])

            for s in range(RING):
                if s >= KD:
                    sp.wait_ge(*chunk_used(CHUNKS - 4 + s - KD))
                sp.dma_start(*slot_copy(s, w_gate_up[0, 0], w_down[0, 0])).then_inc(s_slot[s], 16)
            for t in range(TT):
                sp.wait_ge(hf_ready, t + 1)
                sp.dma_start(hf_rows[t * P:(t + 1) * P, :], hf[:, t, :]).then_inc(hf_stored, 16)
            sp.dma_start(hf_rows[T:T + P, :], hf[:, 0, :]).then_inc(hf_stored, 16)
            for t in range(TT):
                sp.wait_ge(bias_added, t + 1)
                sp.dma_start(y_acc[t * P:(t + 1) * P, :], xs[:, t, :]).then_inc(x1_stored, 16)
            sp.dma_start(y_acc[T:T + P, :], xs[:, 0, :]).then_inc(x1_stored, 16)
            sp.wait_ge(meta_loaded, 1)
            items = sp.value_load(meta_i[0:1, 3 * MI:3 * MI + 1], min_val=E, max_val=E + 15)
            with sp.Fori(1, items) as i:
                e = sp.value_load(meta_i[0:1, bass.ds(i, 1)], min_val=0, max_val=E - 1)
                gu = w_gate_up[0, bass.ds(e, 1)].rearrange("e k n -> (e k) n")
                dn = w_down[0, bass.ds(e, 1)].rearrange("e k n -> (e k) n")
                for s in range(RING):
                    if s == KD - 1:
                        sp.wait_ge(gu_done, i * 2)
                    elif s == RING - 1:
                        sp.wait_ge(down_done, i)
                    else:
                        sp.wait_ge(slot_used, (i - 1) * (RING - 2) + s + 1 - (s > KD - 1))
                    sp.dma_start(*slot_copy(s, gu, dn)).then_inc(s_slot[s], 16)
            sp.wait_ge(y_added, items * 16)
            sp.dma_start(out[0], y_acc[0:T, :]).then_inc(out_stored, 16)
            sp.wait_ge(out_stored, 16)

        @block.gpsimd
        def _(pool):
            step = Steps(pool, pool_step)
            pool.sem_inc(rows_free, 1)
            pool.sem_inc(merged, 1)
            step(pool.memset(ident[:, :], 0.0))
            pool.affine_select(out=ident[:, :], in_=ident[:, :], compare_op=ALU.not_equal, fill=1.0, base=0,
                               pattern=[[-1, P]], channel_multiplier=1).then_inc(consts, 1)
            step(pool.memset(ones[:, :], 1.0))
            pool.affine_select(out=upper[:, :], in_=ones[:, :], compare_op=ALU.is_gt, fill=0.0, base=0,
                               pattern=[[1, P]], channel_multiplier=-1)
            for c in range(HALF):
                ins = pool.memset(inv_f[:, c:c + 1], float(np.float32(10000.0) ** (-np.float32(c) / np.float32(HALF))))
            ins.then_inc(consts, 1)
            pool.wait_ge(s_small, 16 * SMALL)
            pool.affine_select(out=wsp_raw, in_=wsp_raw, compare_op=ALU.is_ge, fill=0.0, base=0,
                               pattern=[[0, SG], [-1, P]], channel_multiplier=1).then_inc(consts, 1)
            step(pool.memset(band[:, :], 0.0))
            step(pool.affine_select(out=band[:, :], in_=band[:, :], compare_op=ALU.is_ge, fill=NEG, base=P,
                                    pattern=[[-1, 2 * P]], channel_multiplier=1))
            step(pool.affine_select(out=band[:, :], in_=band[:, :], compare_op=ALU.is_ge, fill=NEG, base=0,
                                    pattern=[[1, 2 * P]], channel_multiplier=-1))
            pool.iota(dist, pattern=[[-1, P]], base=T, channel_multiplier=1)
            pool.iota(iota_e[:, :], pattern=[[1, E]], base=0, channel_multiplier=0,
                      allow_small_or_imprecise_dtypes=True)
            pool.iota(pcol[:, 0:1], pattern=[[1, 1]], base=0, channel_multiplier=1,
                      allow_small_or_imprecise_dtypes=True)
            step(pool.memset(pcol[:, 2:3], 1.0))
            pool.affine_select(out=pcol[:, 2:3], in_=pcol[:, 2:3], compare_op=ALU.is_ge, fill=0.0, base=-HW,
                               pattern=[[0, 1]], channel_multiplier=1)
            pool.iota(pcol[:, 1:2], pattern=[[1, 1]], base=T + 1, channel_multiplier=1,
                      allow_small_or_imprecise_dtypes=True).then_inc(consts, 1)
            step(pool.memset(pick[:, :, :], 1.0))
            pool.affine_select(out=pick[:, :, :].rearrange("p i (a d) -> p i a d", a=2),
                               in_=pick[:, :, :].rearrange("p i (a d) -> p i a d", a=2),
                               compare_op=ALU.is_equal, fill=0.0, base=0,
                               pattern=[[-1, 2], [-2, 2], [0, HD]], channel_multiplier=1).then_inc(consts, 1)
            for kind in range(2):
                for t in range(TT):
                    pool.wait_ge(scaled, kind * TT + t + 1)
                    v = qk[:, kind, t, :].rearrange("p (h d) -> p h d", d=HD)
                    pool.tensor_tensor(v, v, qkg[:, kind, :].unsqueeze(1).to_broadcast([P, HEADS, HD]),
                                       ALU.mult).then_inc(gained, 1)
            for t in range(TT):
                pool.wait_ge(ln_scaled, t + 1)
                step(pool.tensor_tensor(ztok[:, t, :], ztok[:, t, :], lnb[:, 0, :], ALU.mult))
                pool.tensor_tensor(ztok[:, t, :], ztok[:, t, :], lnb[:, 1, :], ALU.add).then_inc(ln_done, 1)
            with pool.Fori(0, PAIRS) as i:
                for jj in range(2):
                    pool.wait_ge(part_b, 2 * i + jj + 1)
                    m = mergedT[:, bass.ds(2 * i + jj, 1), :].rearrange("p a t -> p (a t)")
                    pool.tensor_tensor(m, m, pt[:, jj * T:jj * T + T], ALU.add).then_inc(merged, 1)
            pool.wait_ge(out_done, 1)
            pool.iota(slots_iota, pattern=[[1, T]], base=0, channel_multiplier=0,
                      allow_small_or_imprecise_dtypes=True)
            pool.iota(slots_twice, pattern=[[0, 2], [1, HW]], base=0, channel_multiplier=0,
                      allow_small_or_imprecise_dtypes=True)
            pool.iota(aux[:, :, :, 0], pattern=[[P, TT], [0, E]], base=1, channel_multiplier=1,
                      allow_small_or_imprecise_dtypes=True).then_inc(consts2, 1)
            for t in range(TT):
                pool.wait_ge(bsum_read, t + 1)
                pool.tensor_tensor(xs[:, t, :], xs[:, t, :], bsum[:, t, :], ALU.add).then_inc(bias_added, 1)
            pool.wait_ge(meta_loaded, 1)
            items = pool.value_load(meta_i[0:1, 3 * MI:3 * MI + 1], min_val=E, max_val=E + 15)

            def gather(cls):
                rows = slice(0, WIDTHS[cls])
                pool.indirect_dma_start(xg_tok[rows, :], None, hf_rows,
                                        bass.IndirectOffsetOnAxis(ap=idx_next[rows, 0:1], axis=0)
                                        ).then_inc(x_gathered, 16)

            cls0 = pool.value_load(meta_i[0:1, 2 * MI:2 * MI + 1], min_val=0, max_val=2)
            pool.wait_ge(hf_stored, 16 * (TT + 1))
            pool.wait_ge(next_rows, 1)
            pool.sem_inc(gather_turn, 1)
            by_class(pool, cls0, gather)
            with pool.Fori(0, items) as i:
                cls1 = pool.value_load(meta_i[0:1, bass.ds(i + 1 + 2 * MI, 1)], min_val=0, max_val=2)
                pool.wait_ge(next_rows, i + 2)
                pool.wait_ge(xg_t, 2 * i + 2)
                pool.sem_inc(gather_turn, 1)
                by_class(pool, cls1, gather)
                pool.wait_ge(yrow_ready, i + 2)
                pool.wait_ge(x1_stored, 16 * (TT + 1))
                pool.sem_inc(add_turn, 1)
                cls = pool.value_load(meta_i[0:1, bass.ds(i + 2 * MI, 1)], min_val=0, max_val=2)
                with pool.If(cls < 1):
                    pool.indirect_dma_start(y_halves, bass.IndirectOffsetOnAxis(ap=idx[:, 0:1], axis=0),
                                            yrow[:, 0:BW], None, compute_op=ALU.add).then_inc(y_added, 16)
                with pool.Else():
                    pool.indirect_dma_start(y_acc, bass.IndirectOffsetOnAxis(ap=idx[:, 0:1], axis=0), yrow, None,
                                            compute_op=ALU.add).then_inc(y_added, 16)
                pool.wait_ge(y_added, i * 16 + 16)
                pool.sem_inc(rows_free, 1)

        @block.scalar
        def _(ae):
            ae.sem_inc(yrow_ready, 1)
            for dst, src in smalls:
                ae.dma_start(dst, src, allow_slow_non_contiguous=True).then_inc(s_small, 16)
            ae.wait_ge(s_x, 16 * TT)
            for t in range(TT):
                ae.activation(work[:, o_h + t * D:o_h + (t + 1) * D], xs[:, t, :], ACT.Square,
                              accum_out=ss[:, t:t + 1]).then_inc(rms_sum, 1)
            ae.wait_ge(rms_var, 1)
            ae.activation(rs[:, :], rs[:, :], ACT.Sqrt).then_inc(rms_root, 1)
            ae.wait_ge(trig_ready, 1)
            ae.activation(sin_t[:, :, :], trig[:, 2], ACT.Sin).then_inc(trig_done, 1)
            ae.activation(cos_t[:, :, :], trig[:, 3], ACT.Sin).then_inc(trig_done, 1)
            for b in range(SETUP):
                ae.wait_ge(setup_t, b + 1)
                src = bank[:, 4 + b % 4, :]
                if b < SG // 4:
                    ins = ae.copy(wspT[:, 4 * b:4 * b + 4, :], src.rearrange("p (g t) -> p g t", g=4))
                elif b == SG // 4:
                    ins = ae.copy(bsp[:, :], src[:, 0:SG])
                else:
                    j = 4 * (b - SG // 4 - 1)
                    ins = ae.copy(biases[:, j:j + 4, :], src[:, 0:4 * E].rearrange("p (j e) -> p j e", j=4))
                ins.then_inc(setup_e, 1)
            ae.sem_inc(proj_read, 2)

            for kind in range(3):
                for g in range(GROUPS):
                    for t in range(TT):
                        n = kind * 12 + g * TT + t
                        ae.wait_ge(proj_done, n + 1)
                        dst = (qk[:, kind] if kind < 2 else vtok)[:, t, g * GW:(g + 1) * GW]
                        ae.copy(dst, bank[:, n % 2, 0:CW]).then_inc(proj_read, 1)
                if kind < 2:
                    ae.wait_ge(proj_read, 2 + 12 * (kind + 1))
                    for t in range(TT):
                        m = kind * TT + t
                        if m >= 2:
                            ae.wait_ge(sq_read, m - 1)
                        ae.activation(sc[:, m % 2, 0:AW], qk[:, kind, t, :], ACT.Square).then_inc(sq_done, 1)
                    ae.wait_ge(hvar, kind + 1)
                    ae.activation(hss[:, kind], hss[:, kind], ACT.Sqrt).then_inc(hroot, 1)

            def exps(u):
                ae.wait_ge(max_done, u + 1)
                p = heads(sc[:, u % 2, :], unit_width(u))
                for h in range(HPG):
                    ins = ae.activation(p[:, h, :], p[:, h, :], ACT.Exp, bias=nmstat[:, u, h:h + 1], scale=SCALE,
                                        accum_out=lstat[:, u, h:h + 1])
                ins.then_inc(prob_done, 1)

            for s in range(SLOTS):
                if s < 12:
                    ae.wait_ge(pair_t, s + 1)
                    g, r = divmod(s, 4)
                    ae.copy(qkT[:, (r // 2) * KA + 2 * g + r % 2, :], bank[:, 6, :]).then_inc(pair_e, 1)
                if s < 24:
                    ae.wait_ge(proj_done, 36 + s + 1)
                    c, t = divmod(s, TT)
                    dst = ztok if c < 3 else utok
                    ae.copy(dst[:, t, (c % 3) * CW:(c % 3 + 1) * CW], bank[:, s % 2, 0:CW]).then_inc(proj_read, 1)
                if s % 2 == 1 and 5 <= s < 29:
                    exps((s - 5) // 2)
                if s == 12 or s == 24:
                    half, ready = (ztok, ztok_ready) if s == 12 else (utok, utok_ready)
                    ae.wait_ge(proj_read, 2 + 36 + s)
                    for t in range(TT):
                        ae.activation(half[:, t, :], half[:, t, :], ACT.Gelu).then_inc(ready, 1)
                if s == 16:
                    ae.wait_ge(ln_var, TT)
                    ae.activation(mv[:, :, 1], mv[:, :, 1], ACT.Sqrt).then_inc(ln_root, 1)
            for a in range(2):
                for g in range(GROUPS):
                    ae.wait_ge(ml_t, 3 * a + g + 1)
                    src, dst = bank[0:HPG, 2 + 3 * a + g, :], mlrow[:, a, g, :]
                    if g > 0:
                        dst = dst.rearrange("p (m s) -> p s m", s=4)
                        src = src.rearrange("p (s m) -> p s m", s=4)
                    ae.copy(dst, src).then_inc(ml_e, 1)
            ae.wait_ge(gexp_in, 1)
            ae.activation(wrow, wrow, ACT.Exp, scale=SCALE).then_inc(gexp, 1)
            for k in range(KA):
                ae.wait_ge(sgu_t, k + 1)
                ae.copy(sguT[:, k, :], bank[:, 2 + k, :]).then_inc(sgu_e, 1)
            ae.sem_inc(gate_read, 4)
            with ae.Fori(0, PAIRS) as i:
                for ab in range(2):
                    for jj in range(2):
                        n = 4 * i + 2 * ab + jj
                        ae.wait_ge(gate_done, n + 1)
                        ae.wait_ge(y_read, n + 1)
                        ae.activation(sc[:, ab, jj * T:jj * T + T], bank[:, 4 * jj + ab, :],
                                      ACT.Sigmoid).then_inc(gate_read, 1)
            for t in range(TT):
                ae.wait_ge(out_read, 4 * (PAIRS - 1) + t + 1)
                ae.activation(work[:, o_h + t * D:o_h + (t + 1) * D], xs[:, t, :], ACT.Square,
                              accum_out=ss[:, t:t + 1]).then_inc(rms2_sum, 1)
            ae.wait_ge(rms2_var, 1)
            ae.activation(rs[:, :], rs[:, :], ACT.Sqrt).then_inc(rms2_root, 1)
            for t in range(TT):
                ae.wait_ge(hf_t, t + 1)
                b = 2 * (t % 2)
                ae.copy(hfT[:, :, t * P:(t + 1) * P].rearrange("p (a k) c -> p a k c", a=2),
                        bank[:, b:b + 2, :].rearrange("p a (k c) -> p a k c", k=4)).then_inc(hf_e, 1)
            ae.wait_ge(topd, 1)
            ae.activation(ge, ge, ACT.Exp).then_inc(topexp, 1)
            ae.wait_ge(gatesT_t, 1)
            ae.copy(gatesT, bank[0:E, 7, :]).then_inc(gatesT_e, 1)
            for t in range(TT):
                ae.wait_ge(bsum_done, t + 1)
                b = 2 * (t % 2)
                ae.copy(bsum[:, t, :], bank[:, b:b + 2, :].rearrange("p a n -> p (a n)")).then_inc(bsum_read, 1)

            def read_xg(half, n):
                ae.wait_ge(xg_t, n)
                ae.copy(xgT[:, 4 * half:4 * half + 4, :],
                        bank[:, 6 + half, :].rearrange("p (k c) -> p k c", k=4)).then_inc(xg_e, 1)

            ae.wait_ge(meta_loaded, 1)
            items = ae.value_load(meta_i[0:1, 3 * MI:3 * MI + 1], min_val=E, max_val=E + 15)
            read_xg(0, 1)
            read_xg(1, 2)
            with ae.Fori(0, items) as i:
                cls = ae.value_load(meta_i[0:1, bass.ds(i + 2 * MI, 1)], min_val=0, max_val=2)

                def gates_part(N):
                    for h in range(2):
                        ae.wait_ge(gu_done, 2 * i + h + 1)
                        ae.copy(gu_tok[:, h, :], bank[:, h, :]).then_inc(gu_out_a, 1)
                        ae.wait_ge(gated, 2 * i + h + 1)
                        ae.activation(sg[:, 4 * h:4 * h + 4, 0:N], gate[:, 4 * h:4 * h + 4, 0:N], ACT.Sigmoid,
                                      scale=ALPHA).then_inc(sig_done, 1)

                by_class(ae, cls, lambda c: gates_part(WIDTHS[c]))
                for h in range(2):
                    read_xg(h, 2 * i + h + 3)

                def scale_rows(dst, src):
                    ae.wait_ge(down_done, i + 1)
                    ae.wait_ge(now_ready, i + 1)
                    ae.wait_ge(rows_free, i + 1)
                    ae.activation(dst, src, ACT.Copy, scale=slot_now[:, 1:2]).then_inc(yrow_ready, 1)

                with ae.If(cls < 1):
                    scale_rows(yrow[:, 0:BW], bank[:, 4, :])
                with ae.Else():
                    scale_rows(yrow, bank[:, 4:6, :].rearrange("p a n -> p (a n)"))

        @block.vector
        def _(ve):
            step = Steps(ve, dve_step)
            for b in range(8):
                ins = ve.memset(bank[:, b, :], 0.0)
            ins.then_inc(psum_clear, 1)
            ve.wait_ge(consts, 4)
            step(ve.tensor_scalar(dist, dist, 3, None, ALU.bitwise_and))
            step(ve.scalar_tensor_tensor(out=diag[:, :], in0=dist, scalar=NEG, in1=band[:, P:2 * P],
                                         op0=ALU.mult, op1=ALU.add))
            ve.wait_ge(rms_sum, TT)
            ve.tensor_scalar(rs[:, :], ss[:, :], 1.0 / D, EPS, ALU.mult, ALU.add).then_inc(rms_var, 1)
            ve.wait_ge(rms_root, 1)
            step(ve.reciprocal(rs[:, :], rs[:, :]))
            for t in range(TT):
                ve.tensor_scalar(xr[:, t, :], xs[:, t, :], rs[:, t:t + 1], None, ALU.mult).then_inc(xr_ready, 1)
            ve.wait_ge(consts, 2)
            ve.wait_ge(s_small, 16 * SMALL)
            step(ve.tensor_copy(pos_f[:, :], pos_i[:, :]))
            ang, n_t = trig[:, 0], trig[:, 1]
            step(ve.tensor_tensor(ang, pos_f[:, :].unsqueeze(2).to_broadcast([P, 8, HALF]),
                                  inv_f[:, :].unsqueeze(1).to_broadcast([P, 8, HALF]), ALU.mult))
            for which, dst in ((0, trig[:, 2]), (1, trig[:, 3])):
                step(ve.tensor_scalar(n_t, ang, 0.5 / np.pi, 0.25 * which, ALU.mult, ALU.add))
                step(ve.tensor_scalar(n_t, n_t, ROUND, None, ALU.add))
                step(ve.tensor_scalar(n_t, n_t, -ROUND, None, ALU.add))
                src = ang
                for part in TWO_PI:
                    step(ve.scalar_tensor_tensor(out=dst, in0=n_t, scalar=-part, in1=src, op0=ALU.mult, op1=ALU.add))
                    src = dst
                step(ve.tensor_scalar(dst, dst, 0.5 * float(np.pi) * which, PI_IN, ALU.add, ALU.min))
                step(ve.tensor_scalar(dst, dst, -PI_IN, None, ALU.max))
            ve.sem_inc(trig_ready, 1)
            for k in range(KD):
                ve.wait_ge(hT_t, k + 1)
                ve.tensor_scalar(hT[:, k, :], bank[:, k % 4, :], g1[:, k:k + 1], None, ALU.mult).then_inc(hT_e, 1)
            ve.wait_ge(trig_done, 2)
            for kind in range(2):
                def q4(t):
                    return qk[:, kind, t, :].rearrange("p (h d) -> p h d", d=HD)
                for t in range(TT):
                    m = kind * TT + t
                    ve.wait_ge(sq_done, m + 1)
                    ins = ve.tensor_reduce(hss[:, kind, t, :],
                                           sc[:, m % 2, 0:AW].rearrange("p (h d) -> p h d", d=HD), AX_X, ALU.add)
                    ins.then_inc(sq_read, 1)
                ve.wait_ge(sq_read, TT * (kind + 1))
                ve.tensor_scalar(hss[:, kind], hss[:, kind], 1.0 / HD, EPS, ALU.mult, ALU.add).then_inc(hvar, 1)
                ve.wait_ge(hroot, kind + 1)
                step(ve.reciprocal(hss[:, kind], hss[:, kind]))
                for t in range(TT):
                    ve.tensor_tensor(q4(t), q4(t), hss[:, kind, t, :].unsqueeze(2).to_broadcast([P, HEADS, HD]),
                                     ALU.mult).then_inc(scaled, 1)
                for t in range(TT):
                    ve.wait_ge(gained, kind * TT + t + 1)
                    prod = pt[:, 0:AW].rearrange("p (a h d) -> p a h d", a=2, d=HALF)
                    a, b = q4(t)[:, :, 0:HALF], q4(t)[:, :, HALF:HD]
                    for order, hs in ((0, slice(0, HPG)), (1, slice(HPG, HEADS))):
                        n = hs.stop - hs.start
                        cs = cos_t[:, order * TT + t, :].unsqueeze(1).to_broadcast([P, n, HALF])
                        sn = sin_t[:, order * TT + t, :].unsqueeze(1).to_broadcast([P, n, HALF])
                        ve.tensor_tensor(prod[:, 0, hs, :], b[:, hs, :], sn, ALU.mult)
                        step(ve.tensor_tensor(prod[:, 1, hs, :], a[:, hs, :], sn, ALU.mult))
                        ve.tensor_tensor(a[:, hs, :], a[:, hs, :], cs, ALU.mult)
                        step(ve.tensor_tensor(b[:, hs, :], b[:, hs, :], cs, ALU.mult))
                    ve.tensor_tensor(a, a, prod[:, 0], ALU.subtract)
                    step(ve.tensor_tensor(b, b, prod[:, 1], ALU.add))
                    ve.sem_inc(roped, 1)

            def mask_max(u):
                W = unit_width(u)
                ve.wait_ge(score_done, u + 1)
                if u >= 2:
                    ve.wait_ge(pt_t, u - 1)
                s_u = sc[:, u % 2, 0:HPG * W].rearrange("p (a i w) -> p a i w", a=2, i=2)
                step(ve.tensor_tensor(s_u, bank[:, 2:4, 0:2 * W].rearrange("p a (i w) -> p a i w", i=2),
                                      unit_mask(u).unsqueeze(1).unsqueeze(1).to_broadcast([P, 2, 2, W]), ALU.add))
                step(ve.tensor_reduce(mstat[:, u, :], heads(sc[:, u % 2, :], W), AX_X, ALU.max))
                ve.tensor_scalar(nmstat[:, u, :], mstat[:, u, :], -SCALE, None, ALU.mult).then_inc(max_done, 1)

            def read_pt(u):
                ve.wait_ge(pt_t, u + 1)
                ve.wait_ge(o_done, u)
                n = HPG * unit_width(u)
                ve.tensor_copy(pt[:, 0:n], bank[:, 4:6, :].rearrange("p a n -> p (a n)")[:, 0:n]).then_inc(pt_e, 1)

            def read_o(u):
                g, j = divmod(u, 4)
                ve.wait_ge(o_done, u + 1)
                for i in range(2):
                    ins = ve.tensor_copy(order_cols(attnT[:, 2 * g + i, :], g, j), bank[:, 7, i * P:(i + 1) * P])
                ins.then_inc(o_read, 1)

            for s in range(SLOTS):
                if s % 2 == 1 and 5 <= s < 29:
                    mask_max((s - 5) // 2)
                if s % 2 == 1 and 7 <= s < 31:
                    read_pt((s - 7) // 2)
                if s % 2 == 0 and 8 <= s < 31:
                    read_o((s - 8) // 2)
                if s == 14:
                    for t in range(TT):
                        ve.wait_ge(ztok_ready, t + 1)
                        ve.bn_stats(bn[:, t, 0, :], ztok[:, t, 0:SW // 2])
                        step(ve.bn_stats(bn[:, t, 1, :], ztok[:, t, SW // 2:SW]))
                        step(ve.bn_aggr(mv[:, t, :], bn[:, t, :, :]))
                        ve.tensor_scalar(mv[:, t, 1:2], mv[:, t, 1:2], EPS, None, ALU.add).then_inc(ln_var, 1)
                if s == 18:
                    ve.wait_ge(ln_root, 1)
                    step(ve.reciprocal(mv[:, :, 1], mv[:, :, 1]))
                    for t in range(TT):
                        ve.tensor_scalar(ztok[:, t, :], ztok[:, t, :], mv[:, t, 0:1], mv[:, t, 1:2],
                                         ALU.subtract, ALU.mult).then_inc(ln_scaled, 1)
            ve.wait_ge(utok_ready, TT)
            for g in range(SG):
                ve.wait_ge(mix_done, g + 1)
                u_g = utok[:, :, g * HD:(g + 1) * HD]
                ve.scalar_tensor_tensor(out=u_g, in0=bank[:, g % 2, 0:TT * HD].rearrange("p (t d) -> p t d", t=TT),
                                        scalar=bsp[:, g:g + 1], in1=u_g, op0=ALU.add, op1=ALU.mult).then_inc(mix_read, 1)
            ve.wait_ge(ml_e, 6)
            mr, lr = mlrow[:, 0], mlrow[:, 1]
            step(ve.tensor_tensor(mrow, mr[:, 0, :], mr[:, 1, :], ALU.max))
            step(ve.tensor_tensor(mrow, mrow, mr[:, 2, :], ALU.max))
            ve.tensor_tensor(wrow, mr, mrow.unsqueeze(1).to_broadcast([HPG, GROUPS, T]), ALU.subtract).then_inc(gexp_in, 1)
            ve.wait_ge(gexp, 1)
            step(ve.tensor_tensor(lr, lr, wrow, ALU.mult))
            step(ve.tensor_tensor(drow, lr[:, 0, :], lr[:, 1, :], ALU.add))
            step(ve.tensor_tensor(drow, drow, lr[:, 2, :], ALU.add))
            step(ve.reciprocal(drow, drow))
            ve.tensor_tensor(wrow, wrow, drow.unsqueeze(1).to_broadcast([HPG, GROUPS, T]), ALU.mult).then_inc(wrow_ready, 1)
            for k in range(KA):
                ve.wait_ge(spread_done, k + 1)
                ve.tensor_tensor(attnT[:, k, :], attnT[:, k, :], bank[:, 2 + k, :], ALU.mult).then_inc(spread_read, 1)
            ve.sem_inc(y_read, 4)
            with ve.Fori(0, PAIRS) as i:
                for ab in range(2):
                    for jj in range(2):
                        n = 4 * i + 2 * ab + jj
                        ve.wait_ge(y_done, n + 1)
                        ve.wait_ge(gate_read, n + 1 + 4)
                        if ab == 0:
                            dst = mergedT[:, bass.ds(2 * i + jj, 1), :].rearrange("p a t -> p (a t)")
                        else:
                            dst = pt[:, jj * T:jj * T + T]
                            ve.wait_ge(merged, 2 * i + 1)
                        step_ins = ve.tensor_tensor(dst, bank[:, 4 * jj + 2 + ab, :], sc[:, ab, jj * T:jj * T + T],
                                                    ALU.mult)
                        step_ins.then_inc(y_read, 1)
                        if ab == 1:
                            ve.wait_ge(y_read, n + 1 + 4)
                            ve.sem_inc(part_b, 1)
            for c in range(PAIRS):
                for t in range(TT):
                    n = c * TT + t
                    ve.wait_ge(out_done, n + 1)
                    v = xs[:, t, c * CW:(c + 1) * CW]
                    ve.tensor_tensor(v, v, bank[:, n % 2, 0:CW], ALU.add).then_inc(out_read, 1)
            ve.wait_ge(rms2_sum, TT)
            ve.tensor_scalar(rs[:, :], ss[:, :], 1.0 / D, EPS, ALU.mult, ALU.add).then_inc(rms2_var, 1)
            ve.wait_ge(rms2_root, 1)
            step(ve.reciprocal(rs[:, :], rs[:, :]))
            ve.wait_ge(s_g2, 32)
            for t in range(TT):
                ve.scalar_tensor_tensor(out=hf[:, t, :], in0=xs[:, t, :], scalar=rs[:, t:t + 1], in1=g2b,
                                        op0=ALU.mult, op1=ALU.mult).then_inc(hf_ready, 1)
            ve.wait_ge(logit_done, 1)
            step(ve.tensor_tensor(lg, bank[:, 4, 0:TT * E].rearrange("p (t e) -> p t e", t=TT),
                                  brb[:, :].unsqueeze(1).to_broadcast([P, TT, E]), ALU.add))
            for t in range(TT):
                ins = ve.max(out=top[:, t, :], in_=lg[:, t, :])
            step(ins)
            for t in range(TT):
                ins = ve.max_index(out=topi[:, t, :], in_max=top[:, t, :], in_values=lg[:, t, :])
            ve.tensor_tensor(ge, top[:, :, 0:TOPK], top[:, :, 0:1].to_broadcast([P, TT, TOPK]),
                             ALU.subtract).then_inc(topd, 1)
            step(ins)
            step(ve.tensor_copy(topf, topi[:, :, 0:TOPK]))
            step(ve.tensor_tensor(hot, iota_e[:, :].unsqueeze(1).unsqueeze(1).to_broadcast([P, TT, TOPK, E]),
                                  topf.unsqueeze(3).to_broadcast([P, TT, TOPK, E]), ALU.is_equal))
            ve.tensor_reduce(chosen, hot.rearrange("p t k e -> p t e k"), AX_X, ALU.add).then_inc(chosen_ready, 1)
            ve.wait_ge(topexp, 1)
            step(ve.tensor_reduce(gsum, ge, AX_X, ALU.add))
            step(ve.reciprocal(gsum, gsum))
            step(ve.tensor_tensor(ge, ge, gsum.unsqueeze(2).to_broadcast([P, TT, TOPK]), ALU.mult))
            step(ve.tensor_tensor(hotg, hot, ge.unsqueeze(3).to_broadcast([P, TT, TOPK, E]), ALU.mult))
            ve.wait_ge(consts2, 1)
            ve.tensor_reduce(gates, hotg.rearrange("p t k e -> p t e k"), AX_X, ALU.add).then_inc(gates_ready, 1)
            ve.wait_ge(gates_ready, 1)
            step(ve.tensor_copy(aux[:, :, :, 1], gates))
            ve.wait_ge(place_done, 1)
            places = bank[:, 5, 0:TT * E].rearrange("p (t e) -> p t e", t=TT)
            step(ve.scalar_tensor_tensor(out=posm, in0=places, scalar=1.0, in1=chosen, op0=ALU.add, op1=ALU.mult))
            ve.tensor_scalar(posm, posm, -1.0, None, ALU.add)
            step(ve.tensor_copy(cnt, bank[:, 5, TT * E:TT * E + E]))
            step(ve.tensor_scalar(nblk, cnt, float(P), 1.0, ALU.is_gt, ALU.add))
            for b in (2, 3):
                step(ve.scalar_tensor_tensor(out=nblk, in0=cnt, scalar=float(b * P), in1=nblk, op0=ALU.is_gt, op1=ALU.add))
            step(ve.memset(scan, 0.0))
            step(ve.tensor_copy(scan[:, 0, 16:16 + E], nblk))
            for b in range(5):
                w = 1 << b
                step(ve.tensor_tensor(scan[:, (b + 1) % 2, 16:16 + E], scan[:, b % 2, 16:16 + E],
                                      scan[:, b % 2, 16 - w:16 + E - w], ALU.add))
            ends = scan[:, 1, 16:16 + E]
            step(ve.tensor_scalar(cmpe, ends, pcol[:, 0:1], None, ALU.is_le))
            step(ve.tensor_reduce(tiny[:, 0:1], cmpe, AX_X, ALU.add))
            step(ve.tensor_tensor(cmpn, cmpe, nblk, ALU.mult))
            step(ve.tensor_reduce(tiny[:, 1:2], cmpn, AX_X, ALU.add))
            step(ve.tensor_scalar(meta[:, 0:1], tiny[:, 0:1], float(E - 1), None, ALU.min))
            step(ve.tensor_tensor(meta[:, 1:2], pcol[:, 0:1], tiny[:, 1:2], ALU.subtract))
            step(ve.scalar_tensor_tensor(out=cmpn, in0=iota_e[:, :], scalar=meta[:, 0:1], in1=cnt,
                                         op0=ALU.is_equal, op1=ALU.mult))
            step(ve.tensor_reduce(tiny[:, 2:3], cmpn, AX_X, ALU.add))
            step(ve.scalar_tensor_tensor(out=tiny[:, 3:4], in0=meta[:, 1:2], scalar=-float(P), in1=tiny[:, 2:3],
                                         op0=ALU.mult, op1=ALU.add))
            step(ve.tensor_scalar(tiny[:, 5:6], meta[:, 1:2], 0.0, None, ALU.is_gt))
            step(ve.scalar_tensor_tensor(out=tiny[:, 4:5], in0=tiny[:, 3:4], scalar=float(WIDTHS[0]), in1=tiny[:, 5:6],
                                         op0=ALU.is_gt, op1=ALU.max))
            step(ve.scalar_tensor_tensor(out=meta[:, 2:3], in0=tiny[:, 3:4], scalar=float(WIDTHS[1]), in1=tiny[:, 4:5],
                                         op0=ALU.is_gt, op1=ALU.add))
            step(ve.tensor_scalar(tiny[:, 6:7], tiny[:, 4:5], -float(T), float(T), ALU.mult, ALU.add))
            step(ve.scalar_tensor_tensor(out=meta[:, 1:2], in0=meta[:, 1:2], scalar=float(P), in1=tiny[:, 6:7],
                                         op0=ALU.mult, op1=ALU.add))
            ve.tensor_copy(meta[:, 3:4], ends[:, E - 1:E]).then_inc(meta_ready, 1)
            ve.wait_ge(metarow_done, 1)
            ve.tensor_copy(meta_i, bank[0:1, 6, 0:4 * MI]).then_inc(meta_loaded, 1)
            ve.wait_ge(meta_loaded, 1)
            items = ve.value_load(meta_i[0:1, 3 * MI:3 * MI + 1], min_val=E, max_val=E + 15)

            def select(e, at):
                ve.tensor_copy(aux_now, aux[:, :, bass.ds(e, 1), :].rearrange("p t e a -> p t (e a)"))
                step_v(ve.tensor_copy(rel, posm[:, :, bass.ds(e, 1)].rearrange("p t e -> p (t e)")))
                for t in range(TT):
                    ins = ve.tensor_scalar(sel[:, t, :], pt[:, bass.ds(at, P)], rel[:, t:t + 1], None,
                                           ALU.is_equal)
                ins.then_inc(sel_ready, 1)

            step_v = Steps(ve, dve_moe)
            at0 = ve.value_load(meta_i[0:1, MI:MI + 1], min_val=0, max_val=T)
            select(0, at0)
            def place_rows(n, step_v):
                ve.wait_ge(slot_idx, n + 1)
                ve.tensor_copy(slot_next, bank[:, 7, 0:2]).then_inc(slot_idx_read, 1)
                ve.wait_ge(slot_idx_read, n + 1)
                step_v(ve.tensor_scalar(slot_pad, slot_next[:, 0:1], 0.0, pcol[:, 1:2], ALU.is_equal, ALU.mult))
                step_v(ve.scalar_tensor_tensor(out=row_next, in0=slot_next[:, 0:1], scalar=-1.0, in1=slot_pad,
                                               op0=ALU.add, op1=ALU.add))

            MOE_STEPS = 13
            place_rows(0, step_v)
            ve.tensor_copy(idx_next[:, :], row_next).then_inc(next_rows, 1)
            ve.wait_ge(bias_added, TT)
            with ve.Fori(0, items) as i:
                step_v = Steps(ve, dve_moe, i * MOE_STEPS + 3)
                e = ve.value_load(meta_i[0:1, bass.ds(i, 1)], min_val=0, max_val=E - 1)
                cls = ve.value_load(meta_i[0:1, bass.ds(i + 2 * MI, 1)], min_val=0, max_val=2)
                step_v(ve.tensor_copy(bias_now, biases[:, :, bass.ds(e, 1)].rearrange("p j e -> p (j e)")))
                e1 = ve.value_load(meta_i[0:1, bass.ds(i + 1, 1)], min_val=0, max_val=E - 1)
                at1 = ve.value_load(meta_i[0:1, bass.ds(i + 1 + MI, 1)], min_val=0, max_val=T)
                ve.wait_ge(slot_idx, i + 1)
                select(e1, at1)
                ve.wait_ge(rows_free, i + 1)
                ve.wait_ge(yrow_ready, i + 1)
                step_v(ve.tensor_copy(slot_now, slot_next))
                ve.tensor_copy(row_f, row_next).then_inc(row_ready, 1)
                ve.wait_ge(row_ready, i + 1)
                place_rows(i + 1, step_v)
                ve.wait_ge(x_gathered, 16 * i + 16)
                ve.tensor_copy(idx_next[:, :], row_next).then_inc(next_rows, 1)

                def add_bias(dst, b, cls, bias):
                    src = bank[:, b, :].rearrange("p (k c) -> p k c", k=4)
                    if cls == 0:
                        b, src = 3, bank[:, 2 + b % 2, :].rearrange("p (k a c) -> p k a c", k=4, a=2)[:, :, b // 2, :]
                    if cls != 1 or b == 3:
                        n = WIDTHS[cls]
                        return ve.tensor_tensor(dst, src[:, :, 0:n], bias.unsqueeze(2).to_broadcast([P, 4, n]), ALU.add)
                    ve.tensor_tensor(dst[:, :, QW * b:QW * (b + 1)], src[:, :, 3 * QW:4 * QW],
                                     bias.unsqueeze(2).to_broadcast([P, 4, QW]), ALU.add)
                    if b == 1:
                        rest = slice(0, 3, 2)
                        split = "p k (c w) -> p k c w"
                        return ve.tensor_tensor(dst.rearrange(split, w=QW)[:, :, rest, :],
                                                src.rearrange(split, w=QW)[:, :, rest, :],
                                                bias.unsqueeze(2).unsqueeze(3).to_broadcast([P, 4, 2, QW]), ALU.add)
                    rest = slice(QW, 3 * QW) if b == 0 else slice(0, 2 * QW)
                    return ve.tensor_tensor(dst[:, :, rest], src[:, :, rest],
                                            bias.unsqueeze(2).to_broadcast([P, 4, 2 * QW]), ALU.add)

                def swiglu(h, cls):
                    lo, hi = 4 * h, 4 * h + 4
                    g_h, u_h, s_h, a_h = (v[:, lo:hi, 0:WIDTHS[cls]] for v in (gate, up, sg, act))
                    ve.wait_ge(gu_t, 2 * i + h + 1)
                    step_v(add_bias(g_h, h, cls, bias_now[:, lo:hi]))
                    ve.tensor_scalar(g_h, g_h, LIMIT, None, ALU.min).then_inc(gated, 1)
                    step_v(add_bias(u_h, 2 + h, cls, bias_now[:, KF + lo:KF + hi]))
                    step_v(ve.tensor_scalar(u_h, u_h, LIMIT, -LIMIT, ALU.min, ALU.max))
                    step_v(ve.scalar_tensor_tensor(out=u_h, in0=u_h, scalar=1.0, in1=g_h, op0=ALU.add, op1=ALU.mult))
                    ve.wait_ge(sig_done, 2 * i + h + 1)
                    ve.tensor_tensor(a_h, u_h, s_h, ALU.mult).then_inc(act_ready, 1)

                n_steps = step_v.n

                def experts_part(cls):
                    step_v.n = n_steps
                    if cls == 0:
                        ve.scalar_tensor_tensor(out=idx[:, :], in0=row_f, scalar=2.0, in1=pcol[:, 2:3],
                                                op0=ALU.mult, op1=ALU.add).then_inc(now_ready, 1)
                        ve.sem_inc(gu_out_b, 2)
                    else:
                        ve.tensor_copy(idx[:, :], row_f).then_inc(now_ready, 1)
                    for h in range(2):
                        if cls > 0:
                            ve.wait_ge(gu_done, 2 * i + h + 1)
                            ve.tensor_copy(gu_tok[:, 2 + h, :], bank[:, 2 + h, :]).then_inc(gu_out_b, 1)
                        swiglu(h, cls)

                by_class(ve, cls, experts_part)
                assert step_v.n == MOE_STEPS, step_v.n

        @block.tensor
        def _(pe):
            pe.wait_ge(psum_clear, 1)
            pe.wait_ge(consts, 3)
            pe.wait_ge(s_small, 16 * SMALL)
            for b in range(SETUP):
                if b >= 4:
                    pe.wait_ge(setup_e, b - 3)
                for a in range(4):
                    dst = bank[:, 4 + b % 4, :]
                    if b < SG // 4:
                        ins = pe.transpose(dst[:, a * P:(a + 1) * P], wsp_raw[:, 4 * b + a, :], ident[:, :])
                    elif b == SG // 4:
                        if a == 0:
                            ins = pe.transpose(dst[:, 0:SG], bsp_raw, ident[0:SG, 0:SG])
                    else:
                        j = 4 * (b - SG // 4 - 1) + a
                        ins = pe.transpose(dst[:, a * E:(a + 1) * E], bias_raw[:, j * P:(j + 1) * P], ident[0:E, 0:E])
                ins.then_inc(setup_t, 1)
            pe.wait_ge(xr_ready, TT)
            for k in range(KD):
                if k >= 4:
                    pe.wait_ge(hT_e, k - 3)
                for t in range(TT):
                    ins = pe.transpose(bank[:, k % 4, t * P:(t + 1) * P], xr[:, t, k * P:(k + 1) * P], ident[:, :])
                ins.then_inc(hT_t, 1)
            pe.wait_ge(hT_e, KD)
            pe.wait_ge(setup_e, SETUP)

            def project(out_bank, group, t, slot):
                w = stream[slot].rearrange("p (k n) -> p k n", k=KD)
                for k in range(KD):
                    ins = pe.matmul(bank[:, out_bank, 0:CW], order_cols(hT[:, k, :], group, t), w[:, k, :],
                                    start=(k == 0), stop=(k == KD - 1))
                return ins

            with pe.Fori(0, 3) as kind:
                for g in range(GROUPS):
                    pe.wait_ge(s_chunk[g], 16 * (kind + 1))
                    for t in range(TT):
                        n = g * TT + t
                        pe.wait_ge(proj_read, 12 * kind + n + 1)
                        project(n % 2, g, t, g).then_inc(proj_done, 1)

            def transpose_pair(s):
                g, r = divmod(s, 4)
                kind, pair = r // 2, 2 * g + r % 2
                pe.wait_ge(roped, TT * (kind + 1))
                if s >= 1:
                    pe.wait_ge(pair_e, s)
                for t in range(TT):
                    ins = pe.transpose(bank[:, 6, t * P:(t + 1) * P], qk[:, kind, t, pair * P:(pair + 1) * P], ident[:, :])
                ins.then_inc(pair_t, 1)

            def scores(u):
                g, j = divmod(u, 4)
                W = unit_width(u)
                k0 = unit_blocks(u)[0] * P
                pe.wait_ge(pair_e, 4 * (g + 1))
                pe.wait_ge(max_done, u)
                for h in range(HPG):
                    par, i = divmod(h, 2)
                    d = slice(par * HD, par * HD + HD)
                    ins = pe.matmul(bank[:, 2 + par, i * W:(i + 1) * W], qkT[d, 2 * g + i, j * P:(j + 1) * P],
                                    qkT[d, KA + 2 * g + i, k0:k0 + W], start=True, stop=True)
                ins.then_inc(score_done, 1)

            def transpose_p(u):
                W = unit_width(u)
                pe.wait_ge(prob_done, u + 1)
                pe.wait_ge(pt_e, u)
                dst = bank[:, 4:6, :].rearrange("p a n -> p (a n)")
                for c in range(HPG * W // P):
                    ins = pe.transpose(dst[:, c * P:(c + 1) * P], sc[:, u % 2, c * P:(c + 1) * P], ident[:, :])
                ins.then_inc(pt_t, 1)

            def weighted(u):
                g, j = divmod(u, 4)
                blocks = unit_blocks(u)
                nb = len(blocks)
                pe.wait_ge(pt_e, u + 1)
                pe.wait_ge(o_read, u)
                for h in range(HPG):
                    par, i = divmod(h, 2)
                    head = g * HPG + 2 * i + par
                    for b, tile in enumerate(blocks):
                        ins = pe.matmul(bank[par * HD:(par + 1) * HD, 7, i * P:(i + 1) * P],
                                        vtok[:, tile, head * HD:(head + 1) * HD],
                                        pt[:, (h * nb + b) * P:(h * nb + b + 1) * P], start=(b == 0), stop=(b == nb - 1))
                ins.then_inc(o_done, 1)

            for s in range(SLOTS):
                if s < 24:
                    c, t = divmod(s, TT)
                    if t == 0:
                        pe.wait_ge(s_chunk[c % 3], 16 * (3 + c // 3 + 1))
                    pe.wait_ge(proj_read, 36 + s + 1)
                    ins = project(s % 2, 0, t, c % 3)
                    ins.then_inc(proj_done, 1)
                if s < 12:
                    transpose_pair(s)
                if s % 2 == 1 and 5 <= s < 29:
                    scores((s - 5) // 2)
                if s % 2 == 1 and 7 <= s < 31:
                    transpose_p((s - 7) // 2)
                if s % 2 == 0 and 8 <= s < 31:
                    weighted((s - 8) // 2)
            pe.wait_ge(o_read, 12)
            for a, stat in enumerate((mstat, lstat)):
                for g in range(GROUPS):
                    for j in range(4):
                        ins = pe.transpose(bank[0:HPG, 2 + 3 * a + g, j * P:(j + 1) * P], stat[:, 4 * g + j, :], ident[:, :])
                    ins.then_inc(ml_t, 1)
            pe.wait_ge(ln_done, TT)
            pe.wait_ge(proj_read, 62)
            for g in range(SG):
                if g >= 2:
                    pe.wait_ge(mix_read, g - 1)
                pe.matmul(bank[:, g % 2, 0:TT * HD].rearrange("p (t d) -> p t d", t=TT), wspT[:, g, :],
                          ztok[:, :, g * HD:(g + 1) * HD], start=True, stop=True).then_inc(mix_done, 1)
            pe.wait_ge(ml_e, 6)
            pe.wait_ge(wrow_ready, 1)
            pe.wait_ge(consts, CONSTS)
            for k in range(KA):
                g, i = divmod(k, 2)
                pe.matmul(bank[:, 2 + k, :], pick[:, i, :], wrow[:, g, :], start=True, stop=True).then_inc(spread_done, 1)
            pe.wait_ge(mix_read, SG)
            for k in range(KA):
                pe.wait_ge(spread_read, k + 1)
                for t in range(TT):
                    ins = pe.transpose(bank[:, 2 + k, t * P:(t + 1) * P], utok[:, t, k * P:(k + 1) * P], ident[:, :])
                ins.then_inc(sgu_t, 1)
            pe.wait_ge(sgu_e, KA)
            with pe.Fori(0, PAIRS) as i:
                for part in range(4):
                    w = stream[part]
                    pe.wait_ge(s_chunk[part], 16 * (i + (6 if part < 3 else 1)))
                    for jj in range(2):
                        free = gate_read if part < 2 else y_read
                        rhs, kt = (hT, KD) if part < 2 else (attnT, KA) if part == 2 else (sguT, KA)
                        pe.wait_ge(free, 4 * i + 2 * (part % 2) + jj + 1)
                        for k in range(kt):
                            ins = pe.matmul(bank[:, 4 * jj + part, :], w[:, k * CW + jj * P:k * CW + (jj + 1) * P],
                                            rhs[:, k, :], start=(k == 0), stop=(k == kt - 1))
                        ins.then_inc(gate_done if part < 2 else y_done, 1)
            pe.wait_ge(merged, 2 * PAIRS + 1)
            pe.wait_ge(gate_read, 4 + 4 * PAIRS)
            for c in range(PAIRS):
                w = stream[c].rearrange("p (k n) -> p k n", k=KD)
                pe.wait_ge(s_chunk[c], 16 * chunk_turn[15 + 4 * PAIRS + c])
                for t in range(TT):
                    n = c * TT + t
                    if n >= 2:
                        pe.wait_ge(out_read, n - 1)
                    for k in range(KD):
                        ins = pe.matmul(bank[:, n % 2, 0:CW], mergedT[:, k, t * P:(t + 1) * P], w[:, k, :],
                                        start=(k == 0), stop=(k == KD - 1))
                    ins.then_inc(out_done, 1)
            pe.wait_ge(out_read, 4 * PAIRS)
            for t in range(TT):
                pe.wait_ge(hf_ready, t + 1)
                if t >= 2:
                    pe.wait_ge(hf_e, t - 1)
                for k in range(KD):
                    ins = pe.transpose(bank[:, 2 * (t % 2) + k // 4, (k % 4) * P:(k % 4 + 1) * P],
                                       hf[:, t, k * P:(k + 1) * P], ident[:, :])
                ins.then_inc(hf_t, 1)
            for t in range(TT):
                pe.wait_ge(hf_e, t + 1)
                for k in range(KD):
                    ins = pe.matmul(bank[:, 4, t * E:(t + 1) * E], hfT[:, k, t * P:(t + 1) * P], wr[:, k, :],
                                    start=(k == 0), stop=(k == KD - 1))
            ins.then_inc(logit_done, 1)
            pe.wait_ge(chosen_ready, 1)
            for t in range(TT):
                for s in range(t + 1):
                    pe.matmul(bank[:, 5, t * E:(t + 1) * E], upper[:, :] if s == t else ones[:, :], chosen[:, s, :],
                              start=(s == 0), stop=(s == t))
            for s in range(TT):
                ins = pe.matmul(bank[:, 5, TT * E:TT * E + E], ones[:, :], chosen[:, s, :],
                                start=(s == 0), stop=(s == TT - 1))
            ins.then_inc(place_done, 1)
            pe.wait_ge(gates_ready, 1)
            pe.wait_ge(s_g2, 32)
            for t in range(TT):
                ins = pe.transpose(bank[0:E, 7, t * P:(t + 1) * P], gates[:, t, :], ident[:, :])
            ins.then_inc(gatesT_t, 1)
            pe.wait_ge(gatesT_e, 1)
            for t in range(TT):
                if t >= 2:
                    pe.wait_ge(bsum_read, t - 1)
                for b in range(2):
                    ins = pe.matmul(bank[:, 2 * (t % 2) + b, :], gatesT[:, t * P:(t + 1) * P], bdn[:, b * BW:(b + 1) * BW],
                                    start=True, stop=True)
                ins.then_inc(bsum_done, 1)
            pe.wait_ge(meta_ready, 1)
            for c in range(4):
                ins = pe.matmul(bank[0:1, 6, c * MI:(c + 1) * MI], meta[:, c:c + 1], ident[:, 0:MI], start=True, stop=True)
            ins.then_inc(metarow_done, 1)
            pe.wait_ge(meta_loaded, 1)
            items = pe.value_load(meta_i[0:1, 3 * MI:3 * MI + 1], min_val=E, max_val=E + 15)

            def transpose_x(cls, half):
                n = WIDTHS[cls]
                for d in range(4 * half, 4 * half + 4):
                    ins = pe.transpose(bank[:, 6 + half, (d % 4) * P:(d % 4) * P + n], xg_tok[0:n, d * P:(d + 1) * P],
                                       ident[0:n, 0:n])
                ins.then_inc(xg_t, 1)

            def slots_of():
                for t in range(TT):
                    ins = pe.matmul(bank[:, 7, 0:2], sel[:, t, :], aux_now[:, t, :], start=(t == 0), stop=(t == TT - 1))
                ins.then_inc(slot_idx, 1)

            cls0 = pe.value_load(meta_i[0:1, 2 * MI:2 * MI + 1], min_val=0, max_val=2)
            pe.wait_ge(sel_ready, 1)

            slots_of()
            pe.wait_ge(slot_idx_read, 1)
            pe.wait_ge(x_gathered, 16)
            by_class(pe, cls0, lambda c: [transpose_x(c, h) for h in range(2)])
            pe.wait_ge(bsum_read, TT)
            with pe.Fori(0, items) as i:
                cls = pe.value_load(meta_i[0:1, bass.ds(i + 2 * MI, 1)], min_val=0, max_val=2)
                cls1 = pe.value_load(meta_i[0:1, bass.ds(i + 1 + 2 * MI, 1)], min_val=0, max_val=2)

                def parts(cls, h):
                    if cls == 0:
                        return [(slice(a * HW, (a + 1) * HW), slice(0, HW), h, 2 * a + h) for a in range(2)]
                    if cls == 2:
                        return [(slice(0, P), slice(0, P), b, b) for b in (h, 2 + h)]
                    out = []
                    for banks in ROUNDS[2 * h:2 * h + 2 - h]:
                        for c, b in enumerate(banks):
                            at = tile_slots(c, b)
                            out.append((slice(c * QW, (c + 1) * QW), slice(at, at + QW), b, b))
                    return out

                def gate_up(cls, k, h):
                    for rows, slots, b, cols in parts(cls, h):
                        ins = pe.matmul(bank[rows, b, :], xgT[:, k, slots], ring[:, k, cols * BW:(cols + 1) * BW],
                                        start=(k == 0), stop=(k == KD - 1))
                    return ins

                def transpose_gu(cls, h):
                    pe.wait_ge(gu_out_a, 2 * i + h + 1)
                    pe.wait_ge(gu_out_b, 2 * i + h + 1)
                    for j in range(4):
                        f = slice(j * P, (j + 1) * P)
                        if cls == 0:
                            ins = pe.transpose(bank[:, 2 + h, f], gu_tok[:, h, f], ident[:, :])
                        else:
                            pe.transpose(bank[:, h, f], gu_tok[:, h, f], ident[:, :])
                            ins = pe.transpose(bank[:, 2 + h, f], gu_tok[:, 2 + h, f], ident[:, :])
                    ins.then_inc(gu_t, 1)

                def down(cls, j):
                    s = KD + j // 2
                    if j % 2 == 0:
                        pe.wait_ge(s_slot[s], 16 * (i + 1))
                    if j % 4 == 0:
                        pe.wait_ge(act_ready, 2 * i + j // 4 + 1)
                    for b in range(2):
                        a_j = act[:, j, 0:WIDTHS[cls]]
                        out_ap = bank[b * HW:(b + 1) * HW, 4, :] if cls == 0 else bank[0:WIDTHS[cls], 4 + b, :]
                        at = (j % 2) * D + b * BW
                        ins = pe.matmul(out_ap, a_j, ring[:, s, at:at + BW], start=(j == 0), stop=(j == KF - 1))
                    if j % 2 == 1 and j < KF - 1:
                        ins.then_inc(slot_used, 1)
                    return ins

                def products(cls):
                    pe.wait_ge(xg_e, 2 * i + 2)
                    for k in range(KD // 2):
                        pe.wait_ge(s_slot[k], 16 * (i + 1))
                        gate_up(cls, k, 0)
                        gate_up(cls, k, 1).then_inc(slot_used, 1)
                    pe.wait_ge(sel_ready, i + 2)
                    slots_of()
                    for k in range(KD // 2, KD):
                        pe.wait_ge(s_slot[k], 16 * (i + 1))
                        ins = gate_up(cls, k, 0)
                    ins.then_inc(gu_done, 1)
                    for k in range(KD // 2, KD):
                        ins = gate_up(cls, k, 1)
                        ins.then_inc(slot_used if k < KD - 1 else gu_done, 1)
                        if k == KD // 2:
                            transpose_gu(cls, 0)
                    pe.wait_ge(yrow_ready, i + 1)
                    for j in range(KF // 2):
                        down(cls, j)
                        if j == 0:
                            transpose_gu(cls, 1)

                def last_products(cls):
                    for j in range(KF // 2, KF):
                        ins = down(cls, j)
                    ins.then_inc(down_done, 1)

                by_class(pe, cls, products)
                pe.wait_ge(slot_idx_read, i + 2)
                pe.wait_ge(x_gathered, 16 * i + 32)
                by_class(pe, cls1, lambda c: [transpose_x(c, h) for h in range(2)])
                by_class(pe, cls, last_products)


_INS = ["x", "positions", "norm1_g", "w_in", "q_norm_g", "k_norm_g", "sgu_ln_g", "sgu_ln_b", "w_spatial", "b_spatial",
        "w_branch_a", "w_branch_b", "w_out", "norm2_g", "w_router", "b_router", "w_gate_up", "b_gate_up", "w_down",
        "b_down"]


def kernel(**inputs):
    import concourse.bacc as bacc
    from concourse.bass_utils import run_bass_kernel_spmd

    nc = bacc.Bacc("TRN2", target_bir_lowering=False, num_devices=1)
    arrays, args = {}, []
    for name in _INS:
        a = np.ascontiguousarray(inputs[name])
        arrays[f"in_{name}"] = a
        args.append(nc.dram_tensor(f"in_{name}", a.shape, mybir.dt.from_np(a.dtype), kind="ExternalInput").ap())
    shape = tuple(inputs["x"].shape)
    args.append(nc.dram_tensor("out_y", shape, F32, kind="ExternalOutput").ap())
    hybrid_layer(nc, *args)
    r = run_bass_kernel_spmd(nc, [arrays], core_ids=[0])
    return r.results[0]["out_y"]
```

```python
from contextlib import ExitStack

import numpy as np
import concourse.bass as bass
from concourse import mybir

P = 128
F32 = mybir.dt.float32
F32R = mybir.dt.float32r
I32 = mybir.dt.int32
U32 = mybir.dt.uint32
ALU = mybir.AluOpType
ACT = mybir.ActivationFunctionType
AX_X = mybir.AxisListType.X
WIDTHS = (64, 96, 128)
HW = WIDTHS[0]
QW = 32
ROUNDS = ((2, 0, 0, 0), (1, 2, 1, 2), (3, 3, 3, 1))


def tile_slots(c, b):
    return QW * (b if c == 3 else c)


def by_class(eng, cls, work):
    with eng.If(cls < 1):
        work(0)
    with eng.Else():
        with eng.If(cls < 2):
            work(1)
        with eng.Else():
            work(2)

ROUND = 1.5 * 2.0 ** 23
PI_IN = 3.1415925
TWO_PI = (6.28125, 0.0019354820251464844, -1.7484556025237907e-07)


class Steps:

    def __init__(self, eng, sem, before=0):
        self.eng, self.sem, self.before, self.n = eng, sem, before, 0

    def __call__(self, ins):
        ins.then_inc(self.sem, 1)
        self.n += 1
        self.eng.wait_ge(self.sem, self.before + self.n)


def hybrid_layer(nc, x, positions, norm1_g, w_in, q_norm_g, k_norm_g, sgu_ln_g, sgu_ln_b, w_spatial,
                 b_spatial, w_branch_a, w_branch_b, w_out, norm2_g, w_router, b_router, w_gate_up,
                 b_gate_up, w_down, b_down, out):
    _, T, D = x.shape
    TT = T // P
    KD = D // P
    HD = q_norm_g.shape[1]
    HALF = HD // 2
    AW = w_branch_a.shape[1]
    KA = AW // P
    HEADS = AW // HD
    GROUPS = 3
    HPG = HEADS // GROUPS
    GW = HPG * HD
    SG = w_spatial.shape[1]
    SW = SG * HD
    E = w_router.shape[2]
    F = w_down.shape[2]
    KF = F // P
    TOPK = 4
    CW = 256
    PAIRS = D // CW
    CH = KD * CW
    EPS = 1e-6
    NEG = -1e30
    SCALE = float(HD) ** -0.5
    LIMIT, ALPHA = 7.0, 1.702
    COL_V = 3 * AW + SW
    COL_U = 3 * AW
    COL_GA = 3 * AW + 2 * SW
    COL_GB = COL_GA + D
    assert T == 4 * P and GW == CW and SW == AW and D == F and KD == 8
    RING = KD + KF // 2
    BW = D // 2

    with ExitStack() as ctx:
        def sb(name, shape, dt=F32):
            return ctx.enter_context(nc.sbuf_tensor(name, shape, dt))

        def sem(name):
            return ctx.enter_context(nc.semaphore(name))

        SLOT = 2 * F
        WORK = 20480
        with ExitStack() as parts:
            def part(name, tiles, width):
                return parts.enter_context(nc.sbuf_tensor(name, [P, tiles, width], F32R))

            merged_high = part("merged_high", KD, T)
            buf_h1 = part("buf_h1", KD, CW)
            attn_high = part("attn_high", KA, T)
            buf_h2 = part("buf_h2", KD, CW)
            buf_h3 = part("buf_h3", KD, CW)
            sgu_high = part("sgu_high", KA, T)
            buf_s = [part(f"buf_s{s}", KD, CW) for s in range(4)]
            h_high = part("h_high", KD, T)
            h_low = part("h_low", KD, T)
            merged_low = part("merged_low", KD, T)
            buf_h0 = part("buf_h0", KD, CW)
            attn_low = part("attn_low", KA, T)
            sgu_low = part("sgu_low", KA, T)
        ring = sb("ring", [P, RING, SLOT])
        flat = ring[:, :, :].rearrange("p s n -> p (s n)")
        qk = flat[:, 0:2 * TT * AW].rearrange("p (k t n) -> p k t n", k=2, t=TT)
        at = 2 * TT * AW
        vtok = flat[:, at:at + TT * AW].rearrange("p (t n) -> p t n", t=TT)
        at += TT * AW
        utok = flat[:, at:at + TT * SW].rearrange("p (t n) -> p t n", t=TT)
        at += TT * SW
        ztok = flat[:, at:at + TT * SW].rearrange("p (t n) -> p t n", t=TT)
        assert at + TT * SW <= 8 * SLOT
        xr = flat[:, 0:TT * D].rearrange("p (t n) -> p t n", t=TT)
        trig = flat[:, TT * D:TT * D + 4 * 8 * HALF].rearrange("p (a u c) -> p a u c", a=4, c=HALF)
        at_h2 = KD * T + CH + KA * T
        raw_mem = [flat[:, (8 + s) * SLOT:(9 + s) * SLOT] for s in range(4)] + [flat[:, at_h2:at_h2 + CH]]
        low_mem = buf_s + [buf_h2]
        high_mem = [buf_s[2], buf_s[3], buf_h3, buf_h0, buf_h1, buf_h2, buf_h3]

        work = sb("work", [P, WORK])
        o_x, o_h, o_qk, o_a, o_s = 0, 4096, 8192, 14336, 17408
        xs = work[:, o_x:o_x + TT * D].rearrange("p (t n) -> p t n", t=TT)
        qkT = work[:, o_qk:o_qk + 12 * T].rearrange("p (k t) -> p k t", k=12)
        mergedT = work[:, o_qk:o_qk + KD * T].rearrange("p (k t) -> p k t", k=KD)
        rows = work[0:HPG, o_qk:o_qk + 8 * T].rearrange("p (r t) -> p r t", t=T)
        mrows, lrows, mrow, drow = rows[:, 0:GROUPS], rows[:, GROUPS:2 * GROUPS], rows[:, 6], rows[:, 7]
        attnT = work[:, o_a:o_a + KA * T].rearrange("p (k t) -> p k t", k=KA)
        bias_raw = work[0:E, o_qk:o_qk + 2 * F]
        bdn = work[0:E, o_qk + (KD * T) + D:o_qk + (KD * T) + 2 * D]
        wsp_raw = work[:, o_a:o_a + SG * P].rearrange("p (g s) -> p g s", g=SG)
        bsp_raw = work[0:SG, o_a + SG * P:o_a + SG * P + P]
        lnb = work[:, o_s:o_s + 2 * SW].rearrange("p (a n) -> p a n", a=2)
        hf = work[:, o_a:o_a + TT * D].rearrange("p (t n) -> p t n", t=TT)
        hfT = work[:, o_h:o_h + KD * T].rearrange("p (k t) -> p k t", k=KD)
        xgT = work[:, o_qk:o_qk + KD * P].rearrange("p (k c) -> p k c", k=KD)
        yrow = work[:, o_qk + D:o_qk + 2 * D]
        xg_tok = work[:, o_qk + 4 * D:o_qk + 5 * D]
        gu_tok = work[:, o_qk + 2 * D:o_qk + 4 * D].rearrange("p (b n) -> p b n", b=4)
        bsum = work[:, o_h:o_h + TT * D].rearrange("p (t n) -> p t n", t=TT)
        gate = work[:, o_h:o_h + D].rearrange("p (k c) -> p k c", k=KF)
        up = work[:, o_h + D:o_h + 2 * D].rearrange("p (k c) -> p k c", k=KF)
        sg = work[:, o_h + 2 * D:o_h + 3 * D].rearrange("p (k c) -> p k c", k=KF)
        act = work[:, o_h + 3 * D:o_h + 4 * D].rearrange("p (k c) -> p k c", k=KF)
        sel = work[:, o_a + TT * D:o_a + TT * D + TT * P].rearrange("p (t c) -> p t c", t=TT)
        aux_at = o_a + TT * D + TT * P
        aux = work[:, aux_at:aux_at + TT * E * 2].rearrange("p (t e a) -> p t e a", t=TT, e=E)
        hot_at = aux_at + TT * E * 2
        hot = work[:, hot_at:hot_at + TT * TOPK * E].rearrange("p (t k e) -> p t k e", t=TT, k=TOPK)
        hotg_at = hot_at + TT * TOPK * E
        hotg = work[:, hotg_at:hotg_at + TT * TOPK * E].rearrange("p (t k e) -> p t k e", t=TT, k=TOPK)
        assert hotg_at + TT * TOPK * E <= WORK

        sc = sb("sc", [P, 2, 1024])
        pt = sb("pt", [P, 1024])
        dist = pt[:, 0:P].bitcast(I32)
        slots_iota, slots_twice = pt[:, 0:T], pt[:, T:T + P]
        ident = sb("ident", [P, P])
        upper = sb("upper", [P, P])
        ones = sb("ones", [P, P])
        wspT = sb("wspT", [P, SG, P])
        cos_t = sb("cos_t", [P, 8, HALF])
        sin_t = sb("sin_t", [P, 8, HALF])
        band = sb("band", [P, 2 * P])
        diag = sb("diag", [P, P])
        qkg = sb("qkg", [P, 2, HD])
        biases = sb("biases", [P, 2 * KF, E])
        wr = sb("wr", [P, KD, E])
        brb = sb("brb", [P, E])
        pick = sb("pick", [HPG, 2, P])
        bsp = sb("bsp", [P, SG])
        g1 = sb("g1", [P, KD])
        pos_i = sb("pos_i", [P, 8], I32)
        pos_f = sb("pos_f", [P, 8])
        inv_f = sb("inv_f", [P, HALF])
        ss = sb("ss", [P, TT])
        rs = sb("rs", [P, TT])
        hss = sb("hss", [P, 2, TT, HEADS])
        mstat = sb("mstat", [P, 12, HPG])
        nmstat = sb("nmstat", [P, 12, HPG])
        lstat = sb("lstat", [P, 12, HPG])
        bn = sb("bn", [P, TT, 2, 6])
        mv = sb("mv", [P, TT, 2])
        iota_e = sb("iota_e", [P, E])
        pcol = sb("pcol", [P, 3])
        tiny = sb("tiny", [P, 16])
        MI = 64
        meta_i = cos_t[0:1, 0:4 * MI // HALF, :].rearrange("p a c -> p (a c)").bitcast(I32)
        idx = sb("idx", [P, 1], U32)
        idx_next = sb("idx_next", [P, 1], U32)
        scf = sc[:, :, :].rearrange("p a n -> p (a n)")
        g2b, squares = scf[:, 0:D], scf[:, D:2 * D]
        lg = scf[:, 0:128].rearrange("p (t e) -> p t e", t=TT)
        top = scf[:, 128:160].rearrange("p (t k) -> p t k", t=TT)
        topi = scf[:, 160:192].bitcast(U32).rearrange("p (t k) -> p t k", t=TT)
        topf = scf[:, 192:208].rearrange("p (t k) -> p t k", t=TT)
        ge = scf[:, 208:224].rearrange("p (t k) -> p t k", t=TT)
        gsum = scf[:, 224:228]
        chosen = scf[:, 256:384].rearrange("p (t e) -> p t e", t=TT)
        posm = scf[:, 384:512].rearrange("p (t e) -> p t e", t=TT)
        cnt = scf[:, 512:544]
        nblk = scf[:, 544:576]
        scan = scf[:, 576:576 + 96].rearrange("p (a n) -> p a n", a=2)
        cmpe = scf[:, 672:704]
        cmpn = scf[:, 704:736]
        meta = scf[:, 736:740]
        bias_now = scf[:, 768:768 + 2 * KF]
        aux_now = scf[:, 800:800 + 2 * TT].rearrange("p (t a) -> p t a", t=TT)
        slot_now = scf[:, 810:812]
        slot_next = scf[:, 812:814]
        slot_pad = scf[:, 814:815]
        rel = scf[:, 816:820]
        row_f = scf[:, 820:821]
        row_next = scf[:, 821:822]
        gates = scf[:, 1024:1024 + TT * E].rearrange("p (t e) -> p t e", t=TT)
        gatesT = scf[0:E, 1280:1280 + T]

        bank = ctx.enter_context(nc.psum_tensor("bank", [P, 8, 512], F32))

        y_acc = nc.dram_tensor("y_acc", [T + P, D], F32, kind="Internal").ap()
        hf_rows = nc.dram_tensor("hf_rows", [T + P, D], F32, kind="Internal").ap()
        y_halves = y_acc.rearrange("t (h n) -> (t h) n", h=2)

        s_xt = [sem(f"x_tile_loaded{t}") for t in range(TT)]
        s_x, s_g1, s_small, s_g2, s_bdn = (
            sem("x_loaded_again"), sem("g1_loaded"), sem("small_loaded"), sem("g2_loaded"), sem("bdn_loaded"))
        psum_clear, trig_ready, trig_done = sem("psum_clear"), sem("trig_ready"), sem("trig_done")
        consts2, ln_scaled = sem("moe_consts_made"), sem("ln_scaled")
        s_chunk = [sem(f"chunk_loaded{s}") for s in range(5)]
        high_made, low_made = sem("chunk_high_made"), sem("chunk_low_made")
        attn_rest, last_split, last_rest, last_merged = sem("attn_low"), sem("last_merged_high"), sem("last_merged_low"), sem("last_merged")
        hT_high, attn_split, sgu_split, merged_split, merged_rest = (
            sem("hT_high"), sem("attn_high"), sem("sgu_high"), sem("merged_high"), sem("merged_low"))
        consts = sem("consts_made")
        dve_step, act_step, pool_step = sem("dve_step"), sem("act_step"), sem("pool_step")
        dve_moe = sem("dve_moe_step")
        rms_sum, rms_var, rms_root, xr_ready = sem("rms_sum"), sem("rms_var"), sem("rms_root"), sem("xr_ready")
        setup_t, setup_e = sem("setup_transposed"), sem("setup_evacuated")
        hT_t, hT_e = sem("hT_transposed"), sem("hT_evacuated")
        proj_done, proj_read = sem("proj_done"), sem("proj_read")
        sq_done, sq_read, hvar, hroot = sem("squares_done"), sem("squares_read"), sem("head_var"), sem("head_root")
        scaled, gained, roped = sem("qk_scaled"), sem("qk_gained"), sem("qk_roped")
        pair_t, pair_e = sem("pair_transposed"), sem("pair_evacuated")
        score_done, max_done, prob_done = sem("score_done"), sem("max_done"), sem("prob_done")
        pt_t, pt_e, o_done, o_read = sem("probT_done"), sem("probT_evacuated"), sem("o_done"), sem("o_read")
        ztok_ready, utok_ready, ln_var, ln_root, ln_done = (
            sem("z_gelu"), sem("u_gelu"), sem("ln_var"), sem("ln_root"), sem("ln_done"))
        ml_t, ml_e, gexp_in, gexp, wrow_ready = sem("ml_t"), sem("ml_e"), sem("gexp_in"), sem("gexp"), sem("wrow_ready")
        mix_done, mix_read = sem("mix_done"), sem("mix_read")
        spread_done, spread_read = sem("spread_done"), sem("spread_read")
        sgu_t, sgu_e = sem("sgu_transposed"), sem("sgu_evacuated")
        gate_done, gate_read, y_done, y_read = sem("gate_done"), sem("gate_read"), sem("branch_done"), sem("branch_read")
        part_b, merged = sem("part_b"), sem("merged")
        out_done, out_read = sem("out_done"), sem("out_read")
        x1_stored = sem("x1_stored")
        rms2_sum, rms2_var, rms2_root, hf_ready = sem("rms2_sum"), sem("rms2_var"), sem("rms2_root"), sem("hf_ready")
        hf_t, hf_e, logit_done = sem("hf_transposed"), sem("hf_evacuated"), sem("logits_done")
        topd, topexp, chosen_ready, place_done, meta_ready, metarow_done, meta_loaded = (
            sem("top_diff"), sem("top_exp"), sem("chosen_ready"), sem("places_done"), sem("meta_ready"),
            sem("meta_rows"), sem("meta_loaded"))
        s_slot = [sem(f"slot_loaded{s}") for s in range(RING)]
        slot_used = sem("slot_used")
        sel_ready, hf_stored, next_rows, x_gathered = (
            sem("sel_ready"), sem("hf_stored"), sem("next_rows_known"), sem("x_gathered"))
        xg_t, xg_e, gather_turn = sem("xg_transposed"), sem("xg_evacuated"), sem("gather_turn")
        gu_done, gated, sig_done, act_ready = (
            sem("gate_up_done"), sem("gate_ready"), sem("sigmoid_done"), sem("act_ready"))
        down_done, yrow_ready, y_added = sem("down_done"), sem("yrow_ready"), sem("y_added")
        gu_out_a, gu_out_b, gu_t = sem("gate_up_out_a"), sem("gate_up_out_b"), sem("gate_up_transposed")
        gates_ready, gatesT_t, gatesT_e, bsum_done, bsum_read, bias_added = (
            sem("gates_ready"), sem("gatesT_transposed"), sem("gatesT_evacuated"), sem("bias_sum_done"),
            sem("bias_sum_read"), sem("bias_added"))
        slot_idx, slot_idx_read, now_ready = sem("slot_idx_done"), sem("slot_idx_read"), sem("slot_now_ready")
        row_ready = sem("slot_rows_ready")
        out_stored, add_turn, rows_free = sem("out_stored"), sem("add_turn"), sem("rows_free")

        block = ctx.enter_context(nc.Block())

        pos = positions[0]
        smalls = [
            (pos_i[:, 0:4], pos.rearrange("(j p) -> p j", p=P)),
            (pos_i[:, 4:8], pos.rearrange("(p j) -> p j", p=P)),
            (qkg[:, 0, :], q_norm_g[0].partition_broadcast(P)),
            (qkg[:, 1, :], k_norm_g[0].partition_broadcast(P)),
            (wsp_raw, w_spatial[0].rearrange("g t s -> t g s")),
            (bsp_raw, b_spatial[0]),
            (bias_raw[:, 0:2 * F], b_gate_up[0]),
            (wr[:, :, :], w_router[0].rearrange("(k p) e -> p k e", p=P)),
            (brb[:, :], b_router[0].partition_broadcast(P)),
            (lnb[:, 0, :], sgu_ln_g[0].partition_broadcast(P)),
            (lnb[:, 1, :], sgu_ln_b[0].partition_broadcast(P)),
        ]
        SMALL = len(smalls)
        SETUP = SG // 4 + 1 + 2 * KF // 4
        CONSTS = 5
        SLOTS = 31

        def unit_blocks(u):
            return [u % 4 - 1, u % 4] if 0 < u < 4 else [u % 4]

        def unit_width(u):
            return P * len(unit_blocks(u))

        def unit_mask(u):
            return band[:, :] if 0 < u < 4 else band[:, P:2 * P] if u < 8 else diag[:, :]

        def heads(ap, width):
            return ap[:, 0:HPG * width].rearrange("p (h w) -> p h w", h=HPG)

        def order_cols(ap, group, j):
            if group == 0:
                return ap[:, j * P:(j + 1) * P]
            return ap[:, j:T:4]

        def chunk_src(n):
            if n < 9:
                return w_in, n * CW, KD
            if n < 12:
                return w_in, COL_V + (n - 9) * CW, KD
            if n < 15:
                return w_in, COL_U + (n - 12) * CW, KD
            if n < 15 + 4 * PAIRS:
                i, s = divmod(n - 15, 4)
                w, c, k = [(w_in, COL_GB, KD), (w_in, COL_GA, KD), (w_branch_b, 0, KA), (w_branch_a, 0, KA)][s]
                return w, c + i * CW, k
            return w_out, (n - 15 - 4 * PAIRS) * CW, KD

        CHUNKS = 15 + 5 * PAIRS
        OUT_ORDER = [(t, c) for t in (0, 1) for c in range(PAIRS - 1)] + [(0, PAIRS - 1), (1, PAIRS - 1)]
        OUT_ORDER += [(t, c) for t in (2, 3) for c in range(PAIRS)]
        BANK_OF = (0, 1, 2, 3, 6, 7)
        SPREAD_BANK = (2, 3, 6, 7, 2, 3)
        x1_at = [OUT_ORDER.index((t, PAIRS - 1)) for t in range(TT)]

        def raw_at(n):
            return (0, 1, 4)[n % 3] if n < 9 else (n - 9) % 2 if n < 15 else (n - 15) % 4

        def high_at(n):
            return n % 3 if n < 9 else (n - 9) % 2 if n < 15 else 3 + (n - 15) % 4

        def k_tiles(n):
            return chunk_src(n)[2]

        def raw(n):
            return raw_mem[raw_at(n)].rearrange("p (k n) -> p k n", k=KD)[:, 0:k_tiles(n), :]

        def low(n):
            return low_mem[raw_at(n)][:, 0:k_tiles(n), :]

        def high(n):
            return high_mem[high_at(n)][:, 0:k_tiles(n), :]

        def chunk_used(n):
            if n < 15:
                return proj_done, TT * (n + 1)
            if n < 15 + 4 * PAIRS:
                i, part = divmod(n - 15, 4)
                return (gate_done, y_done)[part // 2], 4 * i + 2 * (part % 2) + 2
            return out_done, OUT_ORDER.index((TT - 1, n - 15 - 4 * PAIRS)) + 1

        chunk_turn = [sum(raw_at(m) == raw_at(n) for m in range(n + 1)) for n in range(CHUNKS)]

        def split_high(eng, n, loaded=None):
            eng.wait_ge(s_chunk[raw_at(n)], 16 * chunk_turn[n] if loaded is None else loaded)
            eng.copy(high(n), raw(n)).then_inc(high_made, 1)

        def split_low(eng, n, made=None):
            eng.wait_ge(high_made, n + 1 if made is None else made)
            eng.tensor_tensor(low(n), raw(n), high(n).bitcast(F32), ALU.subtract).then_inc(low_made, 1)

        @block.sync
        def _(sp):
            for t in range(TT):
                sp.dma_start(xs[:, t, :], x[0, t * P:(t + 1) * P, :]).then_inc(s_xt[t], 16)
            last = {}
            for n in range(CHUNKS):
                w, c, k = chunk_src(n)
                at = raw_at(n)
                if at in last:
                    sp.wait_ge(*chunk_used(last[at]))
                last[at] = n
                if 9 <= n < 15:
                    last[2 + high_at(n)] = n
                sp.dma_start(raw(n),
                             w[0].rearrange("(k p) n -> p k n", p=P)[:, :, c:c + CW]).then_inc(s_chunk[at], 16)
                if n == 1:
                    for dst, src in smalls:
                        sp.dma_start(dst, src, allow_slow_non_contiguous=True).then_inc(s_small, 16)
                if n == 16 + 4 * PAIRS:
                    for t in range(TT):
                        sp.dma_start(xs[:, t, :], x[0, t * P:(t + 1) * P, :]).then_inc(s_x, 16)

            def slot_copy(s, gate_up, down):
                if s < KD:
                    return ring[:, s, :], gate_up[s * P:(s + 1) * P, :]
                j = 2 * (s - KD)
                return (ring[:, s, :].rearrange("p (j n) -> p j n", j=2),
                        down.rearrange("(j p) n -> p j n", p=P)[:, j:j + 2, :])

            branches, outs = (y_done, 4 * PAIRS), [chunk_used(CHUNKS - PAIRS + c) for c in range(PAIRS)]

            def load_slots(pairs):
                for s, used in pairs:
                    sp.wait_ge(*used)
                    sp.dma_start(*slot_copy(s, w_gate_up[0, 0], w_down[0, 0])).then_inc(s_slot[s], 16)

            load_slots([(3, branches), (7, branches)])
            sp.wait_ge(y_read, 4 + 4 * PAIRS)
            sp.dma_start(g2b, norm2_g[0].partition_broadcast(P)).then_inc(s_g2, 16)
            load_slots([(8, outs[0]), (2, outs[1]), (9, outs[1]), (4, outs[2]), (10, outs[2]), (0, outs[3])])
            sp.dma_start(bdn, b_down[0]).then_inc(s_bdn, 16)
            for t in range(TT):
                sp.wait_ge(hf_ready, t + 1)
                sp.dma_start(hf_rows[t * P:(t + 1) * P, :], hf[:, t, :]).then_inc(hf_stored, 16)
            sp.dma_start(hf_rows[T:T + P, :], hf[:, 0, :]).then_inc(hf_stored, 16)
            load_slots([(1, outs[3]), (5, outs[3]), (6, outs[3]), (11, outs[3])])
            for t in range(TT):
                sp.wait_ge(bias_added, t + 1)
                sp.dma_start(y_acc[t * P:(t + 1) * P, :], xs[:, t, :]).then_inc(x1_stored, 16)
            sp.dma_start(y_acc[T:T + P, :], xs[:, 0, :]).then_inc(x1_stored, 16)
            sp.wait_ge(meta_loaded, 1)
            items = sp.value_load(meta_i[0:1, 3 * MI:3 * MI + 1], min_val=E, max_val=E + 15)
            with sp.Fori(1, items) as i:
                e = sp.value_load(meta_i[0:1, bass.ds(i, 1)], min_val=0, max_val=E - 1)
                gu = w_gate_up[0, bass.ds(e, 1)].rearrange("e k n -> (e k) n")
                dn = w_down[0, bass.ds(e, 1)].rearrange("e k n -> (e k) n")
                for s in range(RING):
                    if s == KD - 1:
                        sp.wait_ge(gu_done, i * 2)
                    elif s == RING - 1:
                        sp.wait_ge(down_done, i)
                    else:
                        sp.wait_ge(slot_used, (i - 1) * (RING - 2) + s + 1 - (s > KD - 1))
                    sp.dma_start(*slot_copy(s, gu, dn)).then_inc(s_slot[s], 16)
            sp.wait_ge(y_added, items * 16)
            sp.dma_start(out[0], y_acc[0:T, :]).then_inc(out_stored, 16)
            sp.wait_ge(out_stored, 16)

        @block.gpsimd
        def _(pool):
            step = Steps(pool, pool_step)
            pool.sem_inc(rows_free, 1)
            pool.sem_inc(merged, 1)
            step(pool.memset(ident[:, :], 0.0))
            pool.affine_select(out=ident[:, :], in_=ident[:, :], compare_op=ALU.not_equal, fill=1.0, base=0,
                               pattern=[[-1, P]], channel_multiplier=1).then_inc(consts, 1)
            step(pool.memset(ones[:, :], 1.0))
            pool.affine_select(out=upper[:, :], in_=ones[:, :], compare_op=ALU.is_gt, fill=0.0, base=0,
                               pattern=[[1, P]], channel_multiplier=-1)
            for c in range(HALF):
                ins = pool.memset(inv_f[:, c:c + 1], float(np.float32(10000.0) ** (-np.float32(c) / np.float32(HALF))))
            ins.then_inc(consts, 1)
            step(pool.memset(band[:, :], 0.0))
            step(pool.affine_select(out=band[:, :], in_=band[:, :], compare_op=ALU.is_ge, fill=NEG, base=P,
                                    pattern=[[-1, 2 * P]], channel_multiplier=1))
            step(pool.affine_select(out=band[:, :], in_=band[:, :], compare_op=ALU.is_ge, fill=NEG, base=0,
                                    pattern=[[1, 2 * P]], channel_multiplier=-1))
            pool.iota(dist, pattern=[[-1, P]], base=T, channel_multiplier=1)
            pool.iota(iota_e[:, :], pattern=[[1, E]], base=0, channel_multiplier=0,
                      allow_small_or_imprecise_dtypes=True)
            pool.iota(pcol[:, 0:1], pattern=[[1, 1]], base=0, channel_multiplier=1,
                      allow_small_or_imprecise_dtypes=True)
            step(pool.memset(pcol[:, 2:3], 1.0))
            pool.affine_select(out=pcol[:, 2:3], in_=pcol[:, 2:3], compare_op=ALU.is_ge, fill=0.0, base=-HW,
                               pattern=[[0, 1]], channel_multiplier=1)
            pool.iota(pcol[:, 1:2], pattern=[[1, 1]], base=T + 1, channel_multiplier=1,
                      allow_small_or_imprecise_dtypes=True).then_inc(consts, 1)
            step(pool.memset(pick[:, :, :], 1.0))
            pool.affine_select(out=pick[:, :, :].rearrange("p i (a d) -> p i a d", a=2),
                               in_=pick[:, :, :].rearrange("p i (a d) -> p i a d", a=2),
                               compare_op=ALU.is_equal, fill=0.0, base=0,
                               pattern=[[-1, 2], [-2, 2], [0, HD]], channel_multiplier=1).then_inc(consts, 1)
            split_low(pool, 0)
            split_low(pool, 1)
            pool.wait_ge(s_small, 16 * SMALL)
            pool.affine_select(out=wsp_raw, in_=wsp_raw, compare_op=ALU.is_ge, fill=0.0, base=0,
                               pattern=[[0, SG], [-1, P]], channel_multiplier=1).then_inc(consts, 1)
            split_low(pool, 2)
            for kind in range(2):
                for n in range(3 * kind + 3, 3 * kind + 6):
                    split_low(pool, n)
                for t in range(TT):
                    pool.wait_ge(scaled, kind * TT + t + 1)
                    v = qk[:, kind, t, :].rearrange("p (h d) -> p h d", d=HD)
                    pool.tensor_tensor(v, v, qkg[:, kind, :].unsqueeze(1).to_broadcast([P, HEADS, HD]),
                                       ALU.mult).then_inc(gained, 1)
            for n in range(9, 15):
                split_low(pool, n)
            for t in range(TT):
                pool.wait_ge(ln_scaled, t + 1)
                step(pool.tensor_tensor(ztok[:, t, :], ztok[:, t, :], lnb[:, 0, :], ALU.mult))
                pool.tensor_tensor(ztok[:, t, :], ztok[:, t, :], lnb[:, 1, :], ALU.add).then_inc(ln_done, 1)
            for n in range(15, 19):
                split_low(pool, n)
            for k in range(KA):
                pool.wait_ge(attn_split, k + 1)
                pool.tensor_tensor(attn_low[:, k, :], attnT[:, k, :], attn_high[:, k, :].bitcast(F32),
                                   ALU.subtract).then_inc(attn_rest, 1)
            with pool.Fori(0, PAIRS - 1) as i:
                for part in range(3):
                    split_low(pool, 19 + part, 4 * i + 20 + part)
                for jj in range(2):
                    pool.wait_ge(part_b, 2 * i + jj + 1)
                    m = mergedT[:, bass.ds(2 * i + jj, 1), :].rearrange("p a t -> p (a t)")
                    pool.tensor_tensor(m, m, pt[:, jj * T:jj * T + T], ALU.add).then_inc(merged, 1)
                for jj in range(2):
                    pool.wait_ge(merged_split, 2 * i + jj + 1)
                    m = mergedT[:, bass.ds(2 * i + jj, 1), :].rearrange("p a t -> p (a t)")
                    m_high = merged_high[:, bass.ds(2 * i + jj, 1), :].rearrange("p a t -> p (a t)")
                    m_low = merged_low[:, bass.ds(2 * i + jj, 1), :].rearrange("p a t -> p (a t)")
                    pool.tensor_tensor(m_low, m, m_high.bitcast(F32), ALU.subtract).then_inc(merged_rest, 1)
                split_low(pool, 22, 4 * i + 23)
            for n in range(15 + 4 * PAIRS, CHUNKS):
                split_low(pool, n)
            pool.wait_ge(out_done, 1)
            pool.iota(slots_iota, pattern=[[1, T]], base=0, channel_multiplier=0,
                      allow_small_or_imprecise_dtypes=True)
            pool.iota(slots_twice, pattern=[[0, 2], [1, HW]], base=0, channel_multiplier=0,
                      allow_small_or_imprecise_dtypes=True)
            pool.iota(aux[:, :, :, 0], pattern=[[P, TT], [0, E]], base=1, channel_multiplier=1,
                      allow_small_or_imprecise_dtypes=True).then_inc(consts2, 1)
            pool.wait_ge(meta_loaded, 1)
            items = pool.value_load(meta_i[0:1, 3 * MI:3 * MI + 1], min_val=E, max_val=E + 15)

            def gather(cls):
                rows = slice(0, WIDTHS[cls])
                pool.indirect_dma_start(xg_tok[rows, :], None, hf_rows,
                                        bass.IndirectOffsetOnAxis(ap=idx_next[rows, 0:1], axis=0)
                                        ).then_inc(x_gathered, 16)

            cls0 = pool.value_load(meta_i[0:1, 2 * MI:2 * MI + 1], min_val=0, max_val=2)
            pool.wait_ge(hf_stored, 16 * (TT + 1))
            pool.wait_ge(next_rows, 1)
            pool.sem_inc(gather_turn, 1)
            by_class(pool, cls0, gather)
            for t in range(TT):
                pool.wait_ge(bsum_read, t + 1)
                pool.tensor_tensor(xs[:, t, :], xs[:, t, :], bsum[:, t, :], ALU.add).then_inc(bias_added, 1)
            with pool.Fori(0, items) as i:
                cls1 = pool.value_load(meta_i[0:1, bass.ds(i + 1 + 2 * MI, 1)], min_val=0, max_val=2)
                pool.wait_ge(next_rows, i + 2)
                pool.wait_ge(xg_t, 2 * i + 2)
                pool.sem_inc(gather_turn, 1)
                by_class(pool, cls1, gather)
                pool.wait_ge(yrow_ready, i + 2)
                pool.wait_ge(x1_stored, 16 * (TT + 1))
                pool.sem_inc(add_turn, 1)
                cls = pool.value_load(meta_i[0:1, bass.ds(i + 2 * MI, 1)], min_val=0, max_val=2)
                with pool.If(cls < 1):
                    pool.indirect_dma_start(y_halves, bass.IndirectOffsetOnAxis(ap=idx[:, 0:1], axis=0),
                                            yrow[:, 0:BW], None, compute_op=ALU.add).then_inc(y_added, 16)
                with pool.Else():
                    pool.indirect_dma_start(y_acc, bass.IndirectOffsetOnAxis(ap=idx[:, 0:1], axis=0), yrow, None,
                                            compute_op=ALU.add).then_inc(y_added, 16)
                pool.wait_ge(y_added, i * 16 + 16)
                pool.sem_inc(rows_free, 1)

        @block.scalar
        def _(ae):
            ae.sem_inc(yrow_ready, 1)
            ae.dma_start(g1[:, :], norm1_g[0].rearrange("(k p) -> p k", p=P),
                         allow_slow_non_contiguous=True).then_inc(s_g1, 16)
            for t in range(TT):
                ae.wait_ge(s_xt[t], 16)
                ae.activation(work[:, o_h + t * D:o_h + (t + 1) * D], xs[:, t, :], ACT.Square,
                              accum_out=ss[:, t:t + 1]).then_inc(rms_sum, 1)
            ae.wait_ge(rms_var, 1)
            ae.activation(rs[:, :], rs[:, :], ACT.Sqrt).then_inc(rms_root, 1)
            split_high(ae, 0)
            ae.wait_ge(s_g1, 16)
            for k in range(KD):
                ae.wait_ge(hT_t, k + 1)
                ae.activation(h_high[:, k, :], bank[:, k % 4, :], ACT.Copy, scale=g1[:, k:k + 1]).then_inc(hT_high, 1)
            ae.sem_inc(proj_read, 2)
            split_high(ae, 1)

            for kind in range(3):
                for g in range(GROUPS):
                    for t in range(TT):
                        n = kind * 12 + g * TT + t
                        ae.wait_ge(proj_done, n + 1)
                        dst = (qk[:, kind] if kind < 2 else vtok)[:, t, g * GW:(g + 1) * GW]
                        ae.copy(dst, bank[:, n % 2, 0:CW]).then_inc(proj_read, 1)
                        if t == 2:
                            split_high(ae, 3 * kind + g + 2)
                    if kind == 0 and g == 1:
                        ae.wait_ge(trig_ready, 1)
                        ae.activation(sin_t[:, :, :], trig[:, 2], ACT.Sin).then_inc(trig_done, 1)
                        ae.activation(cos_t[:, :, :], trig[:, 3], ACT.Sin).then_inc(trig_done, 1)
                if kind < 2:
                    ae.wait_ge(proj_read, 2 + 12 * (kind + 1))
                    for t in range(TT):
                        m = kind * TT + t
                        if m >= 2:
                            ae.wait_ge(sq_read, m - 1)
                        ae.activation(sc[:, m % 2, 0:AW], qk[:, kind, t, :], ACT.Square).then_inc(sq_done, 1)
                    ae.wait_ge(hvar, kind + 1)
                    ae.activation(hss[:, kind], hss[:, kind], ACT.Sqrt).then_inc(hroot, 1)

            for b in range(SETUP):
                ae.wait_ge(setup_t, b + 1)
                src = bank[:, 4 + b % 4, :]
                if b < SG // 4:
                    ins = ae.copy(wspT[:, 4 * b:4 * b + 4, :], src.rearrange("p (g t) -> p g t", g=4))
                elif b == SG // 4:
                    ins = ae.copy(bsp[:, :], src[:, 0:SG])
                else:
                    j = 4 * (b - SG // 4 - 1)
                    ins = ae.copy(biases[:, j:j + 4, :], src[:, 0:4 * E].rearrange("p (j e) -> p j e", j=4))
                ins.then_inc(setup_e, 1)

            def exps(u):
                ae.wait_ge(max_done, u + 1)
                p = heads(sc[:, u % 2, :], unit_width(u))
                for h in range(HPG):
                    ins = ae.activation(p[:, h, :], p[:, h, :], ACT.Exp, bias=nmstat[:, u, h:h + 1], scale=SCALE,
                                        accum_out=lstat[:, u, h:h + 1])
                ins.then_inc(prob_done, 1)

            for s in range(SLOTS):
                if s < 12:
                    ae.wait_ge(pair_t, s + 1)
                    g, r = divmod(s, 4)
                    ae.copy(qkT[:, (r // 2) * KA + 2 * g + r % 2, :], bank[:, 6, :]).then_inc(pair_e, 1)
                if s < 24:
                    ae.wait_ge(proj_done, 36 + s + 1)
                    c, t = divmod(s, TT)
                    dst = ztok if c < 3 else utok
                    ae.copy(dst[:, t, (c % 3) * CW:(c % 3 + 1) * CW], bank[:, s % 2, 0:CW]).then_inc(proj_read, 1)
                    if t == 1 and 0 < c < 5:
                        split_high(ae, 10 + c)
                if s % 2 == 1 and 5 <= s < 29:
                    exps((s - 5) // 2)
                if s == 12 or s == 24:
                    half, ready = (ztok, ztok_ready) if s == 12 else (utok, utok_ready)
                    ae.wait_ge(proj_read, 2 + 36 + s)
                    for t in range(TT):
                        ae.activation(half[:, t, :], half[:, t, :], ACT.Gelu).then_inc(ready, 1)
                if s == 29:
                    ae.wait_ge(score_done, 12)
                    split_high(ae, 15)
                if s == 30:
                    split_high(ae, 16)
                if s == 16:
                    ae.wait_ge(ln_var, TT)
                    ae.activation(mv[:, :, 1], mv[:, :, 1], ACT.Sqrt).then_inc(ln_root, 1)
            for a in range(2):
                for g in range(GROUPS):
                    ae.wait_ge(ml_t, 3 * a + g + 1)
                    src, dst = bank[0:HPG, 2 + 3 * a + g, :], rows[:, 3 * a + g]
                    if g > 0:
                        dst = dst.rearrange("p (m s) -> p s m", s=4)
                        src = src.rearrange("p (s m) -> p s m", s=4)
                    ae.copy(dst, src).then_inc(ml_e, 1)
            for k in range(KA):
                ae.wait_ge(sgu_t, k + 1)
                ae.copy(sgu_high[:, k, :], bank[:, BANK_OF[k], :]).then_inc(sgu_split, 1)
            split_high(ae, 17)
            split_high(ae, 18)
            ae.wait_ge(gexp_in, 1)
            ae.activation(mrows, mrows, ACT.Exp, scale=SCALE).then_inc(gexp, 1)

            def gate_sigmoid(n, part, jj):
                ae.wait_ge(gate_done, n + 1)
                ae.activation(sc[:, part, jj * T:jj * T + T], bank[:, 4 * jj + part, :], ACT.Sigmoid).then_inc(gate_read, 1)

            for n in range(4):
                gate_sigmoid(n, n // 2, n % 2)
            for k in range(KA):
                ae.wait_ge(spread_read, k + 1)
                ae.copy(attn_high[:, k, :], attnT[:, k, :]).then_inc(attn_split, 1)

            def split_pair(i, split, done):
                def chunk(part):
                    if done is merged:
                        split_high(ae, 19 + part, 16 * (i + chunk_turn[19 + part]))
                    else:
                        split_high(ae, 15 + 4 * PAIRS + part)

                chunk(0)
                chunk(1)
                chunk(2)
                for jj in range(2):
                    ae.wait_ge(done, 2 * i + jj + 2 if done is merged else jj + 1)
                    m = mergedT[:, bass.ds(2 * i + jj, 1), :].rearrange("p a t -> p (a t)")
                    m_high = merged_high[:, bass.ds(2 * i + jj, 1), :].rearrange("p a t -> p (a t)")
                    ae.copy(m_high, m).then_inc(split, 1)
                chunk(3)

            with ae.Fori(0, PAIRS - 1) as i:
                split_pair(i, merged_split, merged)
                for part in range(2):
                    for jj in range(2):
                        n = 4 * i + 4 + 2 * part + jj
                        ae.wait_ge(y_read, n + 1)
                        gate_sigmoid(n, part, jj)
            split_pair(PAIRS - 1, last_split, last_merged)
            def norm_square(t):
                ae.wait_ge(out_read, x1_at[t] + 1)
                if t == 0:
                    ae.wait_ge(y_read, 4 + 4 * PAIRS)
                else:
                    ae.wait_ge(rms2_sum, t)
                ae.activation(squares, xs[:, t, :], ACT.Square, accum_out=ss[:, t:t + 1]).then_inc(rms2_sum, 1)

            def norm_root(t):
                ae.wait_ge(rms2_var, t + 1)
                ae.activation(rs[:, t:t + 1], rs[:, t:t + 1], ACT.Sqrt).then_inc(rms2_root, 1)

            def read_hf(t):
                ae.wait_ge(hf_t, t + 1)
                b = 2 + 4 * (t % 2)
                ae.copy(hfT[:, :, t * P:(t + 1) * P].rearrange("p (a k) c -> p a k c", a=2),
                        bank[:, b:b + 2, :].rearrange("p a (k c) -> p a k c", k=4)).then_inc(hf_e, 1)

            for t in range(TT):
                norm_square(t)
                if t >= 2:
                    read_hf(t - 2)
                norm_root(t)
            read_hf(2)
            read_hf(3)
            ae.wait_ge(topd, 1)
            ae.activation(ge, ge, ACT.Exp).then_inc(topexp, 1)
            ae.wait_ge(gatesT_t, 1)
            ae.copy(gatesT, bank[0:E, 7, :]).then_inc(gatesT_e, 1)
            for t in range(TT):
                ae.wait_ge(bsum_done, t + 1)
                b = 2 * (t % 2)
                ae.copy(bsum[:, t, :], bank[:, b:b + 2, :].rearrange("p a n -> p (a n)")).then_inc(bsum_read, 1)

            def read_xg(half, n):
                ae.wait_ge(xg_t, n)
                ae.copy(xgT[:, 4 * half:4 * half + 4, :],
                        bank[:, 6 + half, :].rearrange("p (k c) -> p k c", k=4)).then_inc(xg_e, 1)

            ae.wait_ge(meta_loaded, 1)
            items = ae.value_load(meta_i[0:1, 3 * MI:3 * MI + 1], min_val=E, max_val=E + 15)
            read_xg(0, 1)
            read_xg(1, 2)
            with ae.Fori(0, items) as i:
                cls = ae.value_load(meta_i[0:1, bass.ds(i + 2 * MI, 1)], min_val=0, max_val=2)

                def gates_part(N):
                    for h in range(2):
                        ae.wait_ge(gu_done, 2 * i + h + 1)
                        ae.copy(gu_tok[:, h, :], bank[:, h, :]).then_inc(gu_out_a, 1)
                        ae.wait_ge(gated, 2 * i + h + 1)
                        ae.activation(sg[:, 4 * h:4 * h + 4, 0:N], gate[:, 4 * h:4 * h + 4, 0:N], ACT.Sigmoid,
                                      scale=ALPHA).then_inc(sig_done, 1)

                by_class(ae, cls, lambda c: gates_part(WIDTHS[c]))
                for h in range(2):
                    read_xg(h, 2 * i + h + 3)

                def scale_rows(dst, src):
                    ae.wait_ge(down_done, i + 1)
                    ae.wait_ge(now_ready, i + 1)
                    ae.wait_ge(rows_free, i + 1)
                    ae.activation(dst, src, ACT.Copy, scale=slot_now[:, 1:2]).then_inc(yrow_ready, 1)

                with ae.If(cls < 1):
                    scale_rows(yrow[:, 0:BW], bank[:, 4, :])
                with ae.Else():
                    scale_rows(yrow, bank[:, 4:6, :].rearrange("p a n -> p (a n)"))

        @block.vector
        def _(ve):
            step = Steps(ve, dve_step)
            for b in range(8):
                ins = ve.memset(bank[:, b, :], 0.0)
            ins.then_inc(psum_clear, 1)
            ve.wait_ge(rms_sum, TT)
            ve.tensor_scalar(rs[:, :], ss[:, :], 1.0 / D, EPS, ALU.mult, ALU.add).then_inc(rms_var, 1)
            ve.wait_ge(rms_root, 1)
            step(ve.reciprocal(rs[:, :], rs[:, :]))
            for t in range(TT):
                ve.tensor_scalar(xr[:, t, :], xs[:, t, :], rs[:, t:t + 1], None, ALU.mult).then_inc(xr_ready, 1)
            for k in range(KD):
                ve.wait_ge(hT_high, k + 1)
                ve.scalar_tensor_tensor(out=h_low[:, k, :], in0=bank[:, k % 4, :], scalar=g1[:, k:k + 1],
                                        in1=h_high[:, k, :].bitcast(F32), op0=ALU.mult, op1=ALU.subtract
                                        ).then_inc(hT_e, 1)
            ve.wait_ge(consts, 3)
            step(ve.tensor_scalar(dist, dist, 3, None, ALU.bitwise_and))
            step(ve.scalar_tensor_tensor(out=diag[:, :], in0=dist, scalar=NEG, in1=band[:, P:2 * P],
                                         op0=ALU.mult, op1=ALU.add))
            ve.wait_ge(consts, 2)
            ve.wait_ge(s_small, 16 * SMALL)
            step(ve.tensor_copy(pos_f[:, :], pos_i[:, :]))
            ang, n_t = trig[:, 0], trig[:, 1]
            step(ve.tensor_tensor(ang, pos_f[:, :].unsqueeze(2).to_broadcast([P, 8, HALF]),
                                  inv_f[:, :].unsqueeze(1).to_broadcast([P, 8, HALF]), ALU.mult))
            for which, dst in ((0, trig[:, 2]), (1, trig[:, 3])):
                step(ve.tensor_scalar(n_t, ang, 0.5 / np.pi, 0.25 * which, ALU.mult, ALU.add))
                step(ve.tensor_scalar(n_t, n_t, ROUND, None, ALU.add))
                step(ve.tensor_scalar(n_t, n_t, -ROUND, None, ALU.add))
                src = ang
                for part in TWO_PI:
                    step(ve.scalar_tensor_tensor(out=dst, in0=n_t, scalar=-part, in1=src, op0=ALU.mult, op1=ALU.add))
                    src = dst
                step(ve.tensor_scalar(dst, dst, 0.5 * float(np.pi) * which, PI_IN, ALU.add, ALU.min))
                step(ve.tensor_scalar(dst, dst, -PI_IN, None, ALU.max))
            ve.sem_inc(trig_ready, 1)
            ve.wait_ge(trig_done, 2)
            for kind in range(2):
                def q4(t):
                    return qk[:, kind, t, :].rearrange("p (h d) -> p h d", d=HD)
                for t in range(TT):
                    m = kind * TT + t
                    ve.wait_ge(sq_done, m + 1)
                    ins = ve.tensor_reduce(hss[:, kind, t, :],
                                           sc[:, m % 2, 0:AW].rearrange("p (h d) -> p h d", d=HD), AX_X, ALU.add)
                    ins.then_inc(sq_read, 1)
                ve.wait_ge(sq_read, TT * (kind + 1))
                ve.tensor_scalar(hss[:, kind], hss[:, kind], 1.0 / HD, EPS, ALU.mult, ALU.add).then_inc(hvar, 1)
                ve.wait_ge(hroot, kind + 1)
                step(ve.reciprocal(hss[:, kind], hss[:, kind]))
                for t in range(TT):
                    ve.tensor_tensor(q4(t), q4(t), hss[:, kind, t, :].unsqueeze(2).to_broadcast([P, HEADS, HD]),
                                     ALU.mult).then_inc(scaled, 1)
                for t in range(TT):
                    ve.wait_ge(gained, kind * TT + t + 1)
                    prod = pt[:, 0:AW].rearrange("p (a h d) -> p a h d", a=2, d=HALF)
                    a, b = q4(t)[:, :, 0:HALF], q4(t)[:, :, HALF:HD]
                    for order, hs in ((0, slice(0, HPG)), (1, slice(HPG, HEADS))):
                        n = hs.stop - hs.start
                        cs = cos_t[:, order * TT + t, :].unsqueeze(1).to_broadcast([P, n, HALF])
                        sn = sin_t[:, order * TT + t, :].unsqueeze(1).to_broadcast([P, n, HALF])
                        ve.tensor_tensor(prod[:, 0, hs, :], b[:, hs, :], sn, ALU.mult)
                        step(ve.tensor_tensor(prod[:, 1, hs, :], a[:, hs, :], sn, ALU.mult))
                        ve.tensor_tensor(a[:, hs, :], a[:, hs, :], cs, ALU.mult)
                        step(ve.tensor_tensor(b[:, hs, :], b[:, hs, :], cs, ALU.mult))
                    ve.tensor_tensor(a, a, prod[:, 0], ALU.subtract)
                    step(ve.tensor_tensor(b, b, prod[:, 1], ALU.add))
                    ve.sem_inc(roped, 1)

            def mask_max(u):
                W = unit_width(u)
                ve.wait_ge(score_done, u + 1)
                if u >= 2:
                    ve.wait_ge(pt_t, u - 1)
                s_u = sc[:, u % 2, 0:HPG * W].rearrange("p (a i w) -> p a i w", a=2, i=2)
                step(ve.tensor_tensor(s_u, bank[:, 2:4, 0:2 * W].rearrange("p a (i w) -> p a i w", i=2),
                                      unit_mask(u).unsqueeze(1).unsqueeze(1).to_broadcast([P, 2, 2, W]), ALU.add))
                step(ve.tensor_reduce(mstat[:, u, :], heads(sc[:, u % 2, :], W), AX_X, ALU.max))
                ve.tensor_scalar(nmstat[:, u, :], mstat[:, u, :], -SCALE, None, ALU.mult).then_inc(max_done, 1)

            def read_pt(u):
                ve.wait_ge(pt_t, u + 1)
                ve.wait_ge(o_done, u)
                n = HPG * unit_width(u)
                ve.tensor_copy(pt[:, 0:n], bank[:, 4:6, :].rearrange("p a n -> p (a n)")[:, 0:n]).then_inc(pt_e, 1)

            def read_o(u):
                g, j = divmod(u, 4)
                ve.wait_ge(o_done, u + 1)
                for i in range(2):
                    ins = ve.tensor_copy(order_cols(attnT[:, 2 * g + i, :], g, j), bank[:, 7, i * P:(i + 1) * P])
                ins.then_inc(o_read, 1)

            def mix(g):
                ve.wait_ge(mix_done, g + 1)
                u_g = utok[:, :, g * HD:(g + 1) * HD]
                ve.scalar_tensor_tensor(out=u_g, in0=bank[:, g % 2, 0:TT * HD].rearrange("p (t d) -> p t d", t=TT),
                                        scalar=bsp[:, g:g + 1], in1=u_g, op0=ALU.add, op1=ALU.mult).then_inc(mix_read, 1)

            for s in range(SLOTS):
                if s % 2 == 1 and 5 <= s < 29:
                    mask_max((s - 5) // 2)
                if s % 2 == 1 and 7 <= s < 31:
                    read_pt((s - 7) // 2)
                if s % 2 == 0 and 8 <= s < 31:
                    read_o((s - 8) // 2)
                if s >= 25:
                    if s == 25:
                        ve.wait_ge(utok_ready, TT)
                    for g in (2 * s - 50, 2 * s - 49):
                        mix(g)
                if s == 14:
                    for t in range(TT):
                        ve.wait_ge(ztok_ready, t + 1)
                        ve.bn_stats(bn[:, t, 0, :], ztok[:, t, 0:SW // 2])
                        step(ve.bn_stats(bn[:, t, 1, :], ztok[:, t, SW // 2:SW]))
                        step(ve.bn_aggr(mv[:, t, :], bn[:, t, :, :]))
                        ve.tensor_scalar(mv[:, t, 1:2], mv[:, t, 1:2], EPS, None, ALU.add).then_inc(ln_var, 1)
                if s == 18:
                    ve.wait_ge(ln_root, 1)
                    step(ve.reciprocal(mv[:, :, 1], mv[:, :, 1]))
                    for t in range(TT):
                        ve.tensor_scalar(ztok[:, t, :], ztok[:, t, :], mv[:, t, 0:1], mv[:, t, 1:2],
                                         ALU.subtract, ALU.mult).then_inc(ln_scaled, 1)
            for k in range(KA):
                ve.wait_ge(sgu_split, k + 1)
                ve.tensor_tensor(sgu_low[:, k, :], bank[:, BANK_OF[k], :], sgu_high[:, k, :].bitcast(F32),
                                 ALU.subtract).then_inc(sgu_e, 1)
            ve.wait_ge(ml_e, 6)
            step(ve.tensor_tensor(mrow, mrows[:, 0, :], mrows[:, 1, :], ALU.max))
            step(ve.tensor_tensor(mrow, mrow, mrows[:, 2, :], ALU.max))
            ve.tensor_tensor(mrows, mrows, mrow.unsqueeze(1).to_broadcast([HPG, GROUPS, T]), ALU.subtract).then_inc(gexp_in, 1)
            ve.wait_ge(gexp, 1)
            step(ve.tensor_tensor(lrows, lrows, mrows, ALU.mult))
            step(ve.tensor_tensor(drow, lrows[:, 0, :], lrows[:, 1, :], ALU.add))
            step(ve.tensor_tensor(drow, drow, lrows[:, 2, :], ALU.add))
            step(ve.reciprocal(drow, drow))
            ve.tensor_tensor(mrows, mrows, drow.unsqueeze(1).to_broadcast([HPG, GROUPS, T]), ALU.mult).then_inc(wrow_ready, 1)
            for k in range(KA):
                ve.wait_ge(spread_done, k + 1)
                ve.tensor_tensor(attnT[:, k, :], attnT[:, k, :], bank[:, SPREAD_BANK[k], :], ALU.mult).then_inc(spread_read, 1)
            ve.sem_inc(y_read, 4)

            def merge_pair(i, last):
                for ab in range(2):
                    for jj in range(2):
                        n = 4 * i + 2 * ab + jj
                        ve.wait_ge(y_done, n + 1)
                        ve.wait_ge(gate_read, n + 1)
                        m = mergedT[:, bass.ds(2 * i + jj, 1), :].rearrange("p a t -> p (a t)")
                        if ab == 0:
                            dst = m
                        else:
                            dst = pt[:, jj * T:jj * T + T]
                            ve.wait_ge(merged, 2 * i + 1)
                        ve.tensor_tensor(dst, bank[:, 4 * jj + 2 + ab, :], sc[:, ab, jj * T:jj * T + T],
                                         ALU.mult).then_inc(y_read, 1)
                        if ab == 1:
                            ve.wait_ge(y_read, n + 1 + 4)
                            if last:
                                ve.tensor_tensor(m, m, dst, ALU.add).then_inc(last_merged, 1)
                            else:
                                ve.sem_inc(part_b, 1)

            with ve.Fori(0, PAIRS - 1) as i:
                merge_pair(i, False)
            merge_pair(PAIRS - 1, True)
            for jj in range(2):
                ve.wait_ge(last_split, jj + 1)
                k = 2 * (PAIRS - 1) + jj
                ve.tensor_tensor(merged_low[:, k, :], mergedT[:, k, :], merged_high[:, k, :].bitcast(F32),
                                 ALU.subtract).then_inc(last_rest, 1)
            ve.wait_ge(s_x, 16 * TT)

            def add_out(n):
                t, c = OUT_ORDER[n]
                ve.wait_ge(out_done, n + 1)
                v = xs[:, t, c * CW:(c + 1) * CW]
                ve.tensor_tensor(v, v, bank[:, n % 2, 0:CW], ALU.add).then_inc(out_read, 1)

            def norm_var(t):
                ve.wait_ge(rms2_sum, t + 1)
                ve.tensor_scalar(rs[:, t:t + 1], ss[:, t:t + 1], 1.0 / D, EPS, ALU.mult, ALU.add).then_inc(rms2_var, 1)

            def norm_hf(t):
                ve.wait_ge(rms2_root, t + 1)
                step(ve.reciprocal(rs[:, t:t + 1], rs[:, t:t + 1]))
                ve.scalar_tensor_tensor(out=hf[:, t, :], in0=xs[:, t, :], scalar=rs[:, t:t + 1], in1=g2b,
                                        op0=ALU.mult, op1=ALU.mult).then_inc(hf_ready, 1)

            norms = {x1_at[0] + 2: (norm_var, 0), x1_at[0] + 3: (norm_hf, 0), x1_at[0] + 4: (norm_var, 1),
                     x1_at[0] + 5: (norm_hf, 1), x1_at[2] + 1: (norm_var, 2), x1_at[2] + 2: (norm_hf, 2)}
            for n in range(len(OUT_ORDER)):
                add_out(n)
                if n == x1_at[0]:
                    ve.wait_ge(s_g2, 16)
                if n in norms:
                    part, t = norms[n]
                    part(t)
            norm_var(TT - 1)
            norm_hf(TT - 1)
            ve.wait_ge(logit_done, 1)
            step(ve.tensor_tensor(lg, bank[:, 4, 0:TT * E].rearrange("p (t e) -> p t e", t=TT),
                                  brb[:, :].unsqueeze(1).to_broadcast([P, TT, E]), ALU.add))
            for t in range(TT):
                ins = ve.max(out=top[:, t, :], in_=lg[:, t, :])
            step(ins)
            for t in range(TT):
                ins = ve.max_index(out=topi[:, t, :], in_max=top[:, t, :], in_values=lg[:, t, :])
            ve.tensor_tensor(ge, top[:, :, 0:TOPK], top[:, :, 0:1].to_broadcast([P, TT, TOPK]),
                             ALU.subtract).then_inc(topd, 1)
            step(ins)
            step(ve.tensor_copy(topf, topi[:, :, 0:TOPK]))
            step(ve.tensor_tensor(hot, iota_e[:, :].unsqueeze(1).unsqueeze(1).to_broadcast([P, TT, TOPK, E]),
                                  topf.unsqueeze(3).to_broadcast([P, TT, TOPK, E]), ALU.is_equal))
            ve.tensor_reduce(chosen, hot.rearrange("p t k e -> p t e k"), AX_X, ALU.add).then_inc(chosen_ready, 1)
            ve.wait_ge(topexp, 1)
            step(ve.tensor_reduce(gsum, ge, AX_X, ALU.add))
            step(ve.reciprocal(gsum, gsum))
            step(ve.tensor_tensor(ge, ge, gsum.unsqueeze(2).to_broadcast([P, TT, TOPK]), ALU.mult))
            step(ve.tensor_tensor(hotg, hot, ge.unsqueeze(3).to_broadcast([P, TT, TOPK, E]), ALU.mult))
            ve.wait_ge(consts2, 1)
            ve.tensor_reduce(gates, hotg.rearrange("p t k e -> p t e k"), AX_X, ALU.add).then_inc(gates_ready, 1)
            ve.wait_ge(gates_ready, 1)
            step(ve.tensor_copy(aux[:, :, :, 1], gates))
            ve.wait_ge(place_done, 1)
            places = bank[:, 5, 0:TT * E].rearrange("p (t e) -> p t e", t=TT)
            step(ve.scalar_tensor_tensor(out=posm, in0=places, scalar=1.0, in1=chosen, op0=ALU.add, op1=ALU.mult))
            ve.tensor_scalar(posm, posm, -1.0, None, ALU.add)
            step(ve.tensor_copy(cnt, bank[:, 5, TT * E:TT * E + E]))
            step(ve.tensor_scalar(nblk, cnt, float(P), 1.0, ALU.is_gt, ALU.add))
            for b in (2, 3):
                step(ve.scalar_tensor_tensor(out=nblk, in0=cnt, scalar=float(b * P), in1=nblk, op0=ALU.is_gt, op1=ALU.add))
            step(ve.memset(scan, 0.0))
            step(ve.tensor_copy(scan[:, 0, 16:16 + E], nblk))
            for b in range(5):
                w = 1 << b
                step(ve.tensor_tensor(scan[:, (b + 1) % 2, 16:16 + E], scan[:, b % 2, 16:16 + E],
                                      scan[:, b % 2, 16 - w:16 + E - w], ALU.add))
            ends = scan[:, 1, 16:16 + E]
            step(ve.scalar_tensor_tensor(out=cmpn, in0=cnt, scalar=-2.0 * E, in1=iota_e[:, :], op0=ALU.mult, op1=ALU.subtract))
            step(ve.memset(cmpn[:, 0:1], NEG))
            step(ve.tensor_reduce(tiny[:, 7:8], cmpn, AX_X, ALU.max))
            step(ve.scalar_tensor_tensor(out=cmpe, in0=cmpn, scalar=tiny[:, 7:8], in1=ends, op0=ALU.is_equal, op1=ALU.mult))
            step(ve.tensor_reduce(tiny[:, 8:9], cmpe, AX_X, ALU.add))
            ve.tensor_tensor(tiny[:, 9:10], ends[:, E - 1:E], tiny[:, 8:9], ALU.subtract)
            ve.tensor_scalar(tiny[:, 10:11], pcol[:, 1:2], -float(T), tiny[:, 8:9], ALU.add, ALU.is_equal)
            step(ve.tensor_scalar(tiny[:, 11:12], pcol[:, 1:2], -float(T), ends[:, E - 1:E], ALU.add, ALU.is_equal))
            step(ve.tensor_tensor(tiny[:, 10:11], tiny[:, 10:11], tiny[:, 11:12], ALU.subtract))
            place = tiny[:, 12:13]
            step(ve.scalar_tensor_tensor(out=place, in0=tiny[:, 10:11], scalar=tiny[:, 9:10], in1=pcol[:, 0:1],
                                         op0=ALU.mult, op1=ALU.add))
            step(ve.tensor_scalar(cmpe, ends, place, None, ALU.is_le))
            step(ve.tensor_reduce(tiny[:, 0:1], cmpe, AX_X, ALU.add))
            step(ve.tensor_tensor(cmpn, cmpe, nblk, ALU.mult))
            step(ve.tensor_reduce(tiny[:, 1:2], cmpn, AX_X, ALU.add))
            step(ve.tensor_scalar(meta[:, 0:1], tiny[:, 0:1], float(E - 1), None, ALU.min))
            step(ve.tensor_tensor(meta[:, 1:2], place, tiny[:, 1:2], ALU.subtract))
            step(ve.scalar_tensor_tensor(out=cmpn, in0=iota_e[:, :], scalar=meta[:, 0:1], in1=cnt,
                                         op0=ALU.is_equal, op1=ALU.mult))
            step(ve.tensor_reduce(tiny[:, 2:3], cmpn, AX_X, ALU.add))
            step(ve.scalar_tensor_tensor(out=tiny[:, 3:4], in0=meta[:, 1:2], scalar=-float(P), in1=tiny[:, 2:3],
                                         op0=ALU.mult, op1=ALU.add))
            step(ve.tensor_scalar(tiny[:, 5:6], meta[:, 1:2], 0.0, None, ALU.is_gt))
            step(ve.scalar_tensor_tensor(out=tiny[:, 4:5], in0=tiny[:, 3:4], scalar=float(WIDTHS[0]), in1=tiny[:, 5:6],
                                         op0=ALU.is_gt, op1=ALU.max))
            step(ve.scalar_tensor_tensor(out=meta[:, 2:3], in0=tiny[:, 3:4], scalar=float(WIDTHS[1]), in1=tiny[:, 4:5],
                                         op0=ALU.is_gt, op1=ALU.add))
            step(ve.tensor_scalar(tiny[:, 6:7], tiny[:, 4:5], -float(T), float(T), ALU.mult, ALU.add))
            step(ve.scalar_tensor_tensor(out=meta[:, 1:2], in0=meta[:, 1:2], scalar=float(P), in1=tiny[:, 6:7],
                                         op0=ALU.mult, op1=ALU.add))
            ve.tensor_copy(meta[:, 3:4], ends[:, E - 1:E]).then_inc(meta_ready, 1)
            ve.wait_ge(metarow_done, 1)
            ve.tensor_copy(meta_i, bank[0:1, 6, 0:4 * MI]).then_inc(meta_loaded, 1)
            ve.wait_ge(meta_loaded, 1)
            items = ve.value_load(meta_i[0:1, 3 * MI:3 * MI + 1], min_val=E, max_val=E + 15)

            def select(e, at):
                ve.tensor_copy(aux_now, aux[:, :, bass.ds(e, 1), :].rearrange("p t e a -> p t (e a)"))
                step_v(ve.tensor_copy(rel, posm[:, :, bass.ds(e, 1)].rearrange("p t e -> p (t e)")))
                for t in range(TT):
                    ins = ve.tensor_scalar(sel[:, t, :], pt[:, bass.ds(at, P)], rel[:, t:t + 1], None,
                                           ALU.is_equal)
                ins.then_inc(sel_ready, 1)

            step_v = Steps(ve, dve_moe)
            at0 = ve.value_load(meta_i[0:1, MI:MI + 1], min_val=0, max_val=T)
            select(0, at0)
            def place_rows(n, step_v):
                ve.wait_ge(slot_idx, n + 1)
                ve.tensor_copy(slot_next, bank[:, 7, 0:2]).then_inc(slot_idx_read, 1)
                ve.wait_ge(slot_idx_read, n + 1)
                step_v(ve.tensor_scalar(slot_pad, slot_next[:, 0:1], 0.0, pcol[:, 1:2], ALU.is_equal, ALU.mult))
                step_v(ve.scalar_tensor_tensor(out=row_next, in0=slot_next[:, 0:1], scalar=-1.0, in1=slot_pad,
                                               op0=ALU.add, op1=ALU.add))

            MOE_STEPS = 13
            place_rows(0, step_v)
            ve.tensor_copy(idx_next[:, :], row_next).then_inc(next_rows, 1)
            ve.wait_ge(bias_added, TT)
            with ve.Fori(0, items) as i:
                step_v = Steps(ve, dve_moe, i * MOE_STEPS + 3)
                e = ve.value_load(meta_i[0:1, bass.ds(i, 1)], min_val=0, max_val=E - 1)
                cls = ve.value_load(meta_i[0:1, bass.ds(i + 2 * MI, 1)], min_val=0, max_val=2)
                step_v(ve.tensor_copy(bias_now, biases[:, :, bass.ds(e, 1)].rearrange("p j e -> p (j e)")))
                e1 = ve.value_load(meta_i[0:1, bass.ds(i + 1, 1)], min_val=0, max_val=E - 1)
                at1 = ve.value_load(meta_i[0:1, bass.ds(i + 1 + MI, 1)], min_val=0, max_val=T)
                ve.wait_ge(slot_idx, i + 1)
                select(e1, at1)
                ve.wait_ge(rows_free, i + 1)
                ve.wait_ge(yrow_ready, i + 1)
                step_v(ve.tensor_copy(slot_now, slot_next))
                ve.tensor_copy(row_f, row_next).then_inc(row_ready, 1)
                ve.wait_ge(row_ready, i + 1)
                place_rows(i + 1, step_v)
                ve.wait_ge(x_gathered, 16 * i + 16)
                ve.tensor_copy(idx_next[:, :], row_next).then_inc(next_rows, 1)

                def add_bias(dst, b, cls, bias):
                    src = bank[:, b, :].rearrange("p (k c) -> p k c", k=4)
                    if cls == 0:
                        b, src = 3, bank[:, 2 + b % 2, :].rearrange("p (k a c) -> p k a c", k=4, a=2)[:, :, b // 2, :]
                    if cls != 1 or b == 3:
                        n = WIDTHS[cls]
                        return ve.tensor_tensor(dst, src[:, :, 0:n], bias.unsqueeze(2).to_broadcast([P, 4, n]), ALU.add)
                    ve.tensor_tensor(dst[:, :, QW * b:QW * (b + 1)], src[:, :, 3 * QW:4 * QW],
                                     bias.unsqueeze(2).to_broadcast([P, 4, QW]), ALU.add)
                    if b == 1:
                        rest = slice(0, 3, 2)
                        split = "p k (c w) -> p k c w"
                        return ve.tensor_tensor(dst.rearrange(split, w=QW)[:, :, rest, :],
                                                src.rearrange(split, w=QW)[:, :, rest, :],
                                                bias.unsqueeze(2).unsqueeze(3).to_broadcast([P, 4, 2, QW]), ALU.add)
                    rest = slice(QW, 3 * QW) if b == 0 else slice(0, 2 * QW)
                    return ve.tensor_tensor(dst[:, :, rest], src[:, :, rest],
                                            bias.unsqueeze(2).to_broadcast([P, 4, 2 * QW]), ALU.add)

                def swiglu(h, cls):
                    lo, hi = 4 * h, 4 * h + 4
                    g_h, u_h, s_h, a_h = (v[:, lo:hi, 0:WIDTHS[cls]] for v in (gate, up, sg, act))
                    ve.wait_ge(gu_t, 2 * i + h + 1)
                    step_v(add_bias(g_h, h, cls, bias_now[:, lo:hi]))
                    ve.tensor_scalar(g_h, g_h, LIMIT, None, ALU.min).then_inc(gated, 1)
                    step_v(add_bias(u_h, 2 + h, cls, bias_now[:, KF + lo:KF + hi]))
                    step_v(ve.tensor_scalar(u_h, u_h, LIMIT, -LIMIT, ALU.min, ALU.max))
                    step_v(ve.scalar_tensor_tensor(out=u_h, in0=u_h, scalar=1.0, in1=g_h, op0=ALU.add, op1=ALU.mult))
                    ve.wait_ge(sig_done, 2 * i + h + 1)
                    ve.tensor_tensor(a_h, u_h, s_h, ALU.mult).then_inc(act_ready, 1)

                n_steps = step_v.n

                def experts_part(cls):
                    step_v.n = n_steps
                    if cls == 0:
                        ve.scalar_tensor_tensor(out=idx[:, :], in0=row_f, scalar=2.0, in1=pcol[:, 2:3],
                                                op0=ALU.mult, op1=ALU.add).then_inc(now_ready, 1)
                        ve.sem_inc(gu_out_b, 2)
                    else:
                        ve.tensor_copy(idx[:, :], row_f).then_inc(now_ready, 1)
                    for h in range(2):
                        if cls > 0:
                            ve.wait_ge(gu_done, 2 * i + h + 1)
                            ve.tensor_copy(gu_tok[:, 2 + h, :], bank[:, 2 + h, :]).then_inc(gu_out_b, 1)
                        swiglu(h, cls)

                by_class(ve, cls, experts_part)
                assert step_v.n == MOE_STEPS, step_v.n

        @block.tensor
        def _(pe):
            pe.wait_ge(psum_clear, 1)
            pe.wait_ge(consts, 1)
            pe.wait_ge(xr_ready, TT)
            for k in range(KD):
                if k >= 4:
                    pe.wait_ge(hT_e, k - 3)
                for t in range(TT):
                    ins = pe.transpose(bank[:, k % 4, t * P:(t + 1) * P], xr[:, t, k * P:(k + 1) * P], ident[:, :])
                ins.then_inc(hT_t, 1)
            pe.wait_ge(hT_e, KD)

            def three_passes(out_ap, high_a, low_a, high_b, low_b, first, last):
                pe.matmul(out_ap, high_a, high_b, start=first, stop=False)
                pe.matmul(out_ap, high_a, low_b, start=False, stop=False)
                return pe.matmul(out_ap, low_a, high_b, start=False, stop=last)

            def project(out_bank, group, t, n):
                wh, wl = high(n), low(n)
                for k in range(KD):
                    ins = three_passes(bank[:, out_bank, 0:CW], order_cols(h_high[:, k, :], group, t),
                                       order_cols(h_low[:, k, :], group, t), wh[:, k, :], wl[:, k, :],
                                       k == 0, k == KD - 1)
                return ins

            with pe.Fori(0, 3) as kind:
                for g in range(GROUPS):
                    pe.wait_ge(low_made, 3 * kind + g + 1)
                    for t in range(TT):
                        n = g * TT + t
                        pe.wait_ge(proj_read, 12 * kind + n + 1)
                        project(n % 2, g, t, g).then_inc(proj_done, 1)

            pe.wait_ge(consts, CONSTS)
            pe.wait_ge(s_small, 16 * SMALL)
            for b in range(SETUP):
                if b >= 4:
                    pe.wait_ge(setup_e, b - 3)
                for a in range(4):
                    dst = bank[:, 4 + b % 4, :]
                    if b < SG // 4:
                        ins = pe.transpose(dst[:, a * P:(a + 1) * P], wsp_raw[:, 4 * b + a, :], ident[:, :])
                    elif b == SG // 4:
                        if a == 0:
                            ins = pe.transpose(dst[:, 0:SG], bsp_raw, ident[0:SG, 0:SG])
                    else:
                        j = 4 * (b - SG // 4 - 1) + a
                        ins = pe.transpose(dst[:, a * E:(a + 1) * E], bias_raw[:, j * P:(j + 1) * P], ident[0:E, 0:E])
                ins.then_inc(setup_t, 1)
            pe.wait_ge(setup_e, SETUP)

            def transpose_pair(s):
                g, r = divmod(s, 4)
                kind, pair = r // 2, 2 * g + r % 2
                pe.wait_ge(roped, TT * (kind + 1))
                if s >= 1:
                    pe.wait_ge(pair_e, s)
                for t in range(TT):
                    ins = pe.transpose(bank[:, 6, t * P:(t + 1) * P], qk[:, kind, t, pair * P:(pair + 1) * P], ident[:, :])
                ins.then_inc(pair_t, 1)

            def scores(u):
                g, j = divmod(u, 4)
                W = unit_width(u)
                k0 = unit_blocks(u)[0] * P
                pe.wait_ge(pair_e, 4 * (g + 1))
                pe.wait_ge(max_done, u)
                for h in range(HPG):
                    par, i = divmod(h, 2)
                    d = slice(par * HD, par * HD + HD)
                    ins = pe.matmul(bank[:, 2 + par, i * W:(i + 1) * W], qkT[d, 2 * g + i, j * P:(j + 1) * P],
                                    qkT[d, KA + 2 * g + i, k0:k0 + W], start=True, stop=True)
                ins.then_inc(score_done, 1)

            def transpose_p(u):
                W = unit_width(u)
                pe.wait_ge(prob_done, u + 1)
                pe.wait_ge(pt_e, u)
                dst = bank[:, 4:6, :].rearrange("p a n -> p (a n)")
                for c in range(HPG * W // P):
                    ins = pe.transpose(dst[:, c * P:(c + 1) * P], sc[:, u % 2, c * P:(c + 1) * P], ident[:, :])
                ins.then_inc(pt_t, 1)

            def weighted(u):
                g, j = divmod(u, 4)
                blocks = unit_blocks(u)
                nb = len(blocks)
                pe.wait_ge(pt_e, u + 1)
                pe.wait_ge(o_read, u)
                for h in range(HPG):
                    par, i = divmod(h, 2)
                    head = g * HPG + 2 * i + par
                    for b, tile in enumerate(blocks):
                        ins = pe.matmul(bank[par * HD:(par + 1) * HD, 7, i * P:(i + 1) * P],
                                        vtok[:, tile, head * HD:(head + 1) * HD],
                                        pt[:, (h * nb + b) * P:(h * nb + b + 1) * P], start=(b == 0), stop=(b == nb - 1))
                ins.then_inc(o_done, 1)

            for s in range(SLOTS):
                if s < 24:
                    c, t = divmod(s, TT)
                    if t == 0:
                        pe.wait_ge(low_made, 9 + c + 1)
                    pe.wait_ge(proj_read, 36 + s + 1)
                    ins = project(s % 2, 0, t, 9 + c)
                    ins.then_inc(proj_done, 1)
                if s < 12:
                    transpose_pair(s)
                if s % 2 == 1 and 5 <= s < 29:
                    scores((s - 5) // 2)
                if s % 2 == 1 and 7 <= s < 31:
                    transpose_p((s - 7) // 2)
                if s % 2 == 0 and 8 <= s < 31:
                    weighted((s - 8) // 2)
                if s >= 25:
                    if s == 25:
                        pe.wait_ge(ln_done, TT)
                        pe.wait_ge(proj_read, 62)
                    for g in (2 * s - 50, 2 * s - 49):
                        if g >= 2:
                            pe.wait_ge(mix_read, g - 1)
                        pe.matmul(bank[:, g % 2, 0:TT * HD].rearrange("p (t d) -> p t d", t=TT), wspT[:, g, :],
                                  ztok[:, :, g * HD:(g + 1) * HD], start=True, stop=True).then_inc(mix_done, 1)
            pe.wait_ge(o_read, 12)
            for a, stat in enumerate((mstat, lstat)):
                for g in range(GROUPS):
                    for j in range(4):
                        ins = pe.transpose(bank[0:HPG, 2 + 3 * a + g, j * P:(j + 1) * P], stat[:, 4 * g + j, :], ident[:, :])
                    ins.then_inc(ml_t, 1)
            pe.wait_ge(mix_read, SG)
            for k in range(KA):
                if k >= 2:
                    pe.wait_ge(ml_e, BANK_OF[k] - 1)
                for t in range(TT):
                    ins = pe.transpose(bank[:, BANK_OF[k], t * P:(t + 1) * P], utok[:, t, k * P:(k + 1) * P], ident[:, :])
                ins.then_inc(sgu_t, 1)

            def part_product(i, part, jj, free, count):
                wh, wl = high(15 + part), low(15 + part)
                pe.wait_ge(low_made, 4 * i + 16 + part)
                xh, xl, kt = ((h_high, h_low, KD) if part < 2 else (sgu_high, sgu_low, KA) if part == 2 else
                              (attn_high, attn_low, KA))
                pe.wait_ge(free, count)
                cols = slice(jj * P, (jj + 1) * P)
                for k in range(kt):
                    ins = three_passes(bank[:, 4 * jj + part, :], wh[:, k, cols], wl[:, k, cols],
                                       xh[:, k, :], xl[:, k, :], k == 0, k == kt - 1)
                ins.then_inc(gate_done if part < 2 else y_done, 1)

            part_product(0, 0, 0, sgu_e, 1)
            part_product(0, 0, 1, ml_e, 6)
            part_product(0, 1, 0, sgu_e, 2)
            part_product(0, 1, 1, sgu_e, KA)
            pe.wait_ge(wrow_ready, 1)
            for k in range(KA):
                if k >= 4:
                    pe.wait_ge(spread_read, k - 3)
                g, i = divmod(k, 2)
                pe.matmul(bank[:, SPREAD_BANK[k], :], pick[:, i, :], mrows[:, g, :], start=True, stop=True
                          ).then_inc(spread_done, 1)

            pe.wait_ge(spread_read, KA)

            def branches(i):
                for part in (2, 3):
                    if part == 3:
                        pe.wait_ge(attn_rest, KA)
                    for jj in range(2):
                        part_product(i, part, jj, y_read, 4 * i + 2 * (part - 2) + jj + 1)

            with pe.Fori(0, PAIRS - 1) as i:
                branches(i)
                for part in range(2):
                    for jj in range(2):
                        part_product(i + 1, part, jj, gate_read, 4 * i + 2 * part + jj + 1)
            branches(PAIRS - 1)
            pe.wait_ge(merged_rest, 2 * PAIRS - 2)
            pe.wait_ge(gate_read, 4 * PAIRS)

            def out_product(n):
                t, c = OUT_ORDER[n]
                m = 15 + 4 * PAIRS + c
                pe.wait_ge(low_made, m + 1)
                if n >= 2:
                    pe.wait_ge(out_read, n - 1)
                tokens = slice(t * P, (t + 1) * P)
                for k in range(KD):
                    if n == 0 and k == KD - 2:
                        pe.wait_ge(last_rest, 2)
                    ins = three_passes(bank[:, n % 2, 0:CW], merged_high[:, k, tokens], merged_low[:, k, tokens],
                                       high(m)[:, k, :], low(m)[:, k, :], k == 0, k == KD - 1)
                ins.then_inc(out_done, 1)

            def transpose_hf(t):
                pe.wait_ge(hf_ready, t + 1)
                if t >= 2:
                    pe.wait_ge(hf_e, t - 1)
                for k in range(KD):
                    ins = pe.transpose(bank[:, 2 + 4 * (t % 2) + k // 4, (k % 4) * P:(k % 4 + 1) * P],
                                       hf[:, t, k * P:(k + 1) * P], ident[:, :])
                ins.then_inc(hf_t, 1)

            def logits(t):
                pe.wait_ge(hf_e, t + 1)
                for k in range(KD):
                    ins = pe.matmul(bank[:, 4, t * E:(t + 1) * E], hfT[:, k, t * P:(t + 1) * P], wr[:, k, :],
                                    start=(k == 0), stop=(k == KD - 1))
                return ins

            router = {x1_at[2]: (transpose_hf, 0), x1_at[2] + 2: (transpose_hf, 1), x1_at[2] + 3: (logits, 0)}
            for n in range(len(OUT_ORDER)):
                out_product(n)
                if n in router:
                    part, t = router[n]
                    part(t)
            transpose_hf(2)
            logits(1)
            transpose_hf(3)
            logits(2)
            ins = logits(3)
            ins.then_inc(logit_done, 1)
            pe.wait_ge(chosen_ready, 1)
            flat_chosen = chosen.rearrange("p t e -> p (t e)")
            pe.matmul(bank[:, 5, 0:TT * E], upper[:, :], flat_chosen, start=True, stop=False, skip_group_check=True)
            for back in range(1, TT + 1):
                ins = pe.matmul(bank[:, 5, back * E:(TT + 1) * E], ones[:, :], flat_chosen[:, 0:(TT + 1 - back) * E],
                                start=False, stop=(back == TT), skip_group_check=True)
            ins.then_inc(place_done, 1)
            pe.wait_ge(gates_ready, 1)
            pe.wait_ge(s_bdn, 16)
            for t in range(TT):
                ins = pe.transpose(bank[0:E, 7, t * P:(t + 1) * P], gates[:, t, :], ident[:, :])
            ins.then_inc(gatesT_t, 1)
            pe.wait_ge(gatesT_e, 1)

            def bias_sums(t):
                if t >= 2:
                    pe.wait_ge(bsum_read, t - 1)
                for b in range(2):
                    ins = pe.matmul(bank[:, 2 * (t % 2) + b, :], gatesT[:, t * P:(t + 1) * P], bdn[:, b * BW:(b + 1) * BW],
                                    start=True, stop=True)
                ins.then_inc(bsum_done, 1)

            bias_sums(0)
            pe.wait_ge(meta_ready, 1)
            for c in range(4):
                ins = pe.matmul(bank[0:1, 6, c * MI:(c + 1) * MI], meta[:, c:c + 1], ident[:, 0:MI], start=True, stop=True)
            ins.then_inc(metarow_done, 1)
            pe.wait_ge(meta_loaded, 1)
            items = pe.value_load(meta_i[0:1, 3 * MI:3 * MI + 1], min_val=E, max_val=E + 15)

            def transpose_x(cls, half):
                n = WIDTHS[cls]
                for d in range(4 * half, 4 * half + 4):
                    ins = pe.transpose(bank[:, 6 + half, (d % 4) * P:(d % 4) * P + n], xg_tok[0:n, d * P:(d + 1) * P],
                                       ident[0:n, 0:n])
                ins.then_inc(xg_t, 1)

            def slots_of():
                for t in range(TT):
                    ins = pe.matmul(bank[:, 7, 0:2], sel[:, t, :], aux_now[:, t, :], start=(t == 0), stop=(t == TT - 1))
                ins.then_inc(slot_idx, 1)

            cls0 = pe.value_load(meta_i[0:1, 2 * MI:2 * MI + 1], min_val=0, max_val=2)
            bias_sums(1)
            pe.wait_ge(sel_ready, 1)
            slots_of()
            bias_sums(2)
            bias_sums(3)
            pe.wait_ge(slot_idx_read, 1)
            pe.wait_ge(x_gathered, 16)
            by_class(pe, cls0, lambda c: [transpose_x(c, h) for h in range(2)])
            pe.wait_ge(bsum_read, TT)
            with pe.Fori(0, items) as i:
                cls = pe.value_load(meta_i[0:1, bass.ds(i + 2 * MI, 1)], min_val=0, max_val=2)
                cls1 = pe.value_load(meta_i[0:1, bass.ds(i + 1 + 2 * MI, 1)], min_val=0, max_val=2)

                def parts(cls, h):
                    if cls == 0:
                        return [(slice(a * HW, (a + 1) * HW), slice(0, HW), h, 2 * a + h) for a in range(2)]
                    if cls == 2:
                        return [(slice(0, P), slice(0, P), b, b) for b in (h, 2 + h)]
                    out = []
                    for banks in ROUNDS[2 * h:2 * h + 2 - h]:
                        for c, b in enumerate(banks):
                            at = tile_slots(c, b)
                            out.append((slice(c * QW, (c + 1) * QW), slice(at, at + QW), b, b))
                    return out

                def gate_up(cls, k, h):
                    for rows, slots, b, cols in parts(cls, h):
                        ins = pe.matmul(bank[rows, b, :], xgT[:, k, slots], ring[:, k, cols * BW:(cols + 1) * BW],
                                        start=(k == 0), stop=(k == KD - 1))
                    return ins

                def transpose_gu(cls, h):
                    pe.wait_ge(gu_out_a, 2 * i + h + 1)
                    pe.wait_ge(gu_out_b, 2 * i + h + 1)
                    for j in range(4):
                        f = slice(j * P, (j + 1) * P)
                        if cls == 0:
                            ins = pe.transpose(bank[:, 2 + h, f], gu_tok[:, h, f], ident[:, :])
                        else:
                            pe.transpose(bank[:, h, f], gu_tok[:, h, f], ident[:, :])
                            ins = pe.transpose(bank[:, 2 + h, f], gu_tok[:, 2 + h, f], ident[:, :])
                    ins.then_inc(gu_t, 1)

                def down(cls, j):
                    s = KD + j // 2
                    if j % 2 == 0:
                        pe.wait_ge(s_slot[s], 16 * (i + 1))
                    if j % 4 == 0:
                        pe.wait_ge(act_ready, 2 * i + j // 4 + 1)
                    for b in range(2):
                        a_j = act[:, j, 0:WIDTHS[cls]]
                        out_ap = bank[b * HW:(b + 1) * HW, 4, :] if cls == 0 else bank[0:WIDTHS[cls], 4 + b, :]
                        at = (j % 2) * D + b * BW
                        ins = pe.matmul(out_ap, a_j, ring[:, s, at:at + BW], start=(j == 0), stop=(j == KF - 1))
                    if j % 2 == 1 and j < KF - 1:
                        ins.then_inc(slot_used, 1)
                    return ins

                def products(cls):
                    pe.wait_ge(xg_e, 2 * i + 2)
                    for k in range(KD // 2):
                        pe.wait_ge(s_slot[k], 16 * (i + 1))
                        gate_up(cls, k, 0)
                        gate_up(cls, k, 1).then_inc(slot_used, 1)
                    pe.wait_ge(sel_ready, i + 2)
                    slots_of()
                    for k in range(KD // 2, KD):
                        pe.wait_ge(s_slot[k], 16 * (i + 1))
                        ins = gate_up(cls, k, 0)
                    ins.then_inc(gu_done, 1)
                    for k in range(KD // 2, KD):
                        ins = gate_up(cls, k, 1)
                        ins.then_inc(slot_used if k < KD - 1 else gu_done, 1)
                        if k == KD // 2:
                            transpose_gu(cls, 0)
                    pe.wait_ge(yrow_ready, i + 1)
                    for j in range(KF // 2):
                        down(cls, j)
                        if j == 0:
                            transpose_gu(cls, 1)

                def last_products(cls):
                    for j in range(KF // 2, KF):
                        ins = down(cls, j)
                    ins.then_inc(down_done, 1)

                by_class(pe, cls, products)
                pe.wait_ge(slot_idx_read, i + 2)
                pe.wait_ge(x_gathered, 16 * i + 32)
                by_class(pe, cls1, lambda c: [transpose_x(c, h) for h in range(2)])
                by_class(pe, cls, last_products)


_INS = ["x", "positions", "norm1_g", "w_in", "q_norm_g", "k_norm_g", "sgu_ln_g", "sgu_ln_b", "w_spatial", "b_spatial",
        "w_branch_a", "w_branch_b", "w_out", "norm2_g", "w_router", "b_router", "w_gate_up", "b_gate_up", "w_down",
        "b_down"]


def kernel(**inputs):
    import concourse.bacc as bacc
    from concourse.bass_utils import run_bass_kernel_spmd

    nc = bacc.Bacc("TRN2", target_bir_lowering=False, num_devices=1)
    arrays, args = {}, []
    for name in _INS:
        a = np.ascontiguousarray(inputs[name])
        arrays[f"in_{name}"] = a
        args.append(nc.dram_tensor(f"in_{name}", a.shape, mybir.dt.from_np(a.dtype), kind="ExternalInput").ap())
    shape = tuple(inputs["x"].shape)
    args.append(nc.dram_tensor("out_y", shape, F32, kind="ExternalOutput").ap())
    hybrid_layer(nc, *args)
    r = run_bass_kernel_spmd(nc, [arrays], core_ids=[0])
    return r.results[0]["out_y"]
```
